# Optimizing a Trainium2 kernel written in Bass

```python
import jax, jax.numpy as jnp
from jax import lax
import numpy as np
import math

D_MODEL = 1024
BATCH = 1
SEQ = 512
DEPTH = 1

CHUNK = 64
HEAD_DIM = 64
CONV_GROUPS = 8
CONV_DIM = CONV_GROUPS * HEAD_DIM
RWKV_HEADS = 8
RWKV_DIM = RWKV_HEADS * HEAD_DIM
MIX_DIM = CONV_DIM + RWKV_DIM
CONV_K = 3
DECAY_RANK = 64
ICLR_RANK = 64
GATE_RANK = 160
D_FF = 2816
RWKV_COLS = 3 * RWKV_DIM + DECAY_RANK + ICLR_RANK + GATE_RANK
IN_COLS = 3 * CONV_DIM + RWKV_COLS
RMS_EPS = 1e-6
GN_EPS = HEAD_DIM * 1e-5


def _rms_norm(z, g):
    zf = z.astype(jnp.float32)
    zf = zf * lax.rsqrt(jnp.mean(zf * zf, axis=-1, keepdims=True) + RMS_EPS)
    return (zf * g.astype(jnp.float32)).astype(z.dtype)

def _causal_dwconv(z, w):
    c = z.shape[-1]
    return lax.conv_general_dilated(
        z, w[:, None, :].astype(z.dtype), window_strides=(1,),
        padding=[(CONV_K - 1, 0)], dimension_numbers=('NWC', 'WIO', 'NWC'),
        feature_group_count=c)

def _token_shift(z):
    return jnp.pad(z[:, :-1], ((0, 0), (1, 0), (0, 0)))

def _wkv7(r, decay, k, v, kk, a):
    b, t, h, n = r.shape
    n_chunks = t // CHUNK

    def to_chunks(z):
        return z.reshape(b, n_chunks, CHUNK, h, n).transpose(1, 2, 0, 3, 4)

    def step(S, inp):
        r_t, w_t, k_t, v_t, kk_t, a_t = inp
        sa = jnp.einsum('bhvk,bhk->bhv', S, -kk_t)
        S = (S * w_t[:, :, None, :] + sa[..., None] * (kk_t * a_t)[:, :, None, :]
             + v_t[..., None] * k_t[:, :, None, :])
        return S, jnp.einsum('bhvk,bhk->bhv', S, r_t)

    def chunk_step(S, inp):
        return lax.scan(step, S, inp)

    S0 = jnp.zeros((b, h, n, n), jnp.float32)
    xs = tuple(to_chunks(z) for z in (r, decay, k, v, kk, a))
    _, y = lax.scan(chunk_step, S0, xs)
    return y.transpose(2, 0, 1, 3, 4).reshape(b, t, h, n)

def _head_group_norm(y, wgt, bias):
    mu = jnp.mean(y, axis=-1, keepdims=True)
    var = jnp.mean(jnp.square(y - mu), axis=-1, keepdims=True)
    yn = (y - mu) * lax.rsqrt(var + GN_EPS)
    b, t, h, n = y.shape
    return yn.reshape(b, t, h * n) * wgt.astype(jnp.float32) + bias.astype(jnp.float32)

def _token_mixer(xn, w_in, conv_a_w, shift_mu, w0, w2, a0, a2, g2, k_k, k_a, r_k,
                 lnx_w, lnx_b, w_out):
    b, t, _ = xn.shape
    p = jnp.einsum('btd,de->bte', xn, w_in)
    gB, gC, hA = jnp.split(p[..., :3 * CONV_DIM], 3, axis=-1)
    y_a = gC * _causal_dwconv(gB * hA, conv_a_w)
    q = p[..., 3 * CONV_DIM:]
    q = q + (_token_shift(q) - q) * shift_mu
    splits = np.cumsum([RWKV_DIM, RWKV_DIM, RWKV_DIM, DECAY_RANK, ICLR_RANK]).tolist()
    r, k, v, wd, ad, gd = jnp.split(q, splits, axis=-1)
    wdf = wd.astype(jnp.float32)
    w_log = -jax.nn.softplus(-(w0.astype(jnp.float32)
                               + jnp.tanh(wdf) @ w2.astype(jnp.float32))) - 0.5
    decay = jnp.exp(-jnp.exp(w_log))
    a = jax.nn.sigmoid(a0 + ad @ a2)
    g = jax.nn.sigmoid(gd) @ g2
    heads = lambda z: z.astype(jnp.float32).reshape(b, t, RWKV_HEADS, HEAD_DIM)
    pheads = lambda z: z.astype(jnp.float32).reshape(RWKV_HEADS, HEAD_DIM)
    r4, k4, v4, a4, d4 = heads(r), heads(k), heads(v), heads(a), heads(decay)
    kk = k4 * pheads(k_k)
    kk = kk / jnp.maximum(jnp.linalg.norm(kk, axis=-1, keepdims=True), 1e-12)
    k4 = k4 * (1.0 + (a4 - 1.0) * pheads(k_a))
    y = _wkv7(r4, d4, k4, v4, kk, a4)
    y_b = _head_group_norm(y, lnx_w, lnx_b)
    bonus = jnp.sum(r4 * k4 * r_k.astype(jnp.float32), axis=-1, keepdims=True) * v4
    y_b = (y_b + bonus.reshape(b, t, RWKV_DIM)).astype(xn.dtype) * g
    return jnp.einsum('bte,ed->btd', jnp.concatenate([y_a, y_b], axis=-1), w_out)

def _channel_mixer(hn, w_up, ffn_conv_w, ffn_conv_b, w_down):
    f = jnp.einsum('btd,df->btf', hn, w_up)
    f = _causal_dwconv(f, ffn_conv_w) + ffn_conv_b
    gate, up = jnp.split(f, 2, axis=-1)
    return jnp.einsum('btf,fd->btd', jax.nn.gelu(gate) * up, w_down)

def first_inputs(seed: int = 0) -> dict:
    key = jax.random.key(seed)
    ks = iter(jax.random.split(key, 32))
    nrm = lambda shape, s: jax.random.normal(next(ks), shape, jnp.float32) * s
    L = DEPTH
    return {
        'x': jax.random.normal(next(ks), (BATCH, SEQ, D_MODEL), jnp.float32),
        'pre_mix_g': 1.0 + nrm((L, D_MODEL), 0.02),
        'w_in': nrm((L, D_MODEL, IN_COLS), D_MODEL ** -0.5),
        'conv_a_w': nrm((L, CONV_K, CONV_DIM), 0.5),
        'shift_mu': jax.random.uniform(next(ks), (L, RWKV_COLS), jnp.float32),
        'w0': jax.random.uniform(next(ks), (L, RWKV_DIM), jnp.float32, -6.0, 0.0),
        'w2': nrm((L, DECAY_RANK, RWKV_DIM), 0.1),
        'a0': nrm((L, RWKV_DIM), 0.1),
        'a2': nrm((L, ICLR_RANK, RWKV_DIM), ICLR_RANK ** -0.5),
        'g2': nrm((L, GATE_RANK, RWKV_DIM), GATE_RANK ** -0.5),
        'k_k': 0.85 + nrm((L, RWKV_DIM), 0.02),
        'k_a': 1.0 + nrm((L, RWKV_DIM), 0.02),
        'r_k': nrm((L, RWKV_HEADS, HEAD_DIM), 0.1),
        'lnx_w': 1.0 + nrm((L, RWKV_DIM), 0.02),
        'lnx_b': nrm((L, RWKV_DIM), 0.01),
        'w_out': nrm((L, MIX_DIM, D_MODEL), MIX_DIM ** -0.5),
        'post_mix_g': 1.0 + nrm((L, D_MODEL), 0.02),
        'pre_ffn_g': 1.0 + nrm((L, D_MODEL), 0.02),
        'w_up': nrm((L, D_MODEL, 2 * D_FF), D_MODEL ** -0.5),
        'ffn_conv_w': nrm((L, CONV_K, 2 * D_FF), 0.5),
        'ffn_conv_b': nrm((L, 2 * D_FF), 0.01),
        'w_down': nrm((L, D_FF, D_MODEL), D_FF ** -0.5),
        'post_ffn_g': 1.0 + nrm((L, D_MODEL), 0.02),
    }

def first_block(x, pre_mix_g, w_in, conv_a_w, shift_mu, w0, w2, a0, a2, g2, k_k, k_a, r_k,
              lnx_w, lnx_b, w_out, post_mix_g, pre_ffn_g, w_up, ffn_conv_w, ffn_conv_b,
              w_down, post_ffn_g):
    h = x
    for l in range(DEPTH):
        mix = _token_mixer(_rms_norm(h, pre_mix_g[l]), w_in[l], conv_a_w[l], shift_mu[l],
                           w0[l], w2[l], a0[l], a2[l], g2[l], k_k[l], k_a[l], r_k[l],
                           lnx_w[l], lnx_b[l], w_out[l])
        h = h + _rms_norm(mix, post_mix_g[l])
        ffn = _channel_mixer(_rms_norm(h, pre_ffn_g[l]), w_up[l], ffn_conv_w[l],
                             ffn_conv_b[l], w_down[l])
        h = h + _rms_norm(ffn, post_ffn_g[l])
    return h


DEPTH_2 = 2

Q_BLOCK = 128
EPS = 1e-6

GLA_HEADS = 4
GLA_DK = 64
GLA_DV = 128
GLA_RANK = 16
GLA_TAU = 16.0
DSA_HEADS = 4
DSA_HD = 128
IDX_HEADS = 8
IDX_HD = 64
TOPK_MAX = 256
DIFF_HEADS = 4
DIFF_HD = 64

BR_W = 512
N_BRANCH = 3

SIZES = [
    GLA_HEADS * GLA_DK, GLA_HEADS * GLA_DK, GLA_HEADS * GLA_DV, GLA_RANK, BR_W,
    DSA_HEADS * DSA_HD, DSA_HEADS * DSA_HD, DSA_HEADS * DSA_HD,
    IDX_HEADS * IDX_HD, IDX_HD, IDX_HEADS, BR_W,
    DIFF_HEADS * 2 * DIFF_HD, DIFF_HEADS * 2 * DIFF_HD, DIFF_HEADS * 2 * DIFF_HD, BR_W,
    N_BRANCH * D_MODEL,
]
N_IN = int(sum(SIZES))
SPLIT_AT = [int(s) for s in np.cumsum(SIZES)[:-1]]


F32 = jnp.float32

def _rms(x, g=None):
    xf = x.astype(F32)
    y = xf * lax.rsqrt(jnp.mean(xf * xf, axis=-1, keepdims=True) + EPS)
    if g is not None:
        y = y * g.astype(F32)
    return y.astype(x.dtype)

def _chunk_visible(start, n_q, n_k):
    pos_q = start + jnp.arange(n_q)
    vis_end = (pos_q // CHUNK + 1) * CHUNK
    return jnp.arange(n_k)[None, :] < vis_end[:, None]

def _to_blocks(a, nb):
    return a.reshape((a.shape[0], nb, Q_BLOCK) + a.shape[2:]).swapaxes(0, 1)

def _gla(q, k, v, a_lr, wa2, ba, norm_g):
    B, T, _ = q.shape
    nc = T // CHUNK
    shp = (B, nc, CHUNK, GLA_HEADS)
    q = q.astype(F32).reshape(shp + (GLA_DK,)) * GLA_DK ** -0.5
    k = k.astype(F32).reshape(shp + (GLA_DK,))
    v = v.astype(F32).reshape(shp + (GLA_DV,))
    log_a = jax.nn.log_sigmoid((a_lr @ wa2 + ba).astype(F32)) / GLA_TAU
    log_a = log_a.reshape(shp + (GLA_DK,))
    cum = jnp.cumsum(log_a, axis=2)
    total = cum[:, :, -1]
    k_dec = k * jnp.exp(total[:, :, None] - cum)
    u = jnp.einsum('bnchk,bnchv->nbhkv', k_dec, v)
    decay = jnp.exp(total).transpose(1, 0, 2, 3)

    def step(S, inp):
        a, uc = inp
        S = a[..., None] * S + uc
        return S, S

    S0 = jnp.zeros((B, GLA_HEADS, GLA_DK, GLA_DV), F32)
    _, states = lax.scan(step, S0, (decay, u))
    o = jnp.einsum('bnchk,nbhkv->bnchv', q, states)
    o = _rms(o, norm_g)
    return o.reshape(B, T, GLA_HEADS * GLA_DV)

def _dsa(q, k, v, iq, ik, iw, qn_g, kn_g):
    B, T, _ = q.shape
    nb = T // Q_BLOCK
    topk = min(TOPK_MAX, T // 4)
    q = _rms(q.reshape(B, T, DSA_HEADS, DSA_HD), qn_g)
    k = _rms(k.reshape(B, T, DSA_HEADS, DSA_HD), kn_g)
    v = v.reshape(B, T, DSA_HEADS, DSA_HD)
    iq = iq.reshape(B, T, IDX_HEADS, IDX_HD)
    iw = iw.astype(F32) * IDX_HEADS ** -0.5
    starts = jnp.arange(nb) * Q_BLOCK

    def one(inp):
        qb, iqb, iwb, start = inp
        allowed = _chunk_visible(start, Q_BLOCK, T)
        dots = jnp.einsum('bqhd,bsd->bqhs', iqb, ik, preferred_element_type=F32) * IDX_HD ** -0.5
        score = jnp.einsum('bqhs,bqh->bqs', jax.nn.relu(dots), iwb)
        score = jnp.where(allowed[None], score, -jnp.inf)
        top_val, top_idx = lax.top_k(score, topk)
        valid = jnp.isfinite(top_val)
        k_sel = jax.vmap(lambda kk, ii: kk[ii])(k, top_idx)
        v_sel = jax.vmap(lambda vv, ii: vv[ii])(v, top_idx)
        logits = jnp.einsum('bqhd,bqshd->bhqs', qb, k_sel, preferred_element_type=F32) * DSA_HD ** -0.5
        logits = jnp.where(valid[:, None], logits, -jnp.inf)
        p = jax.nn.softmax(logits, axis=-1).astype(v.dtype)
        return jnp.einsum('bhqs,bqshd->bqhd', p, v_sel)

    out = lax.map(one, (_to_blocks(q, nb), _to_blocks(iq, nb), _to_blocks(iw, nb), starts))
    return out.swapaxes(0, 1).reshape(B, T, DSA_HEADS * DSA_HD)

def _diff(q, k, v, qn_g, kn_g, lq1, lk1, lq2, lk2, lambda_init):
    B, T, _ = q.shape
    nb = T // Q_BLOCK
    q = _rms(q.reshape(B, T, DIFF_HEADS, 2, DIFF_HD), qn_g)
    k = _rms(k.reshape(B, T, DIFF_HEADS, 2, DIFF_HD), kn_g)
    v = v.reshape(B, T, DIFF_HEADS, 2 * DIFF_HD)
    lam = (jnp.exp(jnp.sum(lq1.astype(F32) * lk1.astype(F32)))
           - jnp.exp(jnp.sum(lq2.astype(F32) * lk2.astype(F32))) + lambda_init)
    starts = jnp.arange(nb) * Q_BLOCK

    def one(inp):
        qb, start = inp
        allowed = _chunk_visible(start, Q_BLOCK, T)
        logits = jnp.einsum('bqhcd,bshcd->bhcqs', qb, k, preferred_element_type=F32) * DIFF_HD ** -0.5
        logits = jnp.where(allowed, logits, -jnp.inf)
        p = jax.nn.softmax(logits, axis=-1)
        attn = (p[:, :, 0] - lam * p[:, :, 1]).astype(v.dtype)
        return jnp.einsum('bhqs,bshd->bqhd', attn, v)

    out = lax.map(one, (_to_blocks(q, nb), starts)).swapaxes(0, 1)
    out = _rms(out) * (1.0 - lambda_init)
    return out.reshape(B, T, DIFF_HEADS * 2 * DIFF_HD)

def second_inputs(seed: int = 0) -> dict:
    key = jax.random.key(seed)
    ks = jax.random.split(key, 16)
    nrm = jax.random.normal
    L = DEPTH_2
    return {
        "x": nrm(ks[0], (BATCH, SEQ, D_MODEL), F32),
        "norm_g": 1.0 + 0.02 * nrm(ks[1], (L, D_MODEL), F32),
        "w_in": nrm(ks[2], (L, D_MODEL, N_IN), F32) * D_MODEL ** -0.5,
        "gla_wa2": nrm(ks[3], (L, GLA_RANK, GLA_HEADS * GLA_DK), F32) * GLA_RANK ** -0.5,
        "gla_ba": 1.0 + 0.1 * nrm(ks[4], (L, GLA_HEADS * GLA_DK), F32),
        "gla_norm_g": 1.0 + 0.02 * nrm(ks[5], (L, GLA_DV), F32),
        "dsa_qn_g": 1.0 + 0.02 * nrm(ks[6], (L, DSA_HD), F32),
        "dsa_kn_g": 1.0 + 0.02 * nrm(ks[7], (L, DSA_HD), F32),
        "diff_qn_g": 1.0 + 0.02 * nrm(ks[8], (L, DIFF_HD), F32),
        "diff_kn_g": 1.0 + 0.02 * nrm(ks[9], (L, DIFF_HD), F32),
        "diff_lq1": 0.1 * nrm(ks[10], (L, DIFF_HD), F32),
        "diff_lk1": 0.1 * nrm(ks[11], (L, DIFF_HD), F32),
        "diff_lq2": 0.1 * nrm(ks[12], (L, DIFF_HD), F32),
        "diff_lk2": 0.1 * nrm(ks[13], (L, DIFF_HD), F32),
        "w_br": nrm(ks[14], (L, N_BRANCH, BR_W, D_MODEL), F32) * BR_W ** -0.5,
        "w_out": nrm(ks[15], (L, D_MODEL, D_MODEL), F32) * D_MODEL ** -0.5,
    }

def second_block(x, norm_g, w_in, gla_wa2, gla_ba, gla_norm_g, dsa_qn_g, dsa_kn_g, diff_qn_g, diff_kn_g,
              diff_lq1, diff_lk1, diff_lq2, diff_lk2, w_br, w_out):
    B, T, _ = x.shape
    for l in range(DEPTH_2):
        h = _rms(x, norm_g[l])
        proj = h @ w_in[l]
        (gq, gk, gv, ga, gz, bq, bk, bv, iq, ik, iw, bz,
         cq, ck, cv, cz, gate) = jnp.split(proj, SPLIT_AT, axis=-1)
        lambda_init = 0.8 - 0.6 * math.exp(-0.3 * l)
        y_a = _gla(gq, gk, gv, ga, gla_wa2[l], gla_ba[l], gla_norm_g[l]).astype(x.dtype) * jax.nn.silu(gz)
        y_b = _dsa(bq, bk, bv, iq, ik, iw, dsa_qn_g[l], dsa_kn_g[l]) * jax.nn.silu(bz)
        y_c = _diff(cq, ck, cv, diff_qn_g[l], diff_kn_g[l], diff_lq1[l], diff_lk1[l],
                    diff_lq2[l], diff_lk2[l], lambda_init) * jax.nn.silu(cz)
        g = jax.nn.sigmoid(gate.reshape(B, T, N_BRANCH, D_MODEL))
        merged = (g[:, :, 0] * (y_a @ w_br[l, 0])
                  + g[:, :, 1] * (y_b @ w_br[l, 1])
                  + g[:, :, 2] * (y_c @ w_br[l, 2]))
        x = x + merged @ w_out[l]
    return x


def setup_inputs(seed=0):
    out = dict(first_inputs(seed))
    for name, value in second_inputs(seed + 1).items():
        if name != "x":
            out[name + "_2"] = value
    return out


def reference(
    x, pre_mix_g, w_in, conv_a_w, shift_mu, w0, w2, a0, a2, g2, k_k, k_a, r_k, lnx_w, lnx_b,
    w_out, post_mix_g, pre_ffn_g, w_up, ffn_conv_w, ffn_conv_b, w_down, post_ffn_g, norm_g_2,
    w_in_2, gla_wa2_2, gla_ba_2, gla_norm_g_2, dsa_qn_g_2, dsa_kn_g_2, diff_qn_g_2, diff_kn_g_2,
    diff_lq1_2, diff_lk1_2, diff_lq2_2, diff_lk2_2, w_br_2, w_out_2,
):
    x = first_block(
        x, pre_mix_g, w_in, conv_a_w, shift_mu, w0, w2, a0, a2, g2, k_k, k_a, r_k, lnx_w, lnx_b,
        w_out, post_mix_g, pre_ffn_g, w_up, ffn_conv_w, ffn_conv_b, w_down, post_ffn_g,
    )
    return second_block(
        x, norm_g_2, w_in_2, gla_wa2_2, gla_ba_2, gla_norm_g_2, dsa_qn_g_2, dsa_kn_g_2,
        diff_qn_g_2, diff_kn_g_2, diff_lq1_2, diff_lk1_2, diff_lq2_2, diff_lk2_2, w_br_2,
        w_out_2,
    )


_drawn_inputs = setup_inputs


def setup_inputs(seed=0):
    import zlib

    import numpy as np

    out = dict(_drawn_inputs(seed))
    spreads = {}
    factors = {'w2': 2.688,
     'a0': 2.822,
     'k_k': 5.236,
     'k_a': 4.63,
     'lnx_w': 5.042,
     'lnx_b': 7.663,
     'post_mix_g': 2.888,
     'pre_ffn_g': 2.881,
     'ffn_conv_b': 4.502,
     'post_ffn_g': 4.039,
     'norm_g_2': 3.809,
     'gla_ba_2': 3.949,
     'gla_norm_g_2': 8.0,
     'dsa_qn_g_2': 8.0,
     'dsa_kn_g_2': 8.0,
     'diff_qn_g_2': 8.0,
     'diff_kn_g_2': 8.0,
     'diff_lq1_2': 4.373,
     'diff_lk1_2': 8.0,
     'diff_lq2_2': 3.369,
     'diff_lk2_2': 8.0}
    for name, (base, spread) in spreads.items():
        noise = np.random.default_rng([zlib.crc32(name.encode()), seed]).standard_normal(out[name].shape)
        drawn = base * np.exp(spread * noise) if base else spread * noise
        out[name] = __import__('jax').numpy.asarray(drawn.astype(out[name].dtype))
    for name, factor in factors.items():
        out[name] = (out[name] * factor).astype(out[name].dtype)
    return out
```

```python
from contextlib import contextmanager

import concourse.bass as bass
from concourse import mybir

F32 = mybir.dt.float32
F32R = mybir.dt.float32r
ALU = mybir.AluOpType
ACT = mybir.ActivationFunctionType
AX_X = mybir.AxisListType.X

P = 128
T = 512
D = 1024
TT = T // P
KT = D // P
RMS_EPS = 1e-6
BASE = 16544
PW = 256
PANEL = KT * PW

BR = 512
JT = BR // P
GN_EPS = 64 * 1e-5
DECAY = 0.6065306597126334
LEVELS = 7
DFF = 2816
FT = DFF // P


def numbered(sizes):
    at, out = 0, {}
    for name, n in sizes:
        out[name] = at
        at += n
    return out, at


ROW, ROWS = numbered((("pre_mix", 8), ("mu_r", 4), ("mu_k", 4), ("mu_v", 4), ("mu_wa", 1), ("mu_g", 2), ("w0", 4),
                      ("a0", 4), ("k_k", 4), ("k_a", 4), ("lnx_w", 4), ("lnx_b", 4), ("r_k", 4), ("conv", 12)))
FROW, FROWS = numbered((("pre_ffn", 8), ("bias", 2 * FT), ("conv0", 2 * FT)))
FROW2, FROWS2 = numbered((("conv1", 2 * FT), ("conv2", 2 * FT)))


class Map:
    pass


class Panel:

    def __init__(self, name, pieces, kt, tokens):
        self.name = name
        self.pieces = pieces
        self.kt = kt
        self.tokens = tokens
        self.w = sum(c[2] for c in pieces)


class Steps:

    def __init__(self, known=None):
        self.known = known
        self.found = {}
        self.stride = {}
        self.rounds = {}


class Engine:

    def __init__(self, steps, name, eng, sems):
        self.steps, self.name, self.eng, self.sems = steps, name, eng, sems
        self.done = sems.get(name)
        self.n, self.open, self.covered = 0, [], {}

    def counted(self, step):
        self.n += 1
        assert step not in self.steps.found, step
        self.steps.found[step] = (self.name, self.n, tuple(i for i, _ in self.open))

    def at(self, step, back=0, at=None):
        known = self.steps.known
        if known is None:
            return 0
        owner, value, loops = known.found[step]
        mine, low = dict(self.open), value
        for n, loop in enumerate(loops):
            stride = known.stride[owner, loop]
            if loop in mine:
                gone = back * stride if n == len(loops) - 1 else 0
                value, low = mine[loop] * stride + (value - gone), low - gone
            else:
                value = value + (known.rounds[owner, loop] - 1 if at is None else at) * stride
        assert low >= 1, step
        return value

    def point(self, step, back=0, at=None):
        known = self.steps.known
        return self.sems[known.found[step][0] if known else "pe"], self.at(step, back, at)

    def so_far(self):
        value = self.n if self.steps.known else 0
        for loop, i in self.open:
            if self.steps.known and self.n:
                value = i * self.steps.known.stride[self.name, loop] + value
        return value

    def wait_ge(self, sem, value):
        if isinstance(value, int):
            if self.covered.get(sem.name, 0) >= value:
                return
            if not self.open:
                self.covered[sem.name] = value
        self.eng.wait_ge(sem, value)

    @contextmanager
    def loop(self, name, rounds):
        start = self.n
        self.steps.rounds[self.name, name] = rounds
        with self.eng.Fori(0, rounds) as i:
            self.open.append((name, i))
            yield i
            self.open.pop()
        self.steps.stride[self.name, name] = self.n - start
        self.n = start + rounds * (self.n - start)


def lay_out(nc, A):
    m = Map()

    def place(name, shape, dt, at):
        return nc.alloc_sbuf_tensor_at(name, shape, dt, offset=at)

    def area(start):
        at = [start]

        def take(name, shape, dt=F32):
            n = 4
            for s in shape[1:]:
                n *= s
            t = place(name, shape, dt, at[0])
            at[0] += (n + 31) // 32 * 32
            assert at[0] <= nc.sbuf_usable_end // 32 * 32, (name, at[0])
            return t
        return take, at

    take, at = area(BASE)
    m.raw = take("w_raw", [P, 2, PANEL])
    m.wh = take("w_hi", [P, 2, PANEL], F32R)
    m.wl = take("w_lo", [P, 2, PANEL], F32R)
    m.hT_at = at[0]
    m.hH = take("h_hi", [P, KT, T], F32R)
    m.hL = take("h_lo", [P, KT, T], F32R)
    m.x_at = at[0]
    m.x = take("x_tokens", [P, TT, D])
    m.ident = take("ident", [P, P])
    m.bd = take("head_blocks", [P, P])
    m.indh = take("half_rows", [P, KT, 16])
    m.indw = take("tile_rows", [P, KT, KT])
    m.indhT = take("half_rows_t", [16, KT, P])
    m.indwT = take("tile_rows_t", [KT, KT, P])
    m.eps = take("eps", [P, 2])
    m.stat = take("row_stats", [P, 4, TT])
    m.arena = at[0]

    take, at = area(m.arena)
    m.smask = take("score_masks", [P, 4, P])
    m.lmask = take("level_masks", [P, LEVELS, P])
    m.prow = take("param_rows", [P, P])
    m.pcol = take("param_cols", [P, P])
    m.omm = take("one_minus", [P, 24])
    m.APR_at = at[0]
    m.APR = take("a_r", [P, 2, JT, T])
    m.BK = take("b_k", [P, 2, JT, T])
    m.Vt = take("v_tokens", [P, TT, BR])
    m.bv = take("bonus_v", [P, JT, T])
    m.yT_at = at[0]
    m.yT = take("y_feats", [P, JT, T])
    m.ya = take("conv_out", [P, JT, T])
    m.gd = take("gate_lr", [P, T])
    m.gd2 = take("gate_lr2", [32, T])
    m.fac = take("state_factor", [P, JT, TT])
    m.emid = take("decay_to_mid", [P, JT, TT])
    shared = at[0]
    m.xn1 = place("x_normed", [P, TT, D], F32, m.APR_at)
    m.vq = place("v_feats", [P, JT, T], F32, m.yT_at)
    take, at = area(shared)
    m.zs = take("shifted", [P, 2, T + 8])
    m.Gx = take("decay_sum", [P, TT, P + 1])
    m.Gc = take("decay_sum_mid", [P, TT, P + 1])
    m.Ep = take("decay_pos", [P, TT, P + 1])
    m.Em = take("decay_neg", [P, TT, P + 1])
    m.cu = take("conv_in", [P, 2, T])
    m.cv = take("conv_sum", [P, T])
    m.rn = take("norm_rows", [16, T])
    m.onesP = take("ones_row", [P, P])
    take, at = area(m.x_at)
    m.sq = take("squares", [P, JT, T])
    m.w2a2 = take("w2_a2", [P, BR])
    m.wad = take("decay_iclr_lr", [P, T])
    m.gB = take("conv_gate", [P, 2, T])
    assert at[0] <= m.x_at + 4 * TT * D
    take, at = area(shared)
    m.Xi = take("inverse", [P, 2, 4, P])
    m.Ti = take("inverse_step", [P, 2, 4, P])
    m.rhs = take("chunk_rhs", [P, BR])
    m.sa = take("chunk_sa", [P, BR])
    m.S = take("state", [P, 2, JT, P])
    m.stmp = take("state_tmp", [P, JT, P])
    take, at = area(m.x_at)
    m.XTi = take("inverse_t", [P, 2, 2, 4, P])
    m.BKT = take("b_k_tokens", [P, 2, JT, P])
    assert at[0] <= m.x_at + 4 * TT * D
    m.SC = place("scores", [P, 2, 2 * JT, 4, P], F32, m.hT_at)
    take, at = area(shared)
    m.g2a = take("g2_a", [P, BR])
    m.g2b = take("g2_b", [32, BR])
    m.ysq = take("y_squares", [P, JT, T])
    m.rn2 = take("y_norm_rows", [16, T])
    take, at = area(m.APR_at)
    m.gain = take("row_gain", [P, D])
    m.otmp = take("out_tmp", [P, 2, D])

    take, at = area(m.arena)
    m.G_at = at[0]
    m.G = take("ffn_hidden", [P, FT, T])
    m.xn2 = place("x_normed_f", [P, TT, D], F32, m.G_at)
    m.gH = take("ffn_hi", [P, 2, 2, T], F32R)
    m.gL = take("ffn_lo", [P, 2, 2, T], F32R)
    m.cgu = take("ffn_conv", [P, 2, 2, T])
    m.gel = take("ffn_gelu", [P, 2, T])
    m.frow = take("ffn_rows", [P, 2, P])
    m.fcol = take("ffn_cols", [P, 2, P])
    m.fgain = take("ffn_gain", [P, D])
    m.ftmp = take("ffn_tmp", [P, 2, D])
    return m


def constants(pool, m):
    q = pool.eng

    def step(ins, name):
        ins.then_inc(pool.done, 1)
        pool.counted(name)
        pool.wait_ge(pool.sems["pool"], pool.at(name))

    step(q.memset(m.prow[:, :], 0.0), "prow zero")
    step(q.memset(m.ident[:, :], 0.0), "ident 0")
    step(q.affine_select(out=m.ident[:, :], in_=m.ident[:, :], compare_op=ALU.not_equal, fill=1.0, base=0,
                         pattern=[[-1, P]], channel_multiplier=1), "ident")
    step(q.memset(m.eps[:, 0:1], RMS_EPS), "table 1")
    step(q.memset(m.eps[:, 1:2], 1.0), "eps")
    step(q.memset(m.bd[:, :], 0.0), "table 2")
    step(q.memset(m.onesP[:, :], 1.0), "table 3")
    step(q.memset(m.indh[:, :, :], 0.0), "table 4")
    step(q.memset(m.zs[:, :, :], 0.0), "table 6")
    step(q.memset(m.Gx[:, :, :], 0.0), "table 7")
    step(q.memset(m.indw[:, :, :], 0.0), "zeros")
    step(q.memset(m.bd[0:64, 0:64], 1.0), "table 8")
    step(q.memset(m.bd[64:P, 64:P], 1.0), "table 9")
    hf = m.indh[:, :, :].rearrange("p a b -> p (a b)")
    step(q.memset(hf[0:64, 0:P:18], 1.0), "table 10")
    step(q.memset(hf[64:P, 1:P:18], 1.0), "table 11")
    step(q.memset(m.indw[:, :, :].rearrange("p a b -> p (a b)")[:, 0:64:9], 1.0), "table 12")
    step(q.memset(m.smask[:, :, :], 1.0), "table 14")
    step(q.memset(m.lmask[:, :, :], 0.0), "ones")
    for i in range(4):
        step(q.affine_select(out=m.smask[:, i, :], in_=m.smask[:, i, :], compare_op=ALU.is_ge if i % 2 else ALU.is_gt,
                        fill=0.0, base=0, pattern=[[1, P]], channel_multiplier=-1), ("table 15", i))
    lower = []
    for l in range(LEVELS):
        b = 1 << l
        v = m.lmask[:, l, :].rearrange("p (n h i) -> p n h i", h=2, i=b)[:, :, 0, :]
        lower.append((v, b))
        step(q.memset(v, 1.0), ("table 16", b))
    for v, b in lower:
        step(q.affine_select(out=v, in_=v, compare_op=ALU.is_ge, fill=0.0, base=-b,
                               pattern=[[-2 * b, P // (2 * b)], [0, b]], channel_multiplier=1), ("table 17", b))
    for v, b in lower:
        step(q.affine_select(out=v, in_=v, compare_op=ALU.is_ge, fill=0.0, base=2 * b - 1,
                               pattern=[[2 * b, P // (2 * b)], [0, b]], channel_multiplier=-1), ("table 18", b))
    step(q.memset(m.onesP[:, :], 1.0), "constants")


def norm_scalar(act, m, pf, ready):
    for t in range(TT):
        act.wait_ge(act.done, act.so_far())
        for before in ready[t]:
            act.wait_ge(*act.point(before))
        act.eng.activation(m.xn[:, t, :], m.x[:, t, :], ACT.Square, accum_out=m.stat[:, 0, t:t + 1]).then_inc(act.done, 1)
        act.counted((pf, "ss", t))
    act.wait_ge(act.done, act.so_far())
    act.eng.activation(m.stat[:, 1, :], m.stat[:, 0, :], ACT.Sqrt, bias=m.eps[:, 0:1], scale=1.0 / D).then_inc(act.done, 1)
    act.counted((pf, "sd"))


def norm_vector(dve, m, pf):
    dve.wait_ge(dve.done, dve.so_far())
    dve.wait_ge(dve.sems["act"], dve.at((pf, "sd")))
    dve.eng.reciprocal(m.stat[:, 2, :], m.stat[:, 1, :]).then_inc(dve.done, 1)
    dve.counted((pf, "rstd"))
    dve.wait_ge(dve.done, dve.so_far())
    for t in range(TT):
        dve.eng.tensor_scalar(m.xn[:, t, :], m.x[:, t, :], m.stat[:, 2, t:t + 1], None, ALU.mult).then_inc(dve.done, 1)
        dve.counted((pf, "xn", t))


def norm_split_scalar(act, m, pf, gcol):
    for j in range(KT):
        act.wait_ge(act.done, act.so_far())
        act.wait_ge(act.sems["pe"], act.at((pf, "turn", j)))
        act.eng.activation(m.hH[:, j, :], m.PS[:, 4 + j % 4, :], ACT.Copy, scale=gcol(j)).then_inc(act.done, 1)
        act.counted((pf, "hi", j))


def norm_split_vector(dve, m, pf, gcol):
    for j in range(KT):
        dve.wait_ge(dve.done, dve.so_far())
        dve.wait_ge(dve.sems["act"], dve.at((pf, "hi", j)))
        dve.eng.scalar_tensor_tensor(m.hL[:, j, :], m.PS[:, 4 + j % 4, :], gcol(j), m.hH[:, j, :].bitcast(F32),
                                     ALU.mult, ALU.subtract).then_inc(dve.done, 1)
        dve.counted((pf, "lo", j))


def split_hi(act, m, s, step, *need):
    act.wait_ge(act.done, act.so_far())
    for before in need:
        act.wait_ge(*act.point(before))
    act.eng.activation(m.wh[:, s, :], m.raw[:, s, :], ACT.Copy).then_inc(act.done, 1)
    act.counted(step)


def split_lo(dve, m, s, step, hi):
    dve.wait_ge(dve.done, dve.so_far())
    dve.wait_ge(dve.sems["act"], dve.at(hi))
    dve.eng.tensor_tensor(m.wl[:, s, :], m.raw[:, s, :], m.wh[:, s, :].bitcast(F32), ALU.subtract).then_inc(dve.done, 1)
    dve.counted(step)


def mix_out_scalar(act, m, pf, need):
    for t in range(TT):
        act.wait_ge(act.done, act.so_far())
        for before in need(t):
            act.wait_ge(*act.point(before))
        act.eng.activation(m.otmp[:, t % 2, :], m.PS[:, 2 * t:2 * t + 2, :].rearrange("p a b -> p (a b)"),
                           ACT.Square, accum_out=m.stat[:, 0, t:t + 1]).then_inc(act.done, 1)
        act.counted((pf, "ss", t))
    act.wait_ge(act.done, act.so_far())
    act.eng.activation(m.stat[:, 1, :], m.stat[:, 0, :], ACT.Sqrt, bias=m.eps[:, 0:1], scale=1.0 / D).then_inc(act.done, 1)
    act.counted((pf, "sd"))


def mix_out_vector(dve, m, pf):
    dve.wait_ge(dve.done, dve.so_far())
    dve.wait_ge(dve.sems["act"], dve.at((pf, "sd")))
    dve.eng.reciprocal(m.stat[:, 2, :], m.stat[:, 1, :]).then_inc(dve.done, 1)
    dve.counted((pf, "rstd"))
    dve.wait_ge(dve.done, dve.so_far())
    for t in range(TT):
        if t > 1:
            dve.wait_ge(dve.done, dve.so_far())
        dve.eng.scalar_tensor_tensor(m.otmp[:, t % 2, :], m.PS[:, 2 * t:2 * t + 2, :].rearrange("p a b -> p (a b)"),
                                     m.stat[:, 2, t:t + 1], m.gain[:, :], ALU.mult, ALU.mult).then_inc(dve.done, 1)
        dve.counted((pf, "out", t))
        dve.wait_ge(dve.done, dve.so_far())
        dve.eng.tensor_tensor(m.x[:, t, :], m.x[:, t, :], m.otmp[:, t % 2, :], ALU.add).then_inc(dve.done, 1)
        dve.counted((pf, "x", t))


class Banks:

    def __init__(self, pe):
        self.pe, self.reader = pe, {}

    def use(self, bank, reader):
        if bank in self.reader:
            self.pe.wait_ge(*self.pe.point(self.reader[bank]))
        self.reader[bank] = reader


def turn(pe, m, banks, step, bank, reader, blocks, rows=P):
    banks.use(bank, reader)
    m.bank[step] = bank
    for i, b in enumerate(blocks):
        n = b.shape[1]
        last = pe.eng.transpose(m.PS[0:n, bank, rows * i:rows * i + rows], b, m.ident[0:rows, 0:rows])
    last.then_inc(pe.done, 1)
    pe.counted(step)


def project(pe, m, w, x, out, kt=KT):
    for k in range(kt):
        for i, (a, b) in enumerate(((w[0], x[0]), (w[0], x[1]), (w[1], x[0]))):
            last = pe.eng.matmul(out, a(k), b(k), start=(k == 0 and i == 0), stop=(k == kt - 1 and i == 2))
    return last


def mixer(nc, m, A, steps, done, sems):
    pe_done, act_done, dve_done, pool_done = (done[n] for n in ("pe", "act", "dve", "pool"))
    PS = m.PS
    m.xn = m.xn1
    w_in, w_out = A["w_in"][0], A["w_out"][0]
    RC = 3 * BR
    panels = [(w_in, RC + 3 * BR, PW), (w_in, RC + 3 * BR + PW, 32)]
    panels += [(w_in, RC + c + PW * i, PW) for c in (BR, 0, 2 * BR) for i in range(2)]
    panels += [(w_in, c + PW * i, PW) for i in range(2) for c in (0, 2 * BR, BR)]
    NPROJ = len(panels)
    panels += [(w_out, PW * i, PW) for i in range(4)]
    NP = len(panels)
    w_loaded = sems("w_loaded0"), sems("w_loaded1")
    x_loaded = [sems(f"x_loaded{t}") for t in range(TT)]
    rows_loaded, lr_loaded, g2_loaded, gain_loaded = (sems(n) for n in ("rows_loaded", "lr_loaded", "g2_loaded",
                                                                        "gain_loaded"))

    def view(buf, p):
        return buf[:, p % 2, 0:KT * panels[p][2]].rearrange("p (k n) -> p k n", k=KT)

    ztiles = [(0, 0, P, ROW["mu_wa"], m.wad[:, :]), (0, 1, P, ROW["mu_g"], m.gd[:, :]), (1, 0, 32, ROW["mu_g"] + 1, m.gd2[:, :])]
    for p0, mu, dst in ((2, "mu_k", m.BK[:, 1]), (4, "mu_r", m.APR[:, 1]), (6, "mu_v", m.vq[:, :])):
        ztiles += [(p0 + j // 2, j % 2, P, ROW[mu] + j, dst[:, j, :]) for j in range(JT)]
    NZ = len(ztiles)

    def col(name, j=0, rows=P):
        return m.pcol[0:rows, ROW[name] + j:ROW[name] + j + 1]

    rowsrc = [(ROW["pre_mix"], A["pre_mix_g"].rearrange("l (a b) -> (l a) b", b=P)),
              (ROW["mu_r"], A["shift_mu"][:, 0:3 * BR + P].rearrange("l (a b) -> (l a) b", b=P)),
              (ROW["mu_g"], A["shift_mu"][:, 3 * BR + P:3 * BR + 2 * P]),
              (ROW["mu_g"] + 1, A["shift_mu"][:, 3 * BR + 2 * P:3 * BR + 2 * P + 32])]
    rowsrc += [(ROW[n], A[n].rearrange("l (a b) -> (l a) b", b=P)) for n in ("w0", "a0", "k_k", "k_a", "lnx_w", "lnx_b")]
    rowsrc += [(ROW["r_k"], A["r_k"].rearrange("l (a c) b -> (l a) (c b)", c=2)),
               (ROW["conv"], A["conv_a_w"].rearrange("l k (a b) -> (l k a) b", b=P))]

    with nc.Block() as block:

        @block.sync
        def _(sp):
            E = Engine(steps, "sp", sp, done)
            for t in range(TT):
                sp.dma_start(m.x[:, t, :], A["x"][0, P * t:P * t + P, :]).then_inc(x_loaded[t], 16)
            for p in range(NP):
                src, c, w = panels[p]
                if p >= 2:
                    E.wait_ge(dve_done, E.at(("w lo", p - 2)))
                s = src.rearrange("(k q) n -> q k n", q=P)
                for k in (0, 4):
                    sp.dma_start(view(m.raw, p)[:, k:k + 4, :], s[:, k:k + 4, c:c + w]).then_inc(w_loaded[p % 2], 16)
                if p == NPROJ + 1:
                    E.wait_ge(act_done, E.at(("y", TT - 1)))
                    for t in range(TT):
                        sp.dma_start(m.x[:, t, :], A["x"][0, P * t:P * t + P, :]).then_inc(x_loaded[t], 16)
                    E.wait_ge(dve_done, E.at(("mix", JT - 1)))
                    sp.dma_start(m.gain[:, :], A["post_mix_g"].partition_broadcast(P)).then_inc(gain_loaded, 16)

        @block.gpsimd
        def _(pool):
            E = Engine(steps, "pool", pool, done)
            constants(E, m)

        @block.tensor
        def _(pe):
            E = Engine(steps, "pe", pe, done)
            banks = Banks(E)
            aux = [0]

            def aux_bank(reader):
                b = 4 + aux[0] % 4
                aux[0] += 1
                banks.use(b, reader)
                return b

            def turned(step, reader, blocks, rows=P):
                b = 4 + aux[0] % 4
                aux[0] += 1
                turn(E, m, banks, step, b, reader, blocks, rows)

            def one(step, reader, lhsT, rhs):
                b = aux_bank(reader)
                m.bank[step] = b
                pe.matmul(PS[0:lhsT.shape[1], b, :], lhsT, rhs, start=True, stop=True).then_inc(pe_done, 1)
                E.counted(step)

            def panel(p):
                E.wait_ge(dve_done, E.at(("w lo", p)))
                H, L = view(m.wh, p), view(m.wl, p)
                for i in range((panels[p][2] + P - 1) // P):
                    n = min(P, panels[p][2] - P * i)
                    b, c = 2 * (p % 2) + i, slice(P * i, P * i + n)
                    banks.use(b, ("evac", p, i))
                    project(E, m, (lambda k: H[:, k, c], lambda k: L[:, k, c]),
                            (lambda k: m.hH[:, k, :], lambda k: m.hL[:, k, :]), PS[0:n, b, :]).then_inc(pe_done, 1)
                    E.counted(("panel", p, i))

            E.wait_ge(pool_done, E.at("ident"))
            E.wait_ge(pool_done, E.at("constants"))
            pe.wait_ge(rows_loaded, 16 * len(rowsrc))
            turned("turn params", "params", [m.prow[:, :]])
            for q in range(2):
                turned(("turn indh", q), ("indh", q), [m.indh[:, 4 * q + i, :] for i in range(4)])
            turned(("turn indw", 0), ("indw", 0), [m.indw[:, i, :] for i in range(4)])
            E.wait_ge(dve_done, E.at(("n1", "xn", TT - 1)))
            aux[0] = 0
            for j in range(KT):
                turned(("n1", "turn", j), ("n1", "lo", j), [m.xn[:, t, P * j:P * j + P] for t in range(TT)])
            turned(("turn indw", 1), ("indw", 1), [m.indw[:, 4 + i, :] for i in range(4)])
            E.wait_ge(dve_done, E.at(("n1", "lo", KT - 1)))
            for p in range(8):
                panel(p)
            E.wait_ge(act_done, E.at("tanh"))
            pe.wait_ge(lr_loaded, 32)
            for j in range(JT):
                one(("zw", j), ("wsig", j), m.w2a2[0:64, P * j:P * j + P], m.wad[0:64, :])
                one(("za", j), ("a", j), m.w2a2[64:P, P * j:P * j + P], m.wad[64:P, :])
            for c in range(TT):
                E.wait_ge(dve_done, E.at(("q", NZ - 1)))
                turned(("turn v", c), ("v tokens", c), [m.vq[:, j, P * c:P * c + P] for j in range(JT)])
            b = m.bank["ss"] = aux_bank("ss max")
            for j in range(JT):
                E.wait_ge(act_done, E.at(("kk sq", j)))
                last = pe.matmul(PS[0:16, b, :], m.indh[:, j, :], m.sq[:, j, :], start=(j == 0), stop=(j == JT - 1))
            last.then_inc(pe_done, 1)
            E.counted("ss")
            panel(8)
            panel(9)
            E.wait_ge(dve_done, E.at("rn"))
            E.wait_ge(act_done, E.at(("indh", 1)))
            for j in range(JT):
                one(("rn spread", j), ("kkn", j), m.indhT[0:16, j, :], m.rn[:, :])
            panel(10)
            panel(11)
            for j in range(JT):
                E.wait_ge(dve_done, E.at(("rkr", j)))
                one(("bonus", j), ("bonus v", j), m.bd[:, :], m.sq[:, j, :])
            panel(12)
            panel(13)

            def scores(c, hf):
                for i in range(4):
                    j, e = 2 * hf + i // 2, i % 2
                    rows, cc, b = slice(64 * e, 64 * e + 64), slice(P * c, P * c + P), 4 * hf + i
                    banks.use(b, ("scores", c, hf, i))
                    for q in range(2):
                        last = pe.matmul(PS[:, b, 256 * q:256 * q + 256], m.BK[rows, q, j, cc], m.APR[rows, :, j, cc],
                                         start=True, stop=True)
                    last.then_inc(pe_done, 1)
                    E.counted(("score mm", c, hf, i))

            def level(c, l, hf):
                b = 4 * hf
                E.wait_ge(dve_done, E.at(("scores", c, hf, 3) if l == 0 else ("X", c, l - 1, hf)))
                banks.use(b, ("T", c, l, hf))
                for i in range(4):
                    r = m.ident[:, :] if l == 0 else m.Xi[:, hf, i, :]
                    last = pe.matmul(PS[:, b, P * i:P * i + P], m.SC[:, c % 2, 4 * hf + i, 0, :], r, start=True, stop=True)
                last.then_inc(pe_done, 1)
                E.counted(("NX", c, l, hf))

            def update(c, l, hf):
                E.wait_ge(dve_done, E.at(("T", c, l, hf)))
                if l > 0:
                    E.wait_ge(dve_done, E.at(("XT", c, l - 1, hf)))
                if 0 < l < LEVELS - 1:
                    banks.use(4 * hf + 1, ("X", c, l, hf))
                    for i in range(4):
                        last = pe.matmul(PS[:, 4 * hf + 1, P * i:P * i + P], m.XTi[:, c % 2, hf, i, :], m.Ti[:, hf, i, :],
                                         start=True, stop=True)
                    last.then_inc(pe_done, 1)
                    E.counted(("dX", c, l, hf))
                banks.use(4 * hf + 2, ("XT", c, l, hf))
                for i in range(4):
                    o = PS[:, 4 * hf + 2, P * i:P * i + P]
                    if l == 0:
                        last = pe.transpose(o, m.Ti[:, hf, i, :], m.ident[:, :])
                    else:
                        last = pe.matmul(o, m.Ti[:, hf, i, :], m.XTi[:, c % 2, hf, i, :], start=True, stop=True)
                last.then_inc(pe_done, 1)
                E.counted(("dXT", c, l, hf))

            def state(c, step):
                par, cc = c % 2, slice(P * c, P * c + P)
                if step == 0:
                    for q in range(2):
                        turn(E, m, banks, ("turn bk", c, q), 3 + 4 * q, ("bk tokens", c, q),
                             [m.BK[:, q, j, cc] for j in range(JT)])
                if step == 1:
                    banks.use(3, ("rhs", c))
                    E.wait_ge(dve_done, E.at(("S", c - 1) if c else "S 0"))
                    for j in range(JT):
                        pe.matmul(PS[:, 3, P * j:P * j + P], m.APR[:, 0, j, cc], m.S[:, par, j, :], start=True, stop=False,
                                  skip_group_check=True)
                        for e in range(2):
                            h = 2 * j + e
                            last = pe.matmul(PS[:, 3, 64 * h:64 * h + 64], m.SC[:, par, h, 2, :],
                                             m.Vt[:, c, 64 * h:64 * h + 64], start=False, stop=True, skip_group_check=True)
                    last.then_inc(pe_done, 1)
                    E.counted(("rhs mm", c))
                if step == 2:
                    banks.use(7, ("sa", c))
                    E.wait_ge(act_done, E.at(("rhs", c)))
                    E.wait_ge(dve_done, E.at(("XT", c, LEVELS - 1, 0)))
                    E.wait_ge(dve_done, E.at(("XT", c, LEVELS - 1, 1)))
                    for h in range(2 * JT):
                        last = pe.matmul(PS[:, 7, 64 * h:64 * h + 64], m.XTi[:, par, h // 4, h % 4, :],
                                         m.rhs[:, 64 * h:64 * h + 64], start=True, stop=True)
                    last.then_inc(pe_done, 1)
                    E.counted(("sa mm", c))
                if step == 3 and c < TT - 1:
                    banks.use(3, ("S add", c))
                    E.wait_ge(act_done, E.at(("sa", c)))
                    E.wait_ge(act_done, E.at(("bk tokens", c, 0)))
                    E.wait_ge(act_done, E.at(("bk tokens", c, 1)))
                    for j in range(JT):
                        o = PS[:, 3, P * j:P * j + P]
                        pe.matmul(o, m.BKT[:, 0, j, :], m.sa[:, P * j:P * j + P], start=True, stop=False)
                        last = pe.matmul(o, m.BKT[:, 1, j, :], m.Vt[:, c, P * j:P * j + P], start=False, stop=True)
                    last.then_inc(pe_done, 1)
                    E.counted(("S mm", c))
                if step == 4:
                    banks.use(7, ("y", c))
                    for j in range(JT):
                        pe.matmul(PS[:, 7, P * j:P * j + P], m.S[:, par, j, :], m.APR[:, 1, j, cc], start=True, stop=False,
                                  skip_group_check=True)
                        for e in range(2):
                            h = 2 * j + e
                            o = PS[64 * e:64 * e + 64, 7, P * j:P * j + P]
                            pe.matmul(o, m.sa[:, 64 * h:64 * h + 64], m.SC[:, par, h, 1, :], start=False, stop=False,
                                      skip_group_check=True)
                            last = pe.matmul(o, m.Vt[:, c, 64 * h:64 * h + 64], m.SC[:, par, h, 3, :], start=False,
                                             stop=True, skip_group_check=True)
                    last.then_inc(pe_done, 1)
                    E.counted(("y mm", c))

            for before in [("prep", j) for j in range(JT)]:
                E.wait_ge(*E.point(before))
            E.wait_ge(*E.point(("v tokens", TT - 1)))
            for c in range(TT + 1):
                if c < TT:
                    scores(c, 0)
                    scores(c, 1)
                for l in range(LEVELS):
                    if c < TT:
                        for hf in range(2):
                            level(c, l, hf)
                        for hf in range(2):
                            update(c, l, hf)
                    if c > 0 and l < 5:
                        state(c - 1, l)

            aux[0] = 0
            E.wait_ge(act_done, E.at(("y", TT - 1)))
            for j in range(JT):
                one(("y mean", j), ("y centred", j), m.bd[:, :], m.yT[:, j, :])
            pe.wait_ge(g2_loaded, 32)
            for j in range(JT):
                banks.use(j, ("mix", j))
                pe.matmul(PS[:, j, :], m.g2a[:, P * j:P * j + P], m.gd[:, :], start=True, stop=False)
                pe.matmul(PS[:, j, :], m.g2b[:, P * j:P * j + P], m.gd2[:, :], start=False, stop=True).then_inc(pe_done, 1)
                E.counted(("gate", j))
            b = m.bank["y ss"] = aux_bank("y var")
            for j in range(JT):
                E.wait_ge(act_done, E.at(("y sq", j)))
                last = pe.matmul(PS[0:16, b, :], m.indh[:, j, :], m.ysq[:, j, :], start=(j == 0), stop=(j == JT - 1))
            last.then_inc(pe_done, 1)
            E.counted("y ss")
            E.wait_ge(dve_done, E.at("y rstd"))
            for j in range(JT):
                one(("y rstd spread", j), ("y scaled", j), m.indhT[0:16, j, :], m.rn2[:, :])
            E.wait_ge(dve_done, E.at(("mix lo", KT - 1)))
            for i in range(4):
                p = NPROJ + i
                E.wait_ge(dve_done, E.at(("w lo", p)))
                H, L = view(m.wh, p), view(m.wl, p)
                for t in range(TT):
                    b, tt = 2 * t + i // 2, slice(P * t, P * t + P)
                    if i % 2 == 0:
                        banks.use(b, ("n2", "out", t))
                    last = project(E, m, (lambda k: m.hH[:, k, tt], lambda k: m.hL[:, k, tt]),
                                   (lambda k: H[:, k, :], lambda k: L[:, k, :]), PS[:, b, PW * (i % 2):PW * (i % 2) + PW])
                    last.then_inc(pe_done, 1)
                    E.counted(("out mm", i, t))

        @block.scalar
        def _(act):
            E = Engine(steps, "act", act, done)
            E.wait_ge(act_done, E.so_far())
            E.wait_ge(pool_done, E.at("prow zero"))
            for r0, src in rowsrc:
                n, w = src.shape
                act.dma_start(m.prow[r0:r0 + n, 0:w], src).then_inc(rows_loaded, 16)
            E.wait_ge(act_done, E.so_far())
            E.wait_ge(pool_done, E.at("eps"))
            for t in range(TT):
                act.wait_ge(x_loaded[t], 16)
                act.activation(m.xn[:, t, :], m.x[:, t, :], ACT.Square, accum_out=m.stat[:, 0, t:t + 1]).then_inc(act_done, 1)
                E.counted(("n1", "ss", t))
            E.wait_ge(act_done, E.so_far())
            act.activation(m.stat[:, 1, :], m.stat[:, 0, :], ACT.Sqrt, bias=m.eps[:, 0:1], scale=1.0 / D).then_inc(act_done, 1)
            E.counted(("n1", "sd"))

            def split(p):
                act.wait_ge(w_loaded[p % 2], 32 * (p // 2 + 1))
                if p >= 2:
                    last = (panels[p - 2][2] + P - 1) // P - 1
                    E.wait_ge(act_done, E.so_far())
                    E.wait_ge(pe_done, E.at(("panel", p - 2, last) if p - 2 < NPROJ else ("out mm", p - 2 - NPROJ, TT - 1)))
                n = KT * panels[p][2]
                act.activation(m.wh[:, p % 2, 0:n], m.raw[:, p % 2, 0:n], ACT.Copy).then_inc(act_done, 1)
                E.counted(("w hi", p))

            split(0)
            split(1)
            for q in range(2):
                E.wait_ge(act_done, E.so_far())
                E.wait_ge(pe_done, E.at(("turn indh", q)))
                act.activation(m.indhT[0:16, 4 * q:4 * q + 4, :].rearrange("p a b -> p (a b)"),
                               PS[0:16, m.bank["turn indh", q], :], ACT.Copy).then_inc(act_done, 1)
                E.counted(("indh", q))
            for q in (0,):
                E.wait_ge(act_done, E.so_far())
                E.wait_ge(pe_done, E.at(("turn indw", q)))
                act.activation(m.indwT[0:8, 4 * q:4 * q + 4, :].rearrange("p a b -> p (a b)"),
                               PS[0:8, m.bank["turn indw", q], :], ACT.Copy).then_inc(act_done, 1)
                E.counted(("indw", q))
            E.wait_ge(act_done, E.so_far())
            E.wait_ge(dve_done, E.at("params"))
            norm_split_scalar(E, m, "n1", lambda j: col("pre_mix", j))
            for q in (1,):
                E.wait_ge(act_done, E.so_far())
                E.wait_ge(pe_done, E.at(("turn indw", q)))
                act.activation(m.indwT[0:8, 4 * q:4 * q + 4, :].rearrange("p a b -> p (a b)"),
                               PS[0:8, m.bank["turn indw", q], :], ACT.Copy).then_inc(act_done, 1)
                E.counted(("indw", q))
            E.wait_ge(act_done, E.so_far())
            E.wait_ge(dve_done, E.at(("n1", "xn", TT - 1)))
            act.dma_start(m.w2a2[0:64, :], A["w2"][0]).then_inc(lr_loaded, 16)
            act.dma_start(m.w2a2[64:P, :], A["a2"][0]).then_inc(lr_loaded, 16)
            z = 0
            for p in range(8):
                while z < NZ and ztiles[z][0] == p:
                    _, i, rows, mu, _ = ztiles[z]
                    E.wait_ge(act_done, E.so_far())
                    E.wait_ge(pe_done, E.at(("panel", p, i)))
                    if z >= 2:
                        E.wait_ge(act_done, E.so_far())
                        E.wait_ge(dve_done, E.at(("q", z - 2)))
                    act.activation(m.zs[0:rows, z % 2, 1:T + 1], PS[0:rows, 2 * (p % 2) + i, :], ACT.Copy,
                                   scale=m.pcol[0:rows, mu:mu + 1]).then_inc(act_done, 1)
                    E.counted(("mu q", z))
                    z += 1
                split(p + 2)
                if p == 1:
                    E.wait_ge(act_done, E.so_far())
                    E.wait_ge(dve_done, E.at(("q", 2)))
                    act.activation(m.wad[0:64, :], m.wad[0:64, :], ACT.Tanh).then_inc(act_done, 1)
                    E.counted("tanh")
                    act.activation(m.gd[:, :], m.gd[:, :], ACT.Sigmoid).then_inc(act_done, 1)
                    E.counted("gd")
                    act.activation(m.gd2[:, :], m.gd2[:, :], ACT.Sigmoid).then_inc(act_done, 1)
                    E.counted("gd2")
                if p == 4:
                    for j in range(JT):
                        E.wait_ge(act_done, E.so_far())
                        E.wait_ge(dve_done, E.at(("kk", j)))
                        act.activation(m.sq[:, j, :], m.APR[:, 0, j, :], ACT.Square).then_inc(act_done, 1)
                        E.counted(("kk sq", j))
            for j in range(JT):
                E.wait_ge(act_done, E.so_far())
                E.wait_ge(pe_done, E.at(("zw", j)))
                act.activation(m.bv[:, j, :], PS[:, m.bank["zw", j], :], ACT.Sigmoid, bias=col("w0", j)).then_inc(act_done, 1)
                E.counted(("wsig", j))
                E.wait_ge(act_done, E.so_far())
                E.wait_ge(pe_done, E.at(("za", j)))
                act.activation(m.BK[:, 0, j, :], PS[:, m.bank["za", j], :], ACT.Sigmoid, bias=col("a0", j)).then_inc(act_done, 1)
                E.counted(("a", j))
            for c in range(TT):
                E.wait_ge(act_done, E.so_far())
                E.wait_ge(pe_done, E.at(("turn v", c)))
                act.activation(m.Vt[:, c, :], PS[:, m.bank["turn v", c], :], ACT.Copy).then_inc(act_done, 1)
                E.counted(("v tokens", c))
            E.wait_ge(act_done, E.so_far())
            E.wait_ge(dve_done, E.at("ss max"))
            act.activation(m.rn[:, :], m.rn[:, :], ACT.Sqrt).then_inc(act_done, 1)
            E.counted("kk norm")

            def conv_gate(p):
                for i in range(2):
                    E.wait_ge(act_done, E.so_far())
                    E.wait_ge(pe_done, E.at(("panel", p, i)))
                    if p > 8:
                        E.wait_ge(act_done, E.so_far())
                        E.wait_ge(dve_done, E.at(("conv in", p - 2, i)))
                    act.activation(m.gB[:, i, :], PS[:, 2 * (p % 2) + i, :], ACT.Copy).then_inc(act_done, 1)
                    E.counted(("evac", p, i))

            def decays(j):
                E.wait_ge(act_done, E.so_far())
                E.wait_ge(dve_done, E.at(("decay mid", j)))
                if j:
                    E.wait_ge(act_done, E.so_far())
                    E.wait_ge(dve_done, E.at(("prep", j - 1)))
                act.activation(m.emid[:, j, :], m.Gx[:, :, 64], ACT.Exp, scale=-DECAY).then_inc(act_done, 1)
                E.counted(("emid", j))
                act.activation(m.Ep[:, :, :], m.Gc[:, :, :], ACT.Exp, scale=-DECAY).then_inc(act_done, 1)
                E.counted(("Ep", j))
                act.activation(m.Em[:, :, :], m.Gc[:, :, :], ACT.Exp, scale=DECAY).then_inc(act_done, 1)
                E.counted(("Em", j))

            conv_gate(8)
            split(10)
            split(11)
            decays(0)
            decays(1)
            split(12)
            decays(2)
            conv_gate(11)
            split(13)
            decays(3)
            split(14)
            split(15)

            for c in range(TT + 1):
                for l in range(5):
                    if c == 0:
                        continue
                    cc = slice(P * (c - 1), P * c)
                    if l == 0:
                        for q in range(2):
                            E.wait_ge(act_done, E.so_far())
                            E.wait_ge(pe_done, E.at(("turn bk", c - 1, q)))
                            if c > 1:
                                E.wait_ge(act_done, E.so_far())
                                E.wait_ge(pe_done, E.at(("S mm", c - 2)))
                            act.activation(m.BKT[:, q, :, :], PS[:, 3 + 4 * q, :], ACT.Copy).then_inc(act_done, 1)
                            E.counted(("bk tokens", c - 1, q))
                    if l == 1:
                        E.wait_ge(act_done, E.so_far())
                        E.wait_ge(pe_done, E.at(("rhs mm", c - 1)))
                        act.activation(m.rhs[:, :], PS[:, 3, :], ACT.Copy).then_inc(act_done, 1)
                        E.counted(("rhs", c - 1))
                    if l == 2:
                        E.wait_ge(act_done, E.so_far())
                        E.wait_ge(pe_done, E.at(("sa mm", c - 1)))
                        act.activation(m.sa[:, :], PS[:, 7, :], ACT.Copy).then_inc(act_done, 1)
                        E.counted(("sa", c - 1))
                    if l == 4:
                        E.wait_ge(act_done, E.so_far())
                        E.wait_ge(pe_done, E.at(("y mm", c - 1)))
                        act.activation(m.yT[:, :, cc], PS[:, 7, :].rearrange("p (a b) -> p a b", a=JT), ACT.Copy).then_inc(act_done, 1)
                        E.counted(("y", c - 1))
            act.dma_start(m.g2a[:, :], A["g2"][0, 0:P, :]).then_inc(g2_loaded, 16)
            act.dma_start(m.g2b[:, :], A["g2"][0, P:P + 32, :]).then_inc(g2_loaded, 16)
            for j in range(JT):
                act.activation(m.hH[:, j, :], m.ya[:, j, :], ACT.Copy).then_inc(act_done, 1)
                E.counted(("mix hi", j))
            for j in range(JT):
                E.wait_ge(act_done, E.so_far())
                E.wait_ge(dve_done, E.at(("y centred", j)))
                act.activation(m.ysq[:, j, :], m.yT[:, j, :], ACT.Square).then_inc(act_done, 1)
                E.counted(("y sq", j))
            E.wait_ge(act_done, E.so_far())
            E.wait_ge(dve_done, E.at("y var"))
            act.activation(m.rn2[:, :], m.rn2[:, :], ACT.Sqrt).then_inc(act_done, 1)
            E.counted("y sd")
            for j in range(JT):
                E.wait_ge(act_done, E.so_far())
                E.wait_ge(dve_done, E.at(("mix", j)))
                act.activation(m.hH[:, JT + j, :], m.yT[:, j, :], ACT.Copy).then_inc(act_done, 1)
                E.counted(("mix hi", JT + j))
            split(16)
            split(17)
            mix_out_scalar(E, m, "n2", lambda t: [("out mm", 3, t)])

        @block.vector
        def _(dve):
            E = Engine(steps, "dve", dve, done)
            E.wait_ge(dve_done, E.so_far())
            E.wait_ge(pe_done, E.at("turn params"))
            dve.tensor_copy(m.pcol[:, :], PS[:, m.bank["turn params"], 0:P]).then_inc(dve_done, 1)
            E.counted("params")
            E.wait_ge(dve_done, E.so_far())
            mus = ROW["w0"] - ROW["mu_r"]
            dve.tensor_scalar(m.omm[:, 0:mus], m.pcol[:, ROW["mu_r"]:ROW["w0"]], -1.0, 1.0, ALU.mult, ALU.add).then_inc(dve_done, 1)
            E.counted("1 - mu")
            dve.tensor_scalar(m.omm[:, 16:20], m.pcol[:, ROW["k_a"]:ROW["k_a"] + 4], -1.0, 1.0, ALU.mult, ALU.add).then_inc(dve_done, 1)
            E.counted("1 - k_a")
            norm_vector(E, m, "n1")

            def split(p):
                n = KT * panels[p][2]
                E.wait_ge(dve_done, E.so_far())
                E.wait_ge(act_done, E.at(("w hi", p)))
                dve.tensor_tensor(m.wl[:, p % 2, 0:n], m.raw[:, p % 2, 0:n], m.wh[:, p % 2, 0:n].bitcast(F32),
                                  ALU.subtract).then_inc(dve_done, 1)
                E.counted(("w lo", p))

            split(0)
            split(1)
            norm_split_vector(E, m, "n1", lambda j: col("pre_mix", j))
            z = 0
            E.wait_ge(dve_done, E.so_far())
            for p in range(8):
                while z < NZ and ztiles[z][0] == p:
                    _, i, rows, mu, dst = ztiles[z]
                    E.wait_ge(dve_done, E.so_far())
                    E.wait_ge(act_done, E.at(("mu q", z)))
                    dve.scalar_tensor_tensor(dst, PS[0:rows, 2 * (p % 2) + i, :],
                                             m.omm[0:rows, mu - ROW["mu_r"]:mu - ROW["mu_r"] + 1],
                                             m.zs[0:rows, z % 2, 0:T], ALU.mult, ALU.add).then_inc(dve_done, 1)
                    E.counted(("q", z))
                    steps.found["evac", p, i] = steps.found["q", z]
                    z += 1
                    if p in (2, 3):
                        j = z - 4
                        E.wait_ge(dve_done, E.so_far())
                        dve.tensor_scalar(m.APR[:, 0, j, :], m.BK[:, 1, j, :], col("k_k", j), None, ALU.mult).then_inc(dve_done, 1)
                        E.counted(("kk", j))
                split(p + 2)
            E.wait_ge(dve_done, E.so_far())
            E.wait_ge(pe_done, E.at("ss"))
            dve.tensor_scalar(m.rn[:, :], PS[0:16, m.bank["ss"], :], 1e-24, None, ALU.max).then_inc(dve_done, 1)
            E.counted("ss max")
            for j in range(JT):
                E.wait_ge(dve_done, E.so_far())
                E.wait_ge(act_done, E.at(("a", j)))
                dve.tensor_scalar(m.cv[:, :], m.BK[:, 0, j, :], col("k_a", j), m.omm[:, 16 + j:17 + j], ALU.mult,
                                  ALU.add).then_inc(dve_done, 1)
                E.counted(("k scale", j))
                E.wait_ge(dve_done, E.so_far())
                dve.tensor_tensor(m.BK[:, 1, j, :], m.BK[:, 1, j, :], m.cv[:, :], ALU.mult).then_inc(dve_done, 1)
                E.counted(("k4", j))
                E.wait_ge(dve_done, E.so_far())
                dve.scalar_tensor_tensor(m.sq[:, j, :], m.BK[:, 1, j, :], col("r_k", j), m.APR[:, 1, j, :], ALU.mult,
                                         ALU.mult).then_inc(dve_done, 1)
                E.counted(("rkr", j))
            E.wait_ge(dve_done, E.so_far())
            E.wait_ge(act_done, E.at("kk norm"))
            dve.reciprocal(m.rn[:, :], m.rn[:, :]).then_inc(dve_done, 1)
            E.counted("rn")

            def conv_in(p):
                for i in range(2):
                    E.wait_ge(dve_done, E.so_far())
                    E.wait_ge(act_done, E.at(("evac", p - 1, i)))
                    E.wait_ge(pe_done, E.at(("panel", p, i)))
                    dve.tensor_tensor(m.cu[:, i, :], PS[:, 2 * (p % 2) + i, :], m.gB[:, i, :], ALU.mult).then_inc(dve_done, 1)
                    E.counted(("conv in", p, i))
                    steps.found["evac", p, i] = steps.found["conv in", p, i]

            def conv_out(p):
                for i in range(2):
                    j = (p - 10) // 3 * 2 + i
                    E.wait_ge(dve_done, E.so_far())
                    tap = lambda k: col("conv", 4 * k + j)
                    dve.tensor_scalar(m.cv[:, :], m.cu[:, i, :], tap(2), None, ALU.mult).then_inc(dve_done, 1)
                    E.counted(("tap 2", j))
                    E.wait_ge(dve_done, E.so_far())
                    dve.scalar_tensor_tensor(m.cv[:, 1:T], m.cu[:, i, 0:T - 1], tap(1), m.cv[:, 1:T], ALU.mult,
                                             ALU.add).then_inc(dve_done, 1)
                    E.counted(("tap 1", j))
                    E.wait_ge(dve_done, E.so_far())
                    dve.scalar_tensor_tensor(m.cv[:, 2:T], m.cu[:, i, 0:T - 2], tap(0), m.cv[:, 2:T], ALU.mult,
                                             ALU.add).then_inc(dve_done, 1)
                    E.counted(("tap 0", j))
                    E.wait_ge(dve_done, E.so_far())
                    E.wait_ge(pe_done, E.at(("panel", p, i)))
                    dve.tensor_tensor(m.ya[:, j, :], PS[:, 2 * (p % 2) + i, :], m.cv[:, :], ALU.mult).then_inc(dve_done, 1)
                    E.counted(("ya", j))
                    steps.found["evac", p, i] = steps.found["ya", j]

            def prep(j):
                for c in range(TT):
                    if j:
                        E.wait_ge(dve_done, E.so_far())
                        E.wait_ge(act_done, E.at(("emid", j - 1)))
                    dve.tensor_tensor_scan(m.Gx[:, c, 1:P + 1], m.onesP[:, :], m.bv[:, j, P * c:P * c + P], 0.0,
                                           ALU.mult, ALU.add).then_inc(dve_done, 1)
                    E.counted(("decay sum", j, c))
                E.wait_ge(dve_done, E.so_far())
                if j:
                    E.wait_ge(dve_done, E.so_far())
                    E.wait_ge(act_done, E.at(("Em", j - 1)))
                dve.tensor_tensor(m.Gc[:, :, :], m.Gx[:, :, :], m.Gx[:, :, 64:65].to_broadcast([P, TT, P + 1]),
                                  ALU.subtract).then_inc(dve_done, 1)
                E.counted(("decay mid", j))
                E.wait_ge(dve_done, E.so_far())
                E.wait_ge(pe_done, E.at(("rn spread", j)))
                dve.tensor_tensor(m.APR[:, 0, j, :], PS[:, m.bank["rn spread", j], :], m.APR[:, 0, j, :], ALU.mult).then_inc(dve_done, 1)
                E.counted(("kkn", j))
                E.wait_ge(dve_done, E.so_far())
                dve.tensor_tensor(m.BK[:, 0, j, :], m.BK[:, 0, j, :], m.APR[:, 0, j, :], ALU.mult).then_inc(dve_done, 1)
                E.counted(("kk a", j))
                E.wait_ge(dve_done, E.so_far())
                E.wait_ge(act_done, E.at(("Em", j)))
                r = lambda ap: ap.rearrange("p (a b) -> p a b", a=TT)
                dve.tensor_tensor(m.fac[:, j, 0:TT - 1], m.Ep[:, 0:TT - 1, P], m.emid[:, j, 1:TT], ALU.mult).then_inc(dve_done, 1)
                E.counted(("fac", j))
                dve.tensor_tensor(r(m.APR[:, 1, j, :]), r(m.APR[:, 1, j, :]), m.Ep[:, :, 1:P + 1], ALU.mult)
                dve.tensor_tensor(r(m.BK[:, 1, j, :]), r(m.BK[:, 1, j, :]), m.Em[:, :, 1:P + 1], ALU.mult)
                dve.tensor_tensor(r(m.APR[:, 0, j, :]), r(m.APR[:, 0, j, :]), m.Ep[:, :, 0:P], ALU.mult)
                dve.scalar_tensor_tensor(r(m.BK[:, 0, j, :]), r(m.BK[:, 0, j, :]), -1.0, m.Em[:, :, 1:P + 1], ALU.mult,
                                         ALU.mult).then_inc(dve_done, 1)
                E.counted(("prep", j))

            conv_in(9)
            split(10)
            split(11)
            prep(0)
            prep(1)
            conv_out(10)
            split(12)
            prep(2)
            split(13)
            prep(3)
            conv_in(12)
            split(14)
            for j in range(JT):
                E.wait_ge(dve_done, E.so_far())
                E.wait_ge(pe_done, E.at(("bonus", j)))
                dve.tensor_tensor(m.bv[:, j, :], PS[:, m.bank["bonus", j], :], m.vq[:, j, :], ALU.mult).then_inc(dve_done, 1)
                E.counted(("bonus v", j))
            conv_out(13)
            split(15)
            dve.memset(m.S[:, 0, :, :], 0.0).then_inc(dve_done, 1)
            E.counted("S 0")

            def four(ap2):
                return bass.AP(tensor=ap2.tensor, offset=ap2.offset, ap=[ap2.ap[0], [0, 4], ap2.ap[1]])

            def f4(ap):
                return ap.rearrange("p (a b) -> p a b", a=4)

            for c in range(TT + 1):
                par = c % 2
                if c < TT:
                    for hf in range(2):
                        for i in range(4):
                            E.wait_ge(dve_done, E.so_far())
                            E.wait_ge(pe_done, E.at(("score mm", c, hf, i)))
                            if c > 1:
                                E.wait_ge(dve_done, E.so_far())
                                E.wait_ge(pe_done, E.at(("y mm", c - 2)))
                            dve.tensor_tensor(m.SC[:, par, 4 * hf + i, :, :], f4(PS[:, 4 * hf + i, :]),
                                              m.smask[:, :, :], ALU.mult).then_inc(dve_done, 1)
                            E.counted(("scores", c, hf, i))
                for l in range(LEVELS):
                    if c < TT:
                        for hf in range(2):
                            E.wait_ge(dve_done, E.so_far())
                            E.wait_ge(pe_done, E.at(("NX", c, l, hf)))
                            dve.tensor_tensor(m.Ti[:, hf, :, :], f4(PS[:, 4 * hf, :]), four(m.lmask[:, l, :]), ALU.mult).then_inc(dve_done, 1)
                            E.counted(("T", c, l, hf))
                        for hf in range(2):
                            if l == 0:
                                E.wait_ge(dve_done, E.so_far())
                                dve.tensor_tensor(m.Xi[:, hf, :, :], m.Ti[:, hf, :, :], four(m.ident[:, :]), ALU.add).then_inc(dve_done, 1)
                                E.counted(("X", c, l, hf))
                                E.wait_ge(dve_done, E.so_far())
                                E.wait_ge(pe_done, E.at(("dXT", c, l, hf)))
                                if c > 1:
                                    E.wait_ge(dve_done, E.so_far())
                                    E.wait_ge(pe_done, E.at(("sa mm", c - 2)))
                                dve.tensor_tensor(m.XTi[:, par, hf, :, :], f4(PS[:, 4 * hf + 2, :]),
                                                  four(m.ident[:, :]), ALU.add).then_inc(dve_done, 1)
                                E.counted(("XT", c, l, hf))
                                continue
                            if l < LEVELS - 1:
                                E.wait_ge(dve_done, E.so_far())
                                E.wait_ge(pe_done, E.at(("dX", c, l, hf)))
                                dve.tensor_tensor(m.Xi[:, hf, :, :], f4(PS[:, 4 * hf + 1, :]), m.Xi[:, hf, :, :],
                                                  ALU.add).then_inc(dve_done, 1)
                                E.counted(("X", c, l, hf))
                            E.wait_ge(dve_done, E.so_far())
                            E.wait_ge(pe_done, E.at(("dXT", c, l, hf)))
                            dve.tensor_tensor(m.XTi[:, par, hf, :, :], f4(PS[:, 4 * hf + 2, :]),
                                              m.XTi[:, par, hf, :, :], ALU.add).then_inc(dve_done, 1)
                            E.counted(("XT", c, l, hf))
                    if 0 < c < TT and l == 3:
                        q = (c - 1) % 2
                        E.wait_ge(dve_done, E.so_far())
                        E.wait_ge(pe_done, E.at(("S mm", c - 1)))
                        dve.tensor_tensor(m.stmp[:, :, :], f4(PS[:, 3, :]), four(m.bd[:, :]), ALU.mult).then_inc(dve_done, 1)
                        E.counted(("S add", c - 1))
                        E.wait_ge(dve_done, E.so_far())
                        dve.tensor_tensor(m.stmp[:, :, :], m.stmp[:, :, :], m.S[:, q, :, :], ALU.add).then_inc(dve_done, 1)
                        E.counted(("S sum", c - 1))
                        E.wait_ge(dve_done, E.so_far())
                        dve.tensor_tensor(m.S[:, 1 - q, :, :], m.stmp[:, :, :],
                                          m.fac[:, :, c - 1:c].to_broadcast([P, JT, P]), ALU.mult).then_inc(dve_done, 1)
                        E.counted(("S", c - 1))

            for j in range(JT):
                E.wait_ge(dve_done, E.so_far())
                E.wait_ge(pe_done, E.at(("y mean", j)))
                dve.scalar_tensor_tensor(m.yT[:, j, :], PS[:, m.bank["y mean", j], :], -1.0 / 64, m.yT[:, j, :],
                                         ALU.mult, ALU.add).then_inc(dve_done, 1)
                E.counted(("y centred", j))
            for j in range(JT):
                E.wait_ge(dve_done, E.so_far())
                E.wait_ge(act_done, E.at(("mix hi", j)))
                dve.tensor_tensor(m.hL[:, j, :], m.ya[:, j, :], m.hH[:, j, :].bitcast(F32), ALU.subtract).then_inc(dve_done, 1)
                E.counted(("mix lo", j))
            E.wait_ge(dve_done, E.so_far())
            E.wait_ge(pe_done, E.at("y ss"))
            dve.tensor_scalar(m.rn2[:, :], PS[0:16, m.bank["y ss"], :], 1.0 / 64, GN_EPS, ALU.mult, ALU.add).then_inc(dve_done, 1)
            E.counted("y var")
            E.wait_ge(dve_done, E.so_far())
            E.wait_ge(act_done, E.at("y sd"))
            dve.reciprocal(m.rn2[:, :], m.rn2[:, :]).then_inc(dve_done, 1)
            E.counted("y rstd")
            for j in range(JT):
                y = m.yT[:, j, :]
                E.wait_ge(dve_done, E.so_far())
                E.wait_ge(pe_done, E.at(("y rstd spread", j)))
                dve.tensor_tensor(y, PS[:, m.bank["y rstd spread", j], :], y, ALU.mult).then_inc(dve_done, 1)
                E.counted(("y scaled", j))
                E.wait_ge(dve_done, E.so_far())
                dve.tensor_scalar(y, y, col("lnx_w", j), col("lnx_b", j), ALU.mult, ALU.add).then_inc(dve_done, 1)
                E.counted(("y affine", j))
                E.wait_ge(dve_done, E.so_far())
                dve.tensor_tensor(y, y, m.bv[:, j, :], ALU.add).then_inc(dve_done, 1)
                E.counted(("y bonus", j))
                E.wait_ge(dve_done, E.so_far())
                E.wait_ge(pe_done, E.at(("gate", j)))
                dve.tensor_tensor(y, PS[:, j, :], y, ALU.mult).then_inc(dve_done, 1)
                E.counted(("mix", j))
            for j in range(JT):
                E.wait_ge(dve_done, E.so_far())
                E.wait_ge(act_done, E.at(("mix hi", JT + j)))
                dve.tensor_tensor(m.hL[:, JT + j, :], m.yT[:, j, :], m.hH[:, JT + j, :].bitcast(F32), ALU.subtract).then_inc(dve_done, 1)
                E.counted(("mix lo", JT + j))
            split(16)
            split(17)
            dve.wait_ge(gain_loaded, 16)
            for t in range(TT):
                dve.wait_ge(x_loaded[t], 32)
            mix_out_vector(E, m, "n2")


def ffn(nc, m, A, steps, done, sems):
    pe_done, act_done, dve_done, pool_done = (done[n] for n in ("pe", "act", "dve", "pool"))
    PS, m.xn, m.gain, m.otmp = m.PS, m.xn2, m.fgain, m.ftmp
    w_up, w_down = A["w_up"][0], A["w_down"][0]
    w_loaded = sems("w_loaded0"), sems("w_loaded1")
    rows_loaded, gain_loaded = sems("rows_loaded"), sems("gain_loaded")
    UP = FT // 2
    DN = FT // 2
    DR = (DN - 3) // 2
    assert DN == 2 + 2 * DR + 1
    rowsrc = [(0, FROW["pre_ffn"], A["pre_ffn_g"].rearrange("l (a b) -> (l a) b", b=P)),
              (0, FROW["bias"], A["ffn_conv_b"].rearrange("l (a b) -> (l a) b", b=P)),
              (0, FROW["conv0"], A["ffn_conv_w"][0, 0:1, :].rearrange("l (a b) -> (l a) b", b=P)),
              (1, FROW2["conv1"], A["ffn_conv_w"][0, 1:2, :].rearrange("l (a b) -> (l a) b", b=P)),
              (1, FROW2["conv2"], A["ffn_conv_w"][0, 2:3, :].rearrange("l (a b) -> (l a) b", b=P))]

    def up_view(buf, s):
        return buf[:, s, :].rearrange("p (k n) -> p k n", k=KT)

    def dn_view(buf, s):
        return buf[:, s, :].rearrange("p (k n) -> p k n", k=2)

    with nc.Block() as block:

        @block.sync
        def _(sp):
            E = Engine(steps, "sp", sp, done)

            def load_up(s, col):
                src = w_up.rearrange("(k q) n -> q k n", q=P)
                for i in range(2):
                    c = col + DFF if i else col
                    sp.dma_start(up_view(m.raw, s)[:, :, P * i:P * i + P], src[:, :, bass.ds(c, P)]).then_inc(w_loaded[s], 16)

            def load_down(s, row):
                for i in range(2):
                    r = row + P if i else row
                    sp.dma_start(dn_view(m.raw, s)[:, i, :], w_down[bass.ds(r, P), :]).then_inc(w_loaded[s], 16)

            load_up(0, 0)
            load_up(1, P)
            for b, r, src in rowsrc:
                sp.dma_start(m.frow[r:r + src.shape[0], b, :], src).then_inc(rows_loaded, 16)
            sp.dma_start(m.gain[:, :], A["post_ffn_g"].partition_broadcast(P)).then_inc(gain_loaded, 16)
            E.wait_ge(dve_done, E.at(("up lo first", 1)))
            with E.loop("up", UP - 1) as i:
                for u in range(2):
                    col = sp.snap(i * (2 * P) + (2 + u) * P)
                    E.wait_ge(dve_done, E.at(("up lo", u), back=1))
                    load_up(u, col)
            for kk in range(2):
                E.wait_ge(dve_done, E.at(("up lo", kk), at=UP - 2))
                load_down(kk, 2 * P * kk)
            for kk in range(2, 4):
                E.wait_ge(dve_done, E.at(("up lo", kk % 2)))
                load_down(kk % 2, 2 * P * kk)
            E.wait_ge(dve_done, E.at(("dn lo first", 3)))
            with E.loop("down", DR - 1) as i:
                for u in range(2):
                    row = sp.snap(i * (4 * P) + (4 + u) * 2 * P)
                    E.wait_ge(dve_done, E.at(("dn lo", u), back=1))
                    load_down(u, row)
            E.wait_ge(dve_done, E.at(("dn lo", 0)))
            load_down(0, 2 * P * (DN - 1))

        @block.tensor
        def _(pe):
            E = Engine(steps, "pe", pe, done)
            banks = Banks(E)
            pe.wait_ge(rows_loaded, 16 * len(rowsrc))
            for b, n in ((0, FROWS), (1, FROWS2)):
                turn(E, m, banks, ("turn frow", b), b, ("fcol", b), [m.frow[0:n, b, :]], rows=n)
            E.wait_ge(dve_done, E.at(("n3", "xn", TT - 1)))
            for j in range(KT):
                turn(E, m, banks, ("n3", "turn", j), 4 + j % 4, ("n3", "lo", j),
                     [m.xn[:, t, P * j:P * j + P] for t in range(TT)])
            E.wait_ge(dve_done, E.at(("n3", "lo", KT - 1)))
            E.wait_ge(dve_done, E.at(("up lo first", 1)))
            with E.loop("up", UP):
                for u in range(2):
                    E.wait_ge(dve_done, E.at(("up lo", u), back=1))
                    H, L = up_view(m.wh, u), up_view(m.wl, u)
                    for i in range(2):
                        E.wait_ge(dve_done, E.at(("conv", u, i), back=1))
                        c = slice(P * i, P * i + P)
                        project(E, m, (lambda k: H[:, k, c], lambda k: L[:, k, c]),
                                (lambda k: m.hH[:, k, :], lambda k: m.hL[:, k, :]), PS[:, 2 * u + i, :]).then_inc(pe_done, 1)
                        E.counted(("up mm", u, i))

            def down(s, start, stop):
                H, L = dn_view(m.wh, s), dn_view(m.wl, s)
                for k in range(2):
                    for t in range(TT):
                        tt = slice(P * t, P * t + P)
                        for n in range(2):
                            cc = slice(T * n, T * n + T)
                            for i, (g, w) in enumerate(((m.gH, H), (m.gL, H), (m.gH, L))):
                                last = pe.matmul(PS[:, 2 * t + n, :], g[:, s, k, tt], w[:, k, cc],
                                                 start=(start and k == 0 and i == 0), stop=(stop and k == 1 and i == 2),
                                                 skip_group_check=True)
                return last

            E.wait_ge(dve_done, E.at(("conv", 1, 1)))
            for kk in range(2):
                E.wait_ge(dve_done, E.at(("g lo first", kk)))
                E.wait_ge(dve_done, E.at(("up lo", kk)))
                down(kk, kk == 0, False).then_inc(pe_done, 1)
                E.counted(("dn mm first", kk))
            E.wait_ge(dve_done, E.at(("dn lo first", 3)))
            with E.loop("down", DR):
                for u in range(2):
                    E.wait_ge(dve_done, E.at(("dn lo", u), back=1))
                    down(u, False, False).then_inc(pe_done, 1)
                    E.counted(("dn mm", u))
            E.wait_ge(dve_done, E.at("dn lo last"))
            down(0, False, True).then_inc(pe_done, 1)
            E.counted("dn mm last")

        @block.scalar
        def _(act):
            E = Engine(steps, "act", act, done)
            norm_scalar(E, m, "n3", [()] * TT)
            for s in range(2):
                act.wait_ge(w_loaded[s], 32)
                split_hi(E, m, s, ("up hi first", s))
            E.wait_ge(act_done, E.so_far())
            E.wait_ge(dve_done, E.at(("fcol", 0)))
            norm_split_scalar(E, m, "n3", lambda j: m.fcol[:, 0, j:j + 1])
            with E.loop("up", UP) as i:
                for u in range(2):
                    E.wait_ge(act_done, E.so_far())
                    E.wait_ge(dve_done, E.at(("G", u), back=1))
                    E.wait_ge(act_done, E.so_far())
                    E.wait_ge(dve_done, E.at(("conv", u, 0)))
                    act.activation(m.gel[:, u, :], m.cgu[:, u, 0, :], ACT.Gelu_apprx_tanh).then_inc(act_done, 1)
                    E.counted(("gelu", u))
                    act.wait_ge(w_loaded[u], i * 32 + 64)
                    split_hi(E, m, u, ("up hi", u), ("up mm", u, 1))

            def g_hi(s, k, step):
                act.activation(m.gH[:, s, :, :], m.G[:, bass.ds(k, 2), :], ACT.Copy).then_inc(act_done, 1)
                E.counted(step)

            E.wait_ge(act_done, E.so_far())
            E.wait_ge(dve_done, E.at(("G", 1)))
            for kk in range(2):
                g_hi(kk, 2 * kk, ("g hi first", kk))
            for kk in range(2, 4):
                s = kk % 2
                act.wait_ge(w_loaded[s], 32 * (UP + kk // 2 + 1))
                split_hi(E, m, s, ("dn hi first", kk), ("dn mm first", s))
                g_hi(s, 2 * kk, ("g hi first", kk))
            with E.loop("down", DR - 1) as i:
                for u in range(2):
                    k = act.snap(i * 4 + 8 + 2 * u)
                    act.wait_ge(w_loaded[u], i * 32 + 32 * (UP + 3))
                    split_hi(E, m, u, ("dn hi", u), ("dn mm", u))
                    g_hi(u, k, ("g hi", u))
            act.wait_ge(w_loaded[0], 32 * (UP + DN // 2 + 1))
            split_hi(E, m, 0, "dn hi last", ("dn mm", 0))
            g_hi(0, 2 * (DN - 1), "g hi last")
            mix_out_scalar(E, m, "n4", lambda t: ["dn mm last"])

        @block.vector
        def _(dve):
            E = Engine(steps, "dve", dve, done)
            for b, n in ((0, FROWS), (1, FROWS2)):
                E.wait_ge(dve_done, E.so_far())
                E.wait_ge(pe_done, E.at(("turn frow", b)))
                dve.tensor_copy(m.fcol[:, b, 0:n], PS[:, b, 0:n]).then_inc(dve_done, 1)
                E.counted(("fcol", b))
            norm_vector(E, m, "n3")
            for s in range(2):
                split_lo(E, m, s, ("up lo first", s), ("up hi first", s))
            norm_split_vector(E, m, "n3", lambda j: m.fcol[:, 0, j:j + 1])
            with E.loop("up", UP) as i:
                for u in range(2):
                    for h in range(2):
                        j = FT * h + u
                        tap = [m.fcol[:, 0, bass.ds(i * 2 + FROW["conv0"] + j, 1)],
                               m.fcol[:, 1, bass.ds(i * 2 + FROW2["conv1"] + j, 1)],
                               m.fcol[:, 1, bass.ds(i * 2 + FROW2["conv2"] + j, 1)]]
                        bias = m.fcol[:, 0, bass.ds(i * 2 + FROW["bias"] + j, 1)]
                        z, c = PS[:, 2 * u + h, :], m.cgu[:, u, h, :]
                        E.wait_ge(dve_done, E.so_far())
                        E.wait_ge(pe_done, E.at(("up mm", u, h)))
                        dve.tensor_scalar(c, z, tap[2], bias, ALU.mult, ALU.add).then_inc(dve_done, 1)
                        E.counted(("tap2", u, h))
                        E.wait_ge(dve_done, E.so_far())
                        dve.scalar_tensor_tensor(c[:, 1:T], z[:, 0:T - 1], tap[1], c[:, 1:T], ALU.mult, ALU.add).then_inc(dve_done, 1)
                        E.counted(("tap1", u, h))
                        E.wait_ge(dve_done, E.so_far())
                        dve.scalar_tensor_tensor(c[:, 2:T], z[:, 0:T - 2], tap[0], c[:, 2:T], ALU.mult, ALU.add).then_inc(dve_done, 1)
                        E.counted(("conv", u, h))
                    E.wait_ge(dve_done, E.so_far())
                    E.wait_ge(act_done, E.at(("gelu", u)))
                    dve.tensor_tensor(m.G[:, bass.ds(i * 2 + u, 1), :], m.gel[:, u:u + 1, :], m.cgu[:, u, 1:2, :],
                                      ALU.mult).then_inc(dve_done, 1)
                    E.counted(("G", u))
                    split_lo(E, m, u, ("up lo", u), ("up hi", u))

            def g_lo(s, k, step, hi):
                E.wait_ge(dve_done, E.so_far())
                E.wait_ge(act_done, E.at(hi))
                dve.tensor_tensor(m.gL[:, s, :, :], m.G[:, bass.ds(k, 2), :], m.gH[:, s, :, :].bitcast(F32),
                                  ALU.subtract).then_inc(dve_done, 1)
                E.counted(step)

            for kk in range(2):
                g_lo(kk, 2 * kk, ("g lo first", kk), ("g hi first", kk))
            for kk in range(2, 4):
                g_lo(kk % 2, 2 * kk, ("g lo first", kk), ("g hi first", kk))
                split_lo(E, m, kk % 2, ("dn lo first", kk), ("dn hi first", kk))
            with E.loop("down", DR - 1) as i:
                for u in range(2):
                    k = i * 4 + 8 + 2 * u
                    g_lo(u, k, ("g lo", u), ("g hi", u))
                    split_lo(E, m, u, ("dn lo", u), ("dn hi", u))
            g_lo(0, 2 * (DN - 1), "g lo last", "g hi last")
            split_lo(E, m, 0, "dn lo last", "dn hi last")
            dve.wait_ge(gain_loaded, 16)
            mix_out_vector(E, m, "n4")


_WIDTHS = (("gq", 256), ("gk", 256), ("gv", 512), ("ga", 16), ("gz", 512), ("bq", 512), ("bk", 512), ("bv", 512),
           ("iq", 512), ("ik", 64), ("iw", 8), ("bz", 512), ("cq", 512), ("ck", 512), ("cv", 512), ("cz", 512),
           ("gate", 3 * D))
COL, N_IN = numbered(_WIDTHS)
LROW, LROWS = numbered((("norm", KT), ("gla", 1), ("dsa_q", 1), ("dsa_k", 1), ("diff_q", 1), ("diff_k", 1)))
NH = 4
IH = 8
CH = T // 64
RANK = 16
TAU = 16.0
TOP = 128
LAMBDA = tuple(0.8 - 0.6 * 2.718281828459045 ** (-0.3 * l) for l in range(2))
TAKEN, HIDDEN, MASK = -3e38, -1e38, 1e30


def lay_out_layers(nc, m):
    at = [m.arena]

    def take(name, shape, dt=F32, over=None):
        n = 4
        for s in shape[1:]:
            n *= s
        start = at[0] if over is None else over
        t = nc.alloc_sbuf_tensor_at(name, shape, dt, offset=start)
        if over is None:
            at[0] += (n + 31) // 32 * 32
            assert at[0] <= nc.sbuf_usable_end // 32 * 32, (name, at[0])
        return t

    KB = 1024
    mg = at[0]
    m.mg = take("merged", [P, KT, T])
    m.gq = take("gla_q", [P, 2, T], over=mg)
    m.gk = take("gla_k_tokens", [P, TT, 256], over=mg + 4 * KB)
    m.la = take("gla_log_decay", [P, TT, 256], over=mg + 8 * KB)
    m.gt = take("gla_tmp", [P, TT, 256], over=mg + 12 * KB)
    yh = at[0]
    m.yH = take("y_hi", [P, NH, T], F32R)
    m.yL = take("y_lo", [P, NH, T], F32R)
    m.gv = take("gla_v_tokens", [P, TT, BR], over=yh)
    m.St = take("gla_states", [P, 2, CH, P], over=yh + 8 * KB)
    q = at[0]
    m.Q = take("q_feats", [P, NH, T])
    m.K = take("k_feats", [P, NH, T])
    m.V = take("v_toks", [P, TT, BR])
    m.Z = take("z_feats", [P, NH, T])
    m.ikf = take("ik_feats", [P, T], over=q + 8 * KB)
    m.lw = take("lowrank_iw", [RANK + IH, T], over=q + 24 * KB)
    o = at[0]
    m.O = take("branch_out", [P, NH, T])
    m.sq3 = take("squares3", [P, NH, T])
    m.xn3 = take("x_normed3", [P, TT, D], over=o)
    p = at[0]
    m.Px = take("probs", [P, 2, 2, T])
    m.gz = take("gla_z", [P, NH, T], over=p)
    m.relu = take("index_relu", [P, 4, T], over=p)
    pt = at[0]
    m.PT = take("probs_t", [P, 2, T])
    m.wa2 = take("gla_wa2", [RANK, 256], over=pt)
    m.ba = take("gla_ba", [1, 256], over=pt + KB)
    m.lam_in = take("lambda_in", [P, 4, 64], over=pt + 2 * KB)
    m.lamt = take("lambda_tmp", [P, 2, 64], over=pt + 3 * KB)
    m.lrow = take("layer_rows", [LROWS, P], over=pt + 7 * KB // 2)
    m.sc = take("index_scores", [P, P * sum(range(2, TT + 1))])
    m.dg = take("diagonals", [P, 2, P])
    m.later = take("later_in_chunk", [P, P])
    m.lcol = take("layer_cols", [P, 16])
    m.lam = take("lambda", [P, 8])
    m.lamc = take("lambda_init", [P, 2, 2])
    m.lc = take("lambda_const", [P, 2])
    m.iw = take("index_weights", [P, TT, IH])
    m.dec = take("gla_decay", [P, 2, CH])
    m.top8 = take("top8", [P, 8])
    m.st = take("softmax_stats", [P, 2, 8])
    m.rn3 = take("norm_rows3", [16, T])
    m.half = take("first_half", [P, P])
    m.neg = take("mask_values", [P, 64])


def layers(nc, m, A, steps, done, sems, clear):
    pe_done, act_done, dve_done, pool_done = (done[n] for n in ("pe", "act", "dve", "pool"))
    lay_out_layers(nc, m)
    PS, m.xn = m.PS, m.xn3
    w_loaded = sems("w_loaded0"), sems("w_loaded1")
    rows_loaded, small_loaded = sems("rows_loaded"), sems("small_loaded")

    panels = []

    def add(name, pieces, kt=KT, tokens=False):
        panels.append(Panel(name, pieces, kt, tokens))
        return len(panels) - 1

    def full(name, n, tokens=False):
        return [add(name, [("w_in_2", COL[name] + PW * i, PW)], tokens=tokens) for i in range(n)]

    add("ik", [("w_in_2", COL["ik"], 64)] * 2)
    add("ga iw", [("w_in_2", COL["ga"], RANK), ("w_in_2", COL["iw"], IH)])
    iq = full("iq", 2)
    gk, gv, gq, gz = full("gk", 1, True), full("gv", 2, True), full("gq", 1), full("gz", 2)
    cq, ck, cv, cz = full("cq", 2), full("ck", 2), full("cv", 2, True), full("cz", 2)

    def merge(b):
        first = len(panels)
        for r in range(4):
            add("gate", [("w_in_2", COL["gate"] + D * b + PW * r, PW)])
            add("br", [(b, PW * r, PW)], kt=4)
        return first

    mergeA = merge(0)
    bq, bk, bv, bz = full("bq", 2), full("bk", 2), full("bv", 2, True), full("bz", 2)
    mergeC = merge(2)
    mergeB = merge(1)
    outs = [add("out", [("w_out_2", PW * r, PW)], tokens=True) for r in range(4)]
    NP = len(panels)

    def view(buf, p):
        a = panels[p]
        return buf[:, p % 2, 0:a.kt * a.w].rearrange("p (k n) -> p k n", k=a.kt)

    def tiles(p):
        a = panels[p]
        return [min(P, a.w - P * i) for i in range((a.w + P - 1) // P)]

    def bank(p, i):
        return 2 * (p % 2) + i

    tokdst = {}
    for i in range(2):
        tokdst[gv[i]], tokdst[cv[i]], tokdst[bv[i]] = (m.gv, i), (m.V, i), (m.V, i)
    tokdst[gk[0]] = (m.gk, 0)
    featdst = {}
    for i in range(2):
        for ps, dst, scale, fn in ((iq, m.Q, 1.0, ACT.Copy), (gz, m.gz, 1.0, ACT.Silu), (cq, m.Q, 1.0, ACT.Copy),
                                   (ck, m.K, 1.0, ACT.Copy), (cz, m.Z, 1.0, ACT.Silu), (bq, m.Q, 1.0, ACT.Copy),
                                   (bk, m.K, 1.0, ACT.Copy), (bz, m.Z, 1.0, ACT.Silu)):
            for t in range(2):
                featdst[ps[i], t] = (dst[:, 2 * i + t, :], scale, fn)
    for t in range(2):
        featdst[gq[0], t] = (m.gq[:, t, :], 64 ** -0.5, ACT.Copy)
    featdst[0, 0] = (m.ikf[:, :], 1.0, ACT.Copy)
    featdst[1, 0] = (m.lw[:, :], 1.0, ACT.Copy)
    by_dve = set(cq + ck + bq + bk)

    def lname(col):
        return m.lcol[:, LROW[col]:LROW[col] + 1]

    def score(i):
        at = P * sum(range(2, i + 1))
        return m.sc[:, at:at + P * (i + 1)]

    units = [(h, i) for h in range(NH) for i in range(TT)]
    NU = len(units)
    idx = [(i, h) for i in range(1, TT) for h in range(IH)]

    with nc.Block() as block:

        @block.gpsimd
        def _(pool):
            E = Engine(steps, "pool", pool, done)

            def step(ins, name):
                ins.then_inc(pool_done, 1)
                E.counted(name)
                E.wait_ge(pool_done, E.at(name))

            step(pool.memset(m.later[:, :], 0.0), "later 0")
            step(pool.memset(m.later[0:64, 0:64], 1.0), "later 1")
            step(pool.memset(m.later[64:P, 64:P], 1.0), "later 2")
            step(pool.affine_select(out=m.later[:, :], in_=m.later[:, :], compare_op=ALU.is_gt, fill=0.0, base=0,
                                    pattern=[[-1, P]], channel_multiplier=1), "later 3")
            for l in range(2):
                step(pool.memset(m.lamc[:, l, 0:1], LAMBDA[l]), ("lambda 0", l))
                step(pool.memset(m.lamc[:, l, 1:2], 1.0 - LAMBDA[l]), ("lambda 1", l))
            step(pool.memset(m.half[:, :], 0.0), "half 0")
            step(pool.memset(m.half[:, 0:64], 1.0), "half 1")
            step(pool.memset(m.neg[:, :], -MASK), "neg")
    clear()

    with nc.Fori(0, 2) as L:
        one_layer = bass.ds(L, 1)
        with nc.Block() as block:

            @block.sync
            def _(sp):
                E = Engine(steps, "sp", sp, done)
                rows = [(LROW["norm"], KT, 0, A["norm_g_2"][one_layer, :].rearrange("l (a b) -> (l a) b", b=P)),
                        (LROW["gla"], 1, 0, A["gla_norm_g_2"][one_layer, :]),
                        (LROW["dsa_q"], 1, 0, A["dsa_qn_g_2"][one_layer, :]), (LROW["dsa_k"], 1, 0, A["dsa_kn_g_2"][one_layer, :])]
                for c in (0, 64):
                    rows += [(LROW["diff_q"], 1, c, A["diff_qn_g_2"][one_layer, :]),
                             (LROW["diff_k"], 1, c, A["diff_kn_g_2"][one_layer, :])]
                assert len(rows) == 8
                for r, n, c, src in rows:
                    sp.dma_start(m.lrow[r:r + n, c:c + src.shape[1]], src).then_inc(rows_loaded, 16)
                for p in range(NP):
                    if p >= 2:
                        E.wait_ge(dve_done, E.at(("Lw lo", p - 2)))
                    v, at, q = view(m.raw, p), 0, w_loaded[p % 2]
                    pieces, kt = panels[p].pieces, panels[p].kt
                    ks = kt if len(pieces) == 2 else kt // 2
                    for name, c, w in pieces:
                        for k in range(0, kt, ks):
                            if name in (0, 1, 2):
                                s = A["w_br_2"][one_layer, name, P * k:P * (k + ks), c:c + w]
                            else:
                                s = A[name][one_layer, P * k:P * (k + ks), c:c + w]
                            sp.dma_start(v[:, k:k + ks, at:at + w], s.rearrange("l (k q) n -> q (l k) n", q=P)).then_inc(q, 16)
                        at += w
                    if p == 1:
                        for i, n in enumerate(("diff_lq1_2", "diff_lk1_2", "diff_lq2_2", "diff_lk2_2")):
                            sp.dma_start(m.lam_in[:, i, :], A[n][one_layer, :].partition_broadcast(P)).then_inc(small_loaded, 16)
                        sp.dma_start(m.wa2[:, :], A["gla_wa2_2"][one_layer, :, :].rearrange("l a b -> (l a) b")).then_inc(small_loaded, 16)
                        sp.dma_start(m.ba[:, :], A["gla_ba_2"][one_layer, :]).then_inc(small_loaded, 16)

            @block.tensor
            def _(pe):
                E = Engine(steps, "pe", pe, done)
                banks = Banks(E)

                def start(step, b, reader):
                    banks.use(b, reader)
                    m.bank[step] = b
                    return PS[:, b, :]

                def panel(p, only=None):
                    a = panels[p]
                    E.wait_ge(dve_done, E.at(("Lw lo", p)))
                    H, W = view(m.wh, p), view(m.wl, p)
                    for i in range(2 if a.tokens else len(tiles(p))):
                        if only is not None and i != only:
                            continue
                        b = bank(p, i)
                        banks.use(b, ("Levac", p, i))
                        if a.tokens:
                            for t in (2 * i, 2 * i + 1):
                                tt = slice(P * t, P * t + P)
                                last = project(E, m, (lambda k: m.hH[:, k, tt], lambda k: m.hL[:, k, tt]),
                                               (lambda k: H[:, k, :], lambda k: W[:, k, :]),
                                               PS[:, b, PW * (t % 2):PW * (t % 2) + PW])
                        else:
                            n = tiles(p)[i]
                            c = slice(P * i, P * i + n)
                            x = (m.yH, m.yL) if a.name == "br" else (m.hH, m.hL)
                            last = project(E, m, (lambda k: H[:, k, c], lambda k: W[:, k, c]),
                                           (lambda k: x[0][:, k, :], lambda k: x[1][:, k, :]), PS[0:n, b, :], kt=a.kt)
                        last.then_inc(pe_done, 1)
                        E.counted(("Lpanel", p, i))

                def index_dots(i):
                    vis = P * (i + 1)
                    for h in range(IH):
                        n = idx.index((i, h))
                        o = start(("dots", n), 4 + n % 4, ("relu", n))
                        r = slice(64 * (h % 2), 64 * (h % 2) + 64)
                        pe.matmul(o[:, 0:vis], m.Q[r, h // 2, P * i:P * i + P], m.ikf[r, 0:vis], start=True, stop=True).then_inc(pe_done, 1)
                        E.counted(("dots", n))

                def squares(step, reader, tag, ind, b, n0, n1, begin, end):
                    o = start(step, b, reader) if begin else PS[:, b, :]
                    rows = ind.shape[2]
                    for n in range(n0, n1):
                        E.wait_ge(act_done, E.at((tag, n)))
                        last = pe.matmul(o[0:rows, :], ind[:, n, :], m.sq3[:, n % 4, :], start=(begin and n == n0),
                                         stop=(end and n == n1 - 1))
                    last.then_inc(pe_done, 1)
                    E.counted(step)

                def spread(tag, indT, n0, n1, reader, bk=(4, 5, 6)):
                    for n in range(n0, n1):
                        o = start((tag, n), bk[n % len(bk)], (reader, n))
                        pe.matmul(o, indT[:, n, :], m.rn3[0:indT.shape[0], :], start=True, stop=True).then_inc(pe_done, 1)
                        E.counted((tag, n))

                def mask(o, vis, r):
                    return pe.matmul(o[:, vis - 64:vis], m.half[r, :], m.neg[r, :], start=False, stop=True,
                                     skip_group_check=True)

                def diff_logits(u):
                    h, i = units[u]
                    vis = P * (i + 1)
                    for c in range(2):
                        r = slice(64 * c, 64 * c + 64)
                        o = start(("dlogits", u, c), 4 + c, ("dexp", u, c))
                        pe.matmul(o[:, 0:vis], m.Q[r, h, P * i:P * i + P], m.K[r, h, 0:vis], start=True, stop=False,
                                  skip_group_check=True)
                        last = mask(o, vis, r)
                    last.then_inc(pe_done, 1)
                    E.counted(("dlogits", u))

                def dsa_logits(u):
                    h, i = units[u]
                    vis = P * (i + 1)
                    o = start(("slogits", u), 4 + u % 2, ("sread", u))
                    last = pe.matmul(o[:, 0:vis], m.Q[:, h, P * i:P * i + P], m.K[:, h, 0:vis], start=True, stop=(i > 0),
                                     skip_group_check=True)
                    if i == 0:
                        last = mask(o, vis, slice(0, P))
                    last.then_inc(pe_done, 1)
                    E.counted(("slogits", u))

                def turn_probs(u, pf, comps):
                    h, i = units[u]
                    E.wait_ge(dve_done, E.at((pf + "diag", u)))
                    o = start((pf + "pt mm", u), 6, (pf + "pt", u))
                    for k in range(i + 1):
                        for n, c in enumerate(comps):
                            last = pe.matmul(o[:, P * k:P * k + P], m.Px[:, u % 2, c, P * k:P * k + P], m.dg[:, n, :],
                                             start=(n == 0), stop=(n == len(comps) - 1), skip_group_check=True)
                    last.then_inc(pe_done, 1)
                    E.counted((pf + "pt mm", u))

                def values(u, pf):
                    h, i = units[u]
                    E.wait_ge(act_done, E.at((pf + "pt", u)))
                    o = start((pf + "pv", u), 7, (pf + "out", u))
                    for k in range(i + 1):
                        last = pe.matmul(o[:, 0:P], m.V[:, k, P * h:P * h + P], m.PT[:, u % 2, P * k:P * k + P],
                                         start=(k == 0), stop=(k == i))
                    last.then_inc(pe_done, 1)
                    E.counted((pf + "pv", u))

                pe.wait_ge(rows_loaded, 16 * 8)
                turn(E, m, banks, "turn lrow", 0, "lcol", [m.lrow[:, :]], rows=LROWS)
                E.wait_ge(dve_done, E.at(("l1", "xn", TT - 1)))
                for j in range(KT):
                    turn(E, m, banks, ("l1", "turn", j), 4 + j % 4, ("l1", "lo", j),
                         [m.xn[:, t, P * j:P * j + P] for t in range(TT)])
                E.wait_ge(dve_done, E.at(("l1", "lo", KT - 1)))
                panel(0)
                panel(1)
                panel(2)
                E.wait_ge(act_done, E.at(("Levac", 1, 0)))
                turn(E, m, banks, "turn iw", 6, "iw", [m.lw[:, P * t:P * t + P] for t in range(TT)], rows=RANK + IH)
                pe.wait_ge(small_loaded, 16 * 6)
                for g in range(2):
                    o = start(("z", g), 4 + g, ("la", g))
                    for q in range(2):
                        t = 2 * g + q
                        oo = o[:, 256 * q:256 * q + 256]
                        pe.matmul(oo, m.lw[0:RANK, P * t:P * t + P], m.wa2[:, :], start=True, stop=False)
                        last = pe.matmul(oo, m.indwT[0:1, 0, :], m.ba[:, :], start=False, stop=True)
                    last.then_inc(pe_done, 1)
                    E.counted(("z", g))
                panel(3)
                E.wait_ge(act_done, E.at(("Levac", 3, 1)))
                for i in range(1, TT):
                    index_dots(i)
                    panel(3 + i)
                E.wait_ge(dve_done, E.at(("la", 1)))
                for g in range(2):
                    o = start(("later", g), 4 + g, ("kdec", g))
                    last = pe.matmul(o, m.later[:, :], m.la[:, 2 * g:2 * g + 2, :].rearrange("p a b -> p (a b)"),
                                     start=True, stop=True)
                    last.then_inc(pe_done, 1)
                    E.counted(("later", g))
                o = start("total", 6, "decay")
                for f in range(2):
                    for t in range(TT):
                        last = pe.matmul(o[:, CH * f + 2 * t:CH * f + 2 * t + 2], m.la[:, t, P * f:P * f + P],
                                         m.indh[:, 0, 0:2], start=True, stop=True)
                last.then_inc(pe_done, 1)
                E.counted("total")
                panel(7)
                E.wait_ge(dve_done, E.at(("kd", 1)))
                for f in range(2):
                    for g in range(2):
                        o = start(("u", f, g), 4 + 2 * f + g, ("S", f, CH - 2 + g))
                        r = slice(64 * g, 64 * g + 64)
                        for t in range(TT):
                            for e in range(2):
                                h = 2 * f + e
                                last = pe.matmul(o[64 * e:64 * e + 64, P * t:P * t + P], m.gk[r, t, 64 * h:64 * h + 64],
                                                 m.gv[r, t, P * h:P * h + P], start=True, stop=True)
                        last.then_inc(pe_done, 1)
                        E.counted(("u", f, g))
                panel(8)
                panel(9)
                panel(10)
                E.wait_ge(act_done, E.at(("Levac", 7, 1)))
                for h in range(NH):
                    o = start(("o", h), 4 + h, ("gla sq", h))
                    E.wait_ge(dve_done, E.at(("S", h // 2, CH - 1)))
                    r = slice(64 * (h % 2), 64 * (h % 2) + 64)
                    for c in range(CH):
                        cc = slice(64 * c, 64 * c + 64)
                        last = pe.matmul(o[:, cc], m.St[r, h // 2, c, :], m.gq[r, h // 2, cc], start=True, stop=True)
                    last.then_inc(pe_done, 1)
                    E.counted(("o", h))
                panel(11)
                squares("gla ss", "gla sd", "gla sq", m.indw, 7, 0, 4, True, True)
                panel(12)
                E.wait_ge(dve_done, E.at("gla rn"))
                spread("gla spread", m.indwT, 0, 4, "gla y1")
                panel(13)
                squares("diff ss q", "diff sd", "diff sq", m.indh, 7, 0, 4, True, False)
                panel(14)
                squares("diff ss", "diff sd", "diff sq", m.indh, 7, 4, 8, False, True)
                panel(15)
                E.wait_ge(dve_done, E.at("diff rn"))
                spread("diff spread", m.indhT, 0, 4, "diff n")
                panel(16)
                spread("diff spread", m.indhT, 4, 8, "diff n")
                panel(17)

                E.wait_ge(dve_done, E.at(("diff n", 7)))
                E.wait_ge(act_done, E.at(("Levac", cv[1], 1)))
                diff_logits(0)
                for u in range(NU):
                    turn_probs(u, "d", (0, 1))
                    if u + 1 < NU:
                        diff_logits(u + 1)
                    if u == 0:
                        E.wait_ge(dve_done, E.at(("gla lo", NH - 1)))
                    panel(mergeA + u // 2, only=u % 2)
                    values(u, "d")
                panel(26)
                panel(27)
                squares("dout ss", "dout sd", "dout sq", m.indw, 4, 0, 4, True, True)
                panel(28)
                squares("dsa ss q", "dsa sd", "dsa sq", m.indw, 7, 0, 4, True, False)
                E.wait_ge(dve_done, E.at("dout rn"))
                spread("dout spread", m.indwT, 0, 4, "dout y1")
                panel(29)
                panel(30)
                squares("dsa ss", "dsa sd", "dsa sq", m.indw, 7, 4, 8, False, True)
                panel(31)
                E.wait_ge(dve_done, E.at("dsa rn"))
                spread("dsa spread", m.indwT, 0, 4, "dsa n")
                panel(32)
                spread("dsa spread", m.indwT, 4, 8, "dsa n")
                panel(33)

                E.wait_ge(dve_done, E.at(("dsa n", 7)))
                E.wait_ge(act_done, E.at(("Levac", bv[1], 1)))
                dsa_logits(0)
                for u in range(NU):
                    turn_probs(u, "s", (1,))
                    if u + 1 < NU:
                        dsa_logits(u + 1)
                    if u == 0:
                        E.wait_ge(dve_done, E.at(("diff lo", NH - 1)))
                    panel(mergeC + u // 2, only=u % 2)
                    values(u, "s")
                panel(mergeB)
                E.wait_ge(dve_done, E.at(("dsa lo", NH - 1)))
                for p in range(mergeB + 1, mergeB + 8):
                    panel(p)
                E.wait_ge(dve_done, E.at(("merged lo", KT - 1)))
                for p in outs:
                    panel(p)

            @block.scalar
            def _(act):
                E = Engine(steps, "act", act, done)

                def high(p):
                    if p < NP:
                        act.wait_ge(w_loaded[p % 2], 32 * (p // 2 + 1))
                        if p >= 2:
                            E.wait_ge(act_done, E.so_far())
                            E.wait_ge(pe_done, E.at(("Lpanel", p - 2, 0 if len(tiles(p - 2)) == 1 else 1)))
                        n = panels[p].kt * panels[p].w
                        act.activation(m.wh[:, p % 2, 0:n], m.raw[:, p % 2, 0:n], ACT.Copy).then_inc(act_done, 1)
                        E.counted(("Lw hi", p))

                def evac(p, i):
                    if p in by_dve or i >= (2 if panels[p].tokens else len(tiles(p))):
                        return
                    b = bank(p, i)
                    E.wait_ge(act_done, E.so_far())
                    E.wait_ge(pe_done, E.at(("Lpanel", p, i)))
                    if panels[p].tokens:
                        dst, q = tokdst[p]
                        ins = act.activation(dst[:, 2 * i:2 * i + 2, PW * q:PW * q + PW],
                                             PS[:, b, :].rearrange("p (a b) -> p a b", a=2), ACT.Copy)
                    else:
                        dst, scale, fn = featdst[p, i]
                        ins = act.activation(dst, PS[0:tiles(p)[i], b, :], fn, scale=scale)
                    ins.then_inc(act_done, 1)
                    E.counted(("Levac", p, i))

                def relus(i):
                    vis = P * (i + 1)
                    for h in range(IH):
                        n = idx.index((i, h))
                        E.wait_ge(act_done, E.so_far())
                        E.wait_ge(pe_done, E.at(("dots", n)))
                        if n > 3:
                            E.wait_ge(act_done, E.so_far())
                            E.wait_ge(dve_done, E.at(("score", n - 4)))
                        act.activation(m.relu[:, n % 4, 0:vis], PS[:, 4 + n % 4, 0:vis], ACT.Relu).then_inc(act_done, 1)
                        E.counted(("relu", n))

                def square(tag, n, src, *need):
                    E.wait_ge(act_done, E.so_far())
                    for before in need:
                        E.wait_ge(*E.point(before))
                    act.activation(m.sq3[:, n % 4, :], src, ACT.Square).then_inc(act_done, 1)
                    E.counted((tag, n))

                def root(step, need, b, rows, scale):
                    E.wait_ge(act_done, E.so_far())
                    E.wait_ge(pe_done, E.at(need))
                    act.activation(m.rn3[0:rows, :], PS[0:rows, b, :], ACT.Sqrt, bias=m.eps[0:rows, 0:1], scale=scale).then_inc(act_done, 1)
                    E.counted(step)

                def exps(u, pf, comps, scale):
                    h, i = units[u]
                    vis = P * (i + 1)
                    E.wait_ge(act_done, E.so_far())
                    E.wait_ge(dve_done, E.at((pf + "max", u)))
                    if u > 1:
                        E.wait_ge(act_done, E.so_far())
                        E.wait_ge(pe_done, E.at((pf + "pt mm", u - 2)))
                    for c in comps:
                        if pf == "d":
                            src, dst, b = PS[:, 4 + c, 0:vis], m.Px[:, u % 2, c, 0:vis], 4 + c
                        elif i == 0:
                            src, dst = PS[:, 4 + u % 2, 0:vis], m.Px[:, u % 2, 1, 0:vis]
                        else:
                            src, dst = m.Px[:, u % 2, 0, 0:vis], m.Px[:, u % 2, 1, 0:vis]
                        ins = act.activation(dst, src, ACT.Exp, bias=m.st[:, u % 2, 2 + c:3 + c], scale=scale,
                                             accum_out=m.st[:, u % 2, 4 + c:5 + c])
                        ins.then_inc(act_done, 1)
                        E.counted((pf + "exp", u, c))
                        if pf == "s" and i == 0:
                            steps.found["sread", u] = steps.found["sexp", u, 0]

                def probs_t(u, pf):
                    vis = P * (units[u][1] + 1)
                    E.wait_ge(act_done, E.so_far())
                    E.wait_ge(pe_done, E.at((pf + "pt mm", u)))
                    if u > 1:
                        E.wait_ge(act_done, E.so_far())
                        E.wait_ge(pe_done, E.at((pf + "pv", u - 2)))
                    act.activation(m.PT[:, u % 2, 0:vis], PS[:, 6, 0:vis], ACT.Copy).then_inc(act_done, 1)
                    E.counted((pf + "pt", u))

                def head_out(u, pf):
                    h, i = units[u]
                    E.wait_ge(act_done, E.so_far())
                    E.wait_ge(pe_done, E.at((pf + "pv", u)))
                    act.activation(m.O[:, h, P * i:P * i + P], PS[:, 7, 0:P], ACT.Copy).then_inc(act_done, 1)
                    E.counted((pf + "out", u))

                def gate(p, i):
                    E.wait_ge(act_done, E.so_far())
                    E.wait_ge(pe_done, E.at(("Lpanel", p, i)))
                    first = {mergeA: mergeA, mergeB: mergeB, mergeC: mergeC}
                    base = max(b for b in first if b <= p)
                    r = (p - base) // 2
                    if r >= 2:
                        E.wait_ge(act_done, E.so_far())
                        E.wait_ge(dve_done, E.at(("gated", base, 2 * (r - 2) + i)))
                    act.activation(m.sq3[:, 2 * (r % 2) + i, :], PS[:, bank(p, i), :], ACT.Tanh, scale=0.5).then_inc(act_done, 1)
                    E.counted(("Levac", p, i))

                def branch_hi(tag, ready):
                    for h in range(NH):
                        E.wait_ge(act_done, E.so_far())
                        E.wait_ge(dve_done, E.at((ready, h)))
                        act.activation(m.yH[:, h, :], m.O[:, h, :], ACT.Copy).then_inc(act_done, 1)
                        E.counted((tag, h))

                def step(p):
                    evac(p, 0)
                    high(p + 2)
                    evac(p, 1)

                norm_scalar(E, m, "l1", [()] * TT)
                high(0)
                high(1)
                E.wait_ge(act_done, E.so_far())
                E.wait_ge(dve_done, E.at("lcol"))
                norm_split_scalar(E, m, "l1", lambda j: m.lcol[:, j:j + 1])
                step(0)
                step(1)
                step(2)
                E.wait_ge(act_done, E.so_far())
                E.wait_ge(dve_done, E.at("lambda sums"))
                act.activation(m.lam[:, 2:4], m.lam[:, 0:2], ACT.Exp).then_inc(act_done, 1)
                E.counted("lambda exps")
                for g in range(2):
                    E.wait_ge(act_done, E.so_far())
                    E.wait_ge(pe_done, E.at(("z", g)))
                    act.activation(m.gt[:, 2 * g:2 * g + 2, :], PS[:, 4 + g, :].rearrange("p (a b) -> p a b", a=2),
                                   ACT.Abs).then_inc(act_done, 1)
                    E.counted(("z abs", g))
                E.wait_ge(act_done, E.so_far())
                act.activation(m.gt[:, :, :], m.gt[:, :, :], ACT.Exp, scale=-1.0).then_inc(act_done, 1)
                E.counted("z exp")
                E.wait_ge(act_done, E.so_far())
                act.activation(m.gt[:, :, :], m.gt[:, :, :], ACT.Ln, bias=m.eps[:, 1:2], scale=1.0).then_inc(act_done, 1)
                E.counted("z ln")
                step(3)
                for i in range(1, TT):
                    relus(i)
                    step(3 + i)
                for g in range(2):
                    E.wait_ge(act_done, E.so_far())
                    E.wait_ge(pe_done, E.at(("later", g)))
                    E.wait_ge(dve_done, E.at(("la", 1)))
                    act.activation(m.gt[:, 2 * g:2 * g + 2, :], PS[:, 4 + g, :].rearrange("p (a b) -> p a b", a=2),
                                   ACT.Exp, scale=1.0 / TAU).then_inc(act_done, 1)
                    E.counted(("kdec", g))
                E.wait_ge(act_done, E.so_far())
                E.wait_ge(pe_done, E.at("total"))
                act.activation(m.dec[:, :, :], PS[:, 6, 0:2 * CH].rearrange("p (a b) -> p a b", a=2), ACT.Exp,
                               scale=1.0 / TAU).then_inc(act_done, 1)
                E.counted("decay")
                step(7)
                E.wait_ge(act_done, E.so_far())
                E.wait_ge(dve_done, E.at(("score", len(idx) - 1)))
                step(8)
                step(9)
                step(10)
                for h in range(NH):
                    E.wait_ge(act_done, E.so_far())
                    E.wait_ge(pe_done, E.at(("o", h)))
                    act.activation(m.O[:, h, :], PS[:, 4 + h, :], ACT.Copy, scale=lname("gla")).then_inc(act_done, 1)
                    E.counted(("gla out", h))
                    square("gla sq", h, PS[:, 4 + h, :])
                step(11)
                root("gla sd", "gla ss", 7, KT, 1.0 / P)
                step(12)
                for n in range(4):
                    square("diff sq", n, m.Q[:, n, :], "gla ss", ("Levac", cq[n // 2], n % 2))
                step(13)
                for n in range(4):
                    square("diff sq", 4 + n, m.K[:, n, :], "diff ss q", ("Levac", ck[n // 2], n % 2))
                step(14)
                E.wait_ge(act_done, E.so_far())
                E.wait_ge(dve_done, E.at("gla spread done"))
                root("diff sd", "diff ss", 7, 16, 1.0 / 64)
                branch_hi("gla hi", "gla y")
                step(15)
                step(16)
                step(17)

                exps(0, "d", (0, 1), 64 ** -0.5)
                for u in range(NU):
                    p = mergeA + u // 2
                    probs_t(u, "d")
                    if u + 1 < NU:
                        exps(u + 1, "d", (0, 1), 64 ** -0.5)
                    if panels[p].name == "gate":
                        gate(p, u % 2)
                    if u % 2:
                        high(p + 2)
                    head_out(u, "d")
                for h in range(NH):
                    square("dout sq", h, m.O[:, h, :], ("dout", NU - 1), "diff ss", ("gated", mergeA, 7))
                step(26)
                step(27)
                root("dout sd", "dout ss", 4, KT, 1.0 / P)
                for n in range(4):
                    square("dsa sq", n, m.Q[:, n, :], "dout ss", ("Levac", bq[n // 2], n % 2))
                step(28)
                branch_hi("diff hi", "diff y")
                step(29)
                for n in range(4):
                    square("dsa sq", 4 + n, m.K[:, n, :], "dsa ss q", ("Levac", bk[n // 2], n % 2))
                step(30)
                root("dsa sd", "dsa ss", 7, KT, 1.0 / P)
                step(31)
                E.wait_ge(act_done, E.so_far())
                E.wait_ge(dve_done, E.at(("diff y", NH - 1)))
                step(32)
                step(33)

                exps(0, "s", (0,), P ** -0.5)
                for u in range(NU):
                    p = mergeC + u // 2
                    probs_t(u, "s")
                    if u + 1 < NU:
                        exps(u + 1, "s", (0,), P ** -0.5)
                    if panels[p].name == "gate":
                        gate(p, u % 2)
                    if u % 2:
                        high(p + 2)
                    head_out(u, "s")
                E.wait_ge(act_done, E.so_far())
                E.wait_ge(pe_done, E.at(("Lpanel", mergeC + 7, 1)))
                branch_hi("dsa hi", "dsa y")
                for p in range(mergeB, mergeB + 8):
                    if panels[p].name == "gate":
                        gate(p, 0)
                        gate(p, 1)
                    high(p + 2)
                E.wait_ge(act_done, E.so_far())
                E.wait_ge(pe_done, E.at(("Lpanel", mergeB + 6, 1)))
                for j in range(KT):
                    E.wait_ge(act_done, E.so_far())
                    E.wait_ge(dve_done, E.at(("merged", mergeB, j)))
                    act.activation(m.hH[:, j, :], m.mg[:, j, :], ACT.Copy).then_inc(act_done, 1)
                    E.counted(("merged hi", j))
                high(outs[2])
                high(outs[3])

            @block.vector
            def _(dve):
                E = Engine(steps, "dve", dve, done)

                def low(p):
                    if p < NP:
                        n = panels[p].kt * panels[p].w
                        E.wait_ge(dve_done, E.so_far())
                        E.wait_ge(act_done, E.at(("Lw hi", p)))
                        dve.tensor_tensor(m.wl[:, p % 2, 0:n], m.raw[:, p % 2, 0:n],
                                          m.wh[:, p % 2, 0:n].bitcast(F32), ALU.subtract).then_inc(dve_done, 1)
                        E.counted(("Lw lo", p))

                def evac(p, i):
                    if p in by_dve:
                        E.wait_ge(dve_done, E.so_far())
                        E.wait_ge(pe_done, E.at(("Lpanel", p, i)))
                        if p == bq[0] and i == 0:
                            E.wait_ge(dve_done, E.so_far())
                            E.wait_ge(pe_done, E.at(("dlogits", NU - 1)))
                        dve.tensor_copy(featdst[p, i][0], PS[:, bank(p, i), :]).then_inc(dve_done, 1)
                        E.counted(("Levac", p, i))

                def step(p):
                    evac(p, 0)
                    low(p + 2)
                    evac(p, 1)

                def scores(i):
                    vis = P * (i + 1)
                    for h in range(IH):
                        n = idx.index((i, h))
                        r, w, s = m.relu[:, n % 4, 0:vis], m.iw[:, i, h:h + 1], score(i)
                        E.wait_ge(dve_done, E.so_far())
                        E.wait_ge(act_done, E.at(("relu", n)))
                        if h == 0:
                            ins = dve.tensor_scalar(s, r, w, None, ALU.mult)
                        else:
                            ins = dve.scalar_tensor_tensor(s, r, w, s, ALU.mult, ALU.add)
                        ins.then_inc(dve_done, 1)
                        E.counted(("score", n))
                    E.wait_ge(dve_done, E.so_far())
                    dve.memset(score(i)[0:64, vis - 64:vis], HIDDEN).then_inc(dve_done, 1)
                    E.counted(("hidden", i))

                tops = [(i, r) for i in range(1, TT) for r in range(TOP // 8)]

                def top(n0, n1):
                    for i, r in tops[n0:n1]:
                        s = score(i)
                        E.wait_ge(dve_done, E.so_far())
                        dve.max(m.top8[:, :], s).then_inc(dve_done, 1)
                        E.counted(("top", i, r))
                        E.wait_ge(dve_done, E.so_far())
                        dve.match_replace(s, m.top8[:, :], s, TAKEN).then_inc(dve_done, 1)
                        E.counted(("taken", i, r))

                def bias(i):
                    s = score(i)
                    E.wait_ge(dve_done, E.so_far())
                    dve.tensor_scalar(s, s, TAKEN, 1.0, ALU.is_equal, ALU.subtract).then_inc(dve_done, 1)
                    E.counted(("mask", i))
                    E.wait_ge(dve_done, E.so_far())
                    dve.tensor_scalar(s, s, MASK, None, ALU.mult).then_inc(dve_done, 1)
                    E.counted(("bias", i))

                def rows(step, need, n):
                    E.wait_ge(dve_done, E.so_far())
                    E.wait_ge(act_done, E.at(need))
                    dve.reciprocal(m.rn3[0:n, :], m.rn3[0:n, :]).then_inc(dve_done, 1)
                    E.counted(step)

                def normed(tag, spread, n, bk=(4, 5, 6)):
                    x = (m.Q if n < 4 else m.K)[:, n % 4, :]
                    g = lname(("diff_" if tag == "diff n" else "dsa_") + ("q" if n < 4 else "k"))
                    E.wait_ge(dve_done, E.so_far())
                    E.wait_ge(pe_done, E.at((spread, n)))
                    dve.scalar_tensor_tensor(x, PS[:, bk[n % 3], :], g, x, ALU.mult, ALU.mult).then_inc(dve_done, 1)
                    E.counted((tag, n))

                def softmax_max(u, pf):
                    h, i = units[u]
                    vis, st = P * (i + 1), m.st[:, u % 2, :]
                    n, scale = (2, 64 ** -0.5) if pf == "d" else (1, P ** -0.5)
                    E.wait_ge(dve_done, E.so_far())
                    E.wait_ge(pe_done, E.at((pf + "logits", u)))
                    if pf == "d":
                        ins = dve.tensor_reduce(st[:, 0:2], PS[:, 4:6, 0:vis], AX_X, ALU.max)
                    elif i == 0:
                        ins = dve.tensor_reduce(st[:, 0:1], PS[:, 4 + u % 2, 0:vis], AX_X, ALU.max)
                    else:
                        if u > 1:
                            E.wait_ge(dve_done, E.so_far())
                            E.wait_ge(act_done, E.at(("sexp", u - 2, 0)))
                        ins = dve.tensor_tensor_reduce(m.Px[:, u % 2, 0, 0:vis], PS[:, 4 + u % 2, 0:vis], score(i),
                                                       1.0, -3e38, ALU.add, ALU.max, st[:, 0:1])
                    ins.then_inc(dve_done, 1)
                    E.counted((pf + "rowmax", u))
                    if pf == "s" and i > 0:
                        steps.found["sread", u] = steps.found["srowmax", u]
                    E.wait_ge(dve_done, E.so_far())
                    dve.tensor_scalar(st[:, 2:2 + n], st[:, 0:n], -scale, None, ALU.mult).then_inc(dve_done, 1)
                    E.counted((pf + "max", u))

                def softmax_diag(u, pf):
                    st = m.st[:, u % 2, :]
                    n = 2 if pf == "d" else 1
                    E.wait_ge(dve_done, E.so_far())
                    E.wait_ge(act_done, E.at((pf + "exp", u, n - 1)))
                    if u > 0:
                        E.wait_ge(dve_done, E.so_far())
                        E.wait_ge(pe_done, E.at((pf + "pt mm", u - 1)))
                    dve.reciprocal(st[:, 6:6 + n], st[:, 4:4 + n]).then_inc(dve_done, 1)
                    E.counted((pf + "rsum", u))
                    E.wait_ge(dve_done, E.so_far())
                    ins = dve.tensor_scalar(m.dg[:, 0, :], m.ident[:, :], st[:, 6:7], None, ALU.mult)
                    if pf == "d":
                        ins.then_inc(dve_done, 1)
                        E.counted(("diag 0", u))
                        ins = dve.tensor_scalar(m.dg[:, 1, :], m.ident[:, :], st[:, 7:8], m.lam[:, 5:6], ALU.mult, ALU.mult)
                    ins.then_inc(dve_done, 1)
                    E.counted((pf + "diag", u))

                def gated(p, i):
                    base = max(b for b in (mergeA, mergeB, mergeC) if b <= p)
                    r = (p - base) // 2
                    s, g = m.sq3[:, 2 * (r % 2) + i, :], m.mg[:, 2 * r + i, :]
                    E.wait_ge(dve_done, E.so_far())
                    E.wait_ge(pe_done, E.at(("Lpanel", p, i)))
                    E.wait_ge(act_done, E.at(("Levac", p - 1, i)))
                    dve.scalar_tensor_tensor(s, s, 1.0, PS[:, bank(p, i), :], ALU.add, ALU.mult).then_inc(dve_done, 1)
                    E.counted(("Levac", p, i))
                    E.wait_ge(dve_done, E.so_far())
                    if base == mergeA:
                        ins = dve.tensor_scalar(g, s, 0.5, None, ALU.mult)
                    else:
                        ins = dve.scalar_tensor_tensor(g, s, 0.5, g, ALU.mult, ALU.add)
                    ins.then_inc(dve_done, 1)
                    E.counted(("gated", base, 2 * r + i))

                def branch_lo(tag, hi):
                    for h in range(NH):
                        E.wait_ge(dve_done, E.so_far())
                        E.wait_ge(act_done, E.at((hi, h)))
                        dve.tensor_tensor(m.yL[:, h, :], m.O[:, h, :], m.yH[:, h, :].bitcast(F32), ALU.subtract).then_inc(dve_done, 1)
                        E.counted((tag, h))

                E.wait_ge(dve_done, E.so_far())
                E.wait_ge(pe_done, E.at("turn lrow"))
                dve.tensor_copy(m.lcol[:, 0:LROWS], PS[:, 0, 0:LROWS]).then_inc(dve_done, 1)
                E.counted("lcol")
                norm_vector(E, m, "l1")
                low(0)
                low(1)
                norm_split_vector(E, m, "l1", lambda j: m.lcol[:, j:j + 1])
                dve.wait_ge(small_loaded, 16 * 6)
                v = m.lam_in[:, :, :].rearrange("p (a b) n -> p a b n", b=2)
                dve.tensor_tensor(m.lamt[:, :, :], v[:, :, 0, :], v[:, :, 1, :], ALU.mult).then_inc(dve_done, 1)
                E.counted("lambda products")
                E.wait_ge(dve_done, E.so_far())
                dve.tensor_reduce(m.lam[:, 0:2], m.lamt[:, :, :], AX_X, ALU.add).then_inc(dve_done, 1)
                E.counted("lambda sums")
                dve.tensor_copy(m.lc[:, :], m.lamc[:, one_layer, :].rearrange("p a b -> p (a b)")).then_inc(dve_done, 1)
                E.counted("lambda const")
                step(0)
                step(1)
                step(2)
                E.wait_ge(dve_done, E.so_far())
                E.wait_ge(pe_done, E.at("turn iw"))
                dve.tensor_scalar(m.iw[:, :, :],
                                  PS[:, 6, 0:TT * (RANK + IH)].rearrange("p (t n) -> p t n", t=TT)[:, :, RANK:],
                                  64 ** -0.5 * IH ** -0.5, None, ALU.mult).then_inc(dve_done, 1)
                E.counted("iw")
                E.wait_ge(dve_done, E.so_far())
                E.wait_ge(act_done, E.at("lambda exps"))
                dve.tensor_tensor(m.lam[:, 4:5], m.lam[:, 3:4], m.lam[:, 2:3], ALU.subtract).then_inc(dve_done, 1)
                E.counted("lambda diff")
                E.wait_ge(dve_done, E.so_far())
                dve.tensor_tensor(m.lam[:, 5:6], m.lam[:, 4:5], m.lc[:, 0:1], ALU.subtract).then_inc(dve_done, 1)
                E.counted("lambda")
                E.wait_ge(dve_done, E.so_far())
                E.wait_ge(act_done, E.at("z ln"))
                for g in range(2):
                    dve.scalar_tensor_tensor(m.la[:, 2 * g:2 * g + 2, :], PS[:, 4 + g, :].rearrange("p (a b) -> p a b", a=2),
                                             0.0, m.gt[:, 2 * g:2 * g + 2, :], ALU.min, ALU.subtract).then_inc(dve_done, 1)
                    E.counted(("la", g))
                step(3)
                for i in range(1, TT):
                    scores(i)
                    step(3 + i)
                E.wait_ge(dve_done, E.so_far())
                E.wait_ge(act_done, E.at(("Levac", gk[0], 1)))
                for g in range(2):
                    s = m.gk[:, 2 * g:2 * g + 2, :]
                    E.wait_ge(dve_done, E.so_far())
                    E.wait_ge(act_done, E.at(("kdec", g)))
                    dve.tensor_tensor(s, s, m.gt[:, 2 * g:2 * g + 2, :], ALU.mult).then_inc(dve_done, 1)
                    E.counted(("kd", g))
                step(7)
                E.wait_ge(dve_done, E.so_far())
                E.wait_ge(act_done, E.at("decay"))
                for c in range(CH):
                    for f in range(2):
                        u = PS[:, 4 + 2 * f + c % 2, P * (c // 2):P * (c // 2) + P]
                        E.wait_ge(dve_done, E.so_far())
                        E.wait_ge(pe_done, E.at(("u", f, c % 2)))
                        if c == 0:
                            ins = dve.tensor_copy(m.St[:, f, 0, :], u)
                        else:
                            ins = dve.scalar_tensor_tensor(m.St[:, f, c, :], m.St[:, f, c - 1, :], m.dec[:, f, c:c + 1], u,
                                                           ALU.mult, ALU.add)
                        ins.then_inc(dve_done, 1)
                        E.counted(("S", f, c))
                step(8)
                top(0, 4)
                step(9)
                top(4, 8)
                step(10)
                top(8, 10)
                step(11)
                rows("gla rn", "gla sd", KT)
                step(12)
                for h in range(NH):
                    o = m.O[:, h, :]
                    E.wait_ge(dve_done, E.so_far())
                    E.wait_ge(pe_done, E.at(("gla spread", h)))
                    dve.tensor_tensor(o, PS[:, (4, 5, 6)[h % 3], :], o, ALU.mult).then_inc(dve_done, 1)
                    E.counted(("gla y1", h))
                    if h == NH - 1:
                        steps.found["gla spread done"] = steps.found["gla y1", h]
                    E.wait_ge(dve_done, E.so_far())
                    dve.tensor_tensor(o, o, m.gz[:, h, :], ALU.mult).then_inc(dve_done, 1)
                    E.counted(("gla y", h))
                step(13)
                top(10, 13)
                step(14)
                rows("diff rn", "diff sd", 16)
                branch_lo("gla lo", "gla hi")
                step(15)
                for n in range(4):
                    normed("diff n", "diff spread", n)
                step(16)
                for n in range(4, 8):
                    normed("diff n", "diff spread", n)
                step(17)
                softmax_max(0, "d")
                softmax_diag(0, "d")
                for u in range(NU):
                    p = mergeA + u // 2
                    if u + 1 < NU:
                        softmax_max(u + 1, "d")
                        softmax_diag(u + 1, "d")
                    if panels[p].name == "br":
                        gated(p, u % 2)
                    if u % 2:
                        low(p + 2)
                step(26)
                top(13, 17)
                step(27)
                rows("dout rn", "dout sd", KT)
                step(28)
                for h in range(NH):
                    o = m.O[:, h, :]
                    E.wait_ge(dve_done, E.so_far())
                    E.wait_ge(pe_done, E.at(("dout spread", h)))
                    dve.scalar_tensor_tensor(o, PS[:, (4, 5, 6)[h % 3], :], m.lc[:, 1:2], o, ALU.mult, ALU.mult).then_inc(dve_done, 1)
                    E.counted(("dout y1", h))
                    E.wait_ge(dve_done, E.so_far())
                    dve.tensor_tensor(o, o, m.Z[:, h, :], ALU.mult).then_inc(dve_done, 1)
                    E.counted(("diff y", h))
                branch_lo("diff lo", "diff hi")
                step(29)
                top(17, 25)
                step(30)
                rows("dsa rn", "dsa sd", KT)
                top(25, 29)
                step(31)
                for n in range(4):
                    normed("dsa n", "dsa spread", n)
                top(29, 34)
                step(32)
                for n in range(4, 8):
                    normed("dsa n", "dsa spread", n)
                top(34, 42)
                step(33)
                top(42, 48)
                for i in range(1, TT):
                    bias(i)
                softmax_max(0, "s")
                softmax_diag(0, "s")
                for u in range(NU):
                    p = mergeC + u // 2
                    if u + 1 < NU:
                        softmax_max(u + 1, "s")
                        softmax_diag(u + 1, "s")
                    if panels[p].name == "br":
                        gated(p, u % 2)
                    if u % 2:
                        low(p + 2)
                for h in range(NH):
                    o = m.O[:, h, :]
                    E.wait_ge(dve_done, E.so_far())
                    E.wait_ge(act_done, E.at(("sout", 4 * h + 3)))
                    dve.tensor_tensor(o, o, m.Z[:, h, :], ALU.mult).then_inc(dve_done, 1)
                    E.counted(("dsa y", h))
                branch_lo("dsa lo", "dsa hi")
                for p in range(mergeB, mergeB + 8):
                    if panels[p].name == "br":
                        gated(p, 0)
                        gated(p, 1)
                        j = p - mergeB - 1
                        steps.found["merged", mergeB, j] = steps.found["gated", mergeB, j]
                        steps.found["merged", mergeB, j + 1] = steps.found["gated", mergeB, j + 1]
                    low(p + 2)
                for j in range(KT):
                    E.wait_ge(dve_done, E.so_far())
                    E.wait_ge(act_done, E.at(("merged hi", j)))
                    dve.tensor_tensor(m.hL[:, j, :], m.mg[:, j, :], m.hH[:, j, :].bitcast(F32), ALU.subtract).then_inc(dve_done, 1)
                    E.counted(("merged lo", j))
                for n, p in enumerate(outs):
                    for i in range(2):
                        E.wait_ge(dve_done, E.so_far())
                        E.wait_ge(pe_done, E.at(("Lpanel", p, i)))
                        x = m.x[:, 2 * i:2 * i + 2, PW * n:PW * n + PW]
                        dve.tensor_tensor(x, PS[:, bank(p, i), :].rearrange("p (a b) -> p a b", a=2), x, ALU.add).then_inc(dve_done, 1)
                        E.counted(("Levac", p, i))
                    low(outs[0] + n + 2 if n < 2 else NP)
        clear()


def program(nc, A, out, steps):
    m = lay_out(nc, A)
    m.PS = nc.alloc_psum_tensor("psum", [P, 8, T], F32)
    m.bank = {}
    made = {}

    def sems(name):
        if name not in made:
            made[name] = nc.alloc_semaphore(name)
        return made[name]

    done = {n: sems(f"{n}_done") for n in ("pe", "act", "dve", "pool")}

    def clear():
        with nc.Block() as block:
            @block.sync
            def _(sp):
                for s in made.values():
                    sp.sem_clear(s)

    mixer(nc, m, A, steps, done, sems)
    clear()
    ffn(nc, m, A, steps, done, sems)
    clear()
    layers(nc, m, A, steps, done, sems, clear)
    stored = sems("stored")
    with nc.Block() as block:
        @block.sync
        def _(sp):
            for t in range(TT):
                sp.dma_start(out[0, P * t:P * t + P, :], m.x[:, t, :]).then_inc(stored, 16)
            sp.wait_ge(stored, 16 * TT)


_INS = ["x", "pre_mix_g", "w_in", "conv_a_w", "shift_mu", "w0", "w2", "a0", "a2", "g2", "k_k", "k_a", "r_k", "lnx_w",
        "lnx_b", "w_out", "post_mix_g", "pre_ffn_g", "w_up", "ffn_conv_w", "ffn_conv_b", "w_down", "post_ffn_g",
        "norm_g_2", "w_in_2", "gla_wa2_2", "gla_ba_2", "gla_norm_g_2", "dsa_qn_g_2", "dsa_kn_g_2", "diff_qn_g_2",
        "diff_kn_g_2", "diff_lq1_2", "diff_lk1_2", "diff_lq2_2", "diff_lk2_2", "w_br_2", "w_out_2"]


def kernel(**inputs):
    import numpy as _np
    import concourse.bacc as _bacc
    from concourse import mybir as _mybir
    from concourse.bass_utils import run_bass_kernel_spmd as _run

    def write(known):
        nc = _bacc.Bacc("TRN2", target_bir_lowering=False, num_devices=1)
        arrays, A = {}, {}
        for name in _INS:
            a = _np.ascontiguousarray(inputs[name])
            arrays[f"in_{name}_dram"] = a
            A[name] = nc.dram_tensor(f"in_{name}_dram", a.shape, _mybir.dt.from_np(a.dtype), kind="ExternalInput").ap()
        out = nc.dram_tensor("out_0_dram", (1, T, D), _mybir.dt.float32, kind="ExternalOutput").ap()
        steps = Steps(known)
        program(nc, A, out, steps)
        return nc, arrays, steps

    _, _, known = write(None)
    nc, arrays, _ = write(known)
    r = _run(nc, [arrays], core_ids=[0])
    return r.results[0]["out_0_dram"]
```

```python
from contextlib import contextmanager

import concourse.bass as bass
from concourse import mybir

F32 = mybir.dt.float32
F32R = mybir.dt.float32r
ALU = mybir.AluOpType
ACT = mybir.ActivationFunctionType
AX_X = mybir.AxisListType.X

P = 128
T = 512
D = 1024
TT = T // P
KT = D // P
RMS_EPS = 1e-6
BASE = 16544
PW = 256
PANEL = KT * PW

BR = 512
JT = BR // P
GN_EPS = 64 * 1e-5
DECAY = 0.6065306597126334
RN = 48
LEVELS = 7
DFF = 2816
FT = DFF // P


def numbered(sizes):
    at, out = 0, {}
    for name, n in sizes:
        out[name] = at
        at += n
    return out, at


ROW, ROWS = numbered((("pre_mix", 8), ("mu_r", 4), ("mu_k", 4), ("mu_v", 4), ("mu_wa", 1), ("mu_g", 2), ("w0", 4),
                      ("a0", 4), ("k_k", 4), ("k_a", 4), ("lnx_w", 4), ("lnx_b", 4), ("r_k", 4), ("conv", 12)))
FROW, FROWS = numbered((("pre_ffn", 8), ("bias", 2 * FT), ("conv0", 2 * FT)))
FROW2, FROWS2 = numbered((("conv1", 2 * FT), ("conv2", 2 * FT)))


class Map:
    pass


class Panel:

    def __init__(self, name, pieces, kt, tokens):
        self.name = name
        self.pieces = pieces
        self.kt = kt
        self.tokens = tokens
        self.w = sum(c[2] for c in pieces)


class Steps:

    def __init__(self, known=None):
        self.known = known
        self.found = {}
        self.stride = {}
        self.rounds = {}


class Engine:

    def __init__(self, steps, name, eng, sems):
        self.steps, self.name, self.eng, self.sems = steps, name, eng, sems
        self.done = sems.get(name)
        self.n, self.open, self.covered = 0, [], {}

    def counted(self, step):
        self.n += 1
        assert step not in self.steps.found, step
        self.steps.found[step] = (self.name, self.n, tuple(i for i, _ in self.open))

    def at(self, step, back=0, at=None):
        known = self.steps.known
        if known is None:
            return 0
        owner, value, loops = known.found[step]
        mine, low = dict(self.open), value
        for n, loop in enumerate(loops):
            stride = known.stride[owner, loop]
            if loop in mine:
                gone = back * stride if n == len(loops) - 1 else 0
                value, low = mine[loop] * stride + (value - gone), low - gone
            else:
                value = value + (known.rounds[owner, loop] - 1 if at is None else at) * stride
        assert low >= 1, step
        return value

    def point(self, step, back=0, at=None):
        known = self.steps.known
        return self.sems[known.found[step][0] if known else "pe"], self.at(step, back, at)

    def so_far(self):
        value = self.n if self.steps.known else 0
        for loop, i in self.open:
            if self.steps.known and self.n:
                value = i * self.steps.known.stride[self.name, loop] + value
        return value

    def wait_ge(self, sem, value):
        if isinstance(value, int):
            if self.covered.get(sem.name, 0) >= value:
                return
            if not self.open:
                self.covered[sem.name] = value
        self.eng.wait_ge(sem, value)

    @contextmanager
    def loop(self, name, rounds):
        start = self.n
        self.steps.rounds[self.name, name] = rounds
        with self.eng.Fori(0, rounds) as i:
            self.open.append((name, i))
            yield i
            self.open.pop()
        self.steps.stride[self.name, name] = self.n - start
        self.n = start + rounds * (self.n - start)


def lay_out(nc, A):
    m = Map()

    def place(name, shape, dt, at):
        return nc.alloc_sbuf_tensor_at(name, shape, dt, offset=at)

    def area(start):
        at = [start]

        def take(name, shape, dt=F32):
            n = 4
            for s in shape[1:]:
                n *= s
            t = place(name, shape, dt, at[0])
            at[0] += (n + 31) // 32 * 32
            assert at[0] <= nc.sbuf_usable_end // 32 * 32, (name, at[0])
            return t
        return take, at

    take, at = area(BASE)
    m.raw = take("w_raw", [P, 2, PANEL])
    m.wh = take("w_hi", [P, 2, PANEL], F32R)
    m.wl = take("w_lo", [P, 2, PANEL], F32R)
    m.hT_at = at[0]
    m.hH = take("h_hi", [P, KT, T], F32R)
    m.hL = take("h_lo", [P, KT, T], F32R)
    m.x_at = at[0]
    m.x = take("x_tokens", [P, TT, D])
    m.ident = take("ident", [P, P])
    m.bd = take("head_blocks", [P, P])
    m.indh = take("half_rows", [P, KT, RN])
    m.indw = take("tile_rows", [P, KT, RN])
    m.indhT = take("half_rows_t", [RN, KT, P], F32R)
    m.indwT = take("tile_rows_t", [RN, KT, P], F32R)
    m.rnS = take("norm_rows_split", [RN, T], F32R)
    m.eps = take("eps", [P, 2])
    m.stat = take("row_stats", [P, 4, TT])
    m.arena = at[0]

    take, at = area(m.arena)
    m.smask = take("score_masks", [P, 4, P])
    m.lmask = take("level_masks", [P, LEVELS, P])
    m.prow = take("param_rows", [P, P])
    m.pcol = take("param_cols", [P, P])
    m.omm = take("one_minus", [P, 24])
    m.APR_at = at[0]
    m.APR = take("a_r", [P, 2, JT, T])
    m.BK = take("b_k", [P, 2, JT, T])
    m.Vt = take("v_tokens", [P, TT, BR])
    m.bv = take("bonus_v", [P, JT, T])
    m.yT_at = at[0]
    m.yT = take("y_feats", [P, JT, T])
    m.ya = take("conv_out", [P, JT, T])
    m.gd = take("gate_lr", [P, T])
    m.gd2 = take("gate_lr2", [32, T])
    m.fac = take("state_factor", [P, JT, TT])
    m.emid = take("decay_to_mid", [P, JT, TT])
    shared = at[0]
    m.xn1 = place("x_normed", [P, TT, D], F32, m.APR_at)
    m.vq = place("v_feats", [P, JT, T], F32, m.yT_at)
    take, at = area(shared)
    m.zs = take("shifted", [P, 2, T + 8])
    m.Gx = take("decay_sum", [P, TT, P + 1])
    m.Gc = take("decay_sum_mid", [P, TT, P + 1])
    m.Ep = take("decay_pos", [P, TT, P + 1])
    m.Em = take("decay_neg", [P, TT, P + 1])
    m.cu = take("conv_in", [P, 2, T])
    m.cv = take("conv_sum", [P, T])
    m.rn = take("norm_rows", [16, T])
    m.onesP = take("ones_row", [P, P])
    take, at = area(m.x_at)
    m.sq = take("squares", [P, JT, T])
    m.w2a2 = take("w2_a2", [P, BR])
    m.wad = take("decay_iclr_lr", [P, T])
    m.gB = take("conv_gate", [P, 2, T])
    assert at[0] <= m.x_at + 4 * TT * D
    take, at = area(shared)
    m.Xi = take("inverse", [P, 2, 4, P])
    m.Ti = take("inverse_step", [P, 2, 4, P])
    m.rhs = take("chunk_rhs", [P, BR])
    m.sa = take("chunk_sa", [P, BR])
    m.S = take("state", [P, 2, JT, P])
    m.stmp = take("state_tmp", [P, JT, P])
    take, at = area(m.x_at)
    m.XTi = take("inverse_t", [P, 2, 2, 4, P])
    m.BKT = take("b_k_tokens", [P, 2, JT, P])
    assert at[0] <= m.x_at + 4 * TT * D
    m.SC = place("scores", [P, 2, 2 * JT, 4, P], F32, m.hT_at)
    take, at = area(shared)
    m.g2a = take("g2_a", [P, BR])
    m.g2b = take("g2_b", [32, BR])
    m.ysq = take("y_squares", [P, JT, T])
    m.rn2 = take("y_norm_rows", [16, T])
    take, at = area(m.APR_at)
    m.gain = take("row_gain", [P, D])
    m.otmp = take("out_tmp", [P, 2, D])

    take, at = area(m.arena)
    m.G_at = at[0]
    m.G = take("ffn_hidden", [P, FT, T])
    m.xn2 = place("x_normed_f", [P, TT, D], F32, m.G_at)
    m.gH = take("ffn_hi", [P, 2, 2, T], F32R)
    m.gL = take("ffn_lo", [P, 2, 2, T], F32R)
    m.cgu = take("ffn_conv", [P, 2, 2, T])
    m.gel = take("ffn_gelu", [P, 2, T])
    m.frow = take("ffn_rows", [P, 2, P])
    m.fcol = take("ffn_cols", [P, 2, P])
    m.fgain = take("ffn_gain", [P, D])
    m.ftmp = take("ffn_tmp", [P, 2, D])
    return m


def constants(pool, m):
    q = pool.eng

    def step(ins, name):
        ins.then_inc(pool.done, 1)
        pool.counted(name)
        pool.wait_ge(pool.sems["pool"], pool.at(name))

    step(q.memset(m.prow[:, :], 0.0), "prow zero")
    step(q.memset(m.ident[:, :], 0.0), "ident 0")
    step(q.affine_select(out=m.ident[:, :], in_=m.ident[:, :], compare_op=ALU.not_equal, fill=1.0, base=0,
                         pattern=[[-1, P]], channel_multiplier=1), "ident")
    step(q.memset(m.eps[:, 0:1], RMS_EPS), "table 1")
    step(q.memset(m.eps[:, 1:2], 1.0), "eps")
    step(q.memset(m.bd[:, :], 0.0), "table 2")
    step(q.memset(m.onesP[:, :], 1.0), "table 3")
    step(q.memset(m.indh[:, :, :], 0.0), "table 4")
    step(q.memset(m.zs[:, :, :], 0.0), "table 6")
    step(q.memset(m.Gx[:, :, :], 0.0), "table 7")
    step(q.memset(m.indw[:, :, :], 0.0), "zeros")
    step(q.memset(m.bd[0:64, 0:64], 1.0), "table 8")
    step(q.memset(m.bd[64:P, 64:P], 1.0), "table 9")
    hf = m.indh[:, :, :].rearrange("p a b -> p (a b)")
    wf = m.indw[:, :, :].rearrange("p a b -> p (a b)")
    for r in (0, 32):
        step(q.memset(hf[0:64, r:KT * RN:RN + 2], 1.0), ("table 10", r))
        step(q.memset(hf[64:P, r + 1:KT * RN:RN + 2], 1.0), ("table 11", r))
        step(q.memset(wf[:, r:KT * RN:RN + 1], 1.0), ("table 12", r))
    step(q.memset(m.smask[:, :, :], 1.0), "table 14")
    step(q.memset(m.lmask[:, :, :], 0.0), "ones")
    for i in range(4):
        step(q.affine_select(out=m.smask[:, i, :], in_=m.smask[:, i, :], compare_op=ALU.is_ge if i % 2 else ALU.is_gt,
                        fill=0.0, base=0, pattern=[[1, P]], channel_multiplier=-1), ("table 15", i))
    lower = []
    for l in range(LEVELS):
        b = 1 << l
        v = m.lmask[:, l, :].rearrange("p (n h i) -> p n h i", h=2, i=b)[:, :, 0, :]
        lower.append((v, b))
        step(q.memset(v, 1.0), ("table 16", b))
    for v, b in lower:
        step(q.affine_select(out=v, in_=v, compare_op=ALU.is_ge, fill=0.0, base=-b,
                               pattern=[[-2 * b, P // (2 * b)], [0, b]], channel_multiplier=1), ("table 17", b))
    for v, b in lower:
        step(q.affine_select(out=v, in_=v, compare_op=ALU.is_ge, fill=0.0, base=2 * b - 1,
                               pattern=[[2 * b, P // (2 * b)], [0, b]], channel_multiplier=-1), ("table 18", b))
    step(q.memset(m.onesP[:, :], 1.0), "constants")


def norm_scalar(act, m, pf):
    act.eng.activation(m.stat[:, 3, 0:1], m.eps[:, 0:1], ACT.Sqrt).then_inc(act.done, 1)
    act.counted((pf, "table"))
    for t in (0, 1):
        act.eng.activation(m.xn[:, t, :], m.x[:, t, :], ACT.Square, accum_out=m.stat[:, 0, t:t + 1]).then_inc(act.done, 1)
        act.counted((pf, "ss", t))
    act.wait_ge(act.done, act.so_far())
    act.wait_ge(act.sems["dve"], act.at((pf, "ss", 3)))
    act.eng.activation(m.stat[:, 1, :], m.stat[:, 0, :], ACT.Sqrt, bias=m.eps[:, 0:1],
                       scale=1.0 / D).then_inc(act.done, 1)
    act.counted((pf, "sd"))
    act.wait_ge(act.sems["dve"], act.at((pf, "rstd")))
    for t in (2, 3):
        act.eng.activation(m.xn[:, t, :], m.x[:, t, :], ACT.Copy, scale=m.stat[:, 2, t:t + 1]).then_inc(act.done, 1)
        act.counted((pf, "xn", t))


def norm_vector(dve, m, pf):
    for t in (2, 3):
        dve.eng.tensor_tensor_reduce(m.xn[:, t, :], m.x[:, t, :], m.x[:, t, :], 1.0, 0.0, ALU.mult, ALU.add,
                                     m.stat[:, 0, t:t + 1]).then_inc(dve.done, 1)
        dve.counted((pf, "ss", t))
    scale_rows(dve, m, pf, (0, 1))


def scale_rows(dve, m, pf, tiles):
    dve.wait_ge(dve.done, dve.so_far())
    dve.wait_ge(dve.sems["act"], dve.at((pf, "sd")))
    dve.eng.reciprocal(m.stat[:, 2, :], m.stat[:, 1, :]).then_inc(dve.done, 1)
    dve.counted((pf, "rstd"))
    dve.wait_ge(dve.done, dve.so_far())
    for t in tiles:
        dve.eng.tensor_scalar(m.xn[:, t, :], m.x[:, t, :], m.stat[:, 2, t:t + 1], None, ALU.mult).then_inc(dve.done, 1)
        dve.counted((pf, "xn", t))


def norm_split_scalar(act, m, pf, gcol):
    for j in range(KT):
        act.wait_ge(act.done, act.so_far())
        act.wait_ge(act.sems["pe"], act.at((pf, "turn", j)))
        act.eng.activation(m.hH[:, j, :], m.PS[:, 4 + j % 4, :], ACT.Copy, scale=gcol(j)).then_inc(act.done, 1)
        act.counted((pf, "hi", j))


def norm_split_vector(dve, m, pf, gcol):
    for j in range(KT):
        dve.wait_ge(dve.done, dve.so_far())
        dve.wait_ge(dve.sems["act"], dve.at((pf, "hi", j)))
        dve.eng.scalar_tensor_tensor(m.hL[:, j, :], m.PS[:, 4 + j % 4, :], gcol(j), m.hH[:, j, :].bitcast(F32),
                                     ALU.mult, ALU.subtract).then_inc(dve.done, 1)
        dve.counted((pf, "lo", j))


def split_hi(act, m, s, step, *need):
    act.wait_ge(act.done, act.so_far())
    for before in need:
        act.wait_ge(*act.point(before))
    act.eng.activation(m.wh[:, s, :], m.raw[:, s, :], ACT.Copy).then_inc(act.done, 1)
    act.counted(step)


def split_lo(dve, m, s, step, hi):
    dve.wait_ge(dve.done, dve.so_far())
    dve.wait_ge(dve.sems["act"], dve.at(hi))
    dve.eng.tensor_tensor(m.wl[:, s, :], m.raw[:, s, :], m.wh[:, s, :].bitcast(F32), ALU.subtract).then_inc(dve.done, 1)
    dve.counted(step)


def mix_out_scalar(act, m, pf, need):
    act.wait_ge(act.done, act.so_far())
    act.eng.activation(m.stat[:, 3, 0:1], m.eps[:, 0:1], ACT.Sqrt).then_inc(act.done, 1)
    act.counted((pf, "table"))
    for t in range(TT):
        act.wait_ge(act.done, act.so_far())
        for before in need(t):
            act.wait_ge(*act.point(before))
        act.eng.activation(m.otmp[:, t % 2, :], m.PS[:, 2 * t:2 * t + 2, :].rearrange("p a b -> p (a b)"),
                           ACT.Square, accum_out=m.stat[:, 0, t:t + 1]).then_inc(act.done, 1)
        act.counted((pf, "ss", t))
    act.wait_ge(act.done, act.so_far())
    act.eng.activation(m.stat[:, 1, :], m.stat[:, 0, :], ACT.Sqrt, bias=m.eps[:, 0:1],
                       scale=1.0 / D).then_inc(act.done, 1)
    act.counted((pf, "sd"))


def mix_out_vector(dve, m, pf):
    dve.wait_ge(dve.done, dve.so_far())
    dve.wait_ge(dve.sems["act"], dve.at((pf, "sd")))
    dve.eng.reciprocal(m.stat[:, 2, :], m.stat[:, 1, :]).then_inc(dve.done, 1)
    dve.counted((pf, "rstd"))
    dve.wait_ge(dve.done, dve.so_far())
    for t in range(TT):
        o = m.PS[:, 2 * t:2 * t + 2, :].rearrange("p a b -> p (a b)")
        dst = m.otmp[:, t, :] if t < 2 else o
        dve.eng.scalar_tensor_tensor(dst, o, m.stat[:, 2, t:t + 1], m.gain[:, :], ALU.mult,
                                     ALU.mult).then_inc(dve.done, 1)
        dve.counted((pf, "out", t))
        if t >= 2:
            dve.wait_ge(dve.done, dve.so_far())
            dve.eng.tensor_tensor(m.x[:, t, :], m.x[:, t, :], o, ALU.add).then_inc(dve.done, 1)
            dve.counted((pf, "x", t))


def mix_out_pool(pool, m, pf):
    for t in (0, 1):
        pool.wait_ge(pool.sems["dve"], pool.at((pf, "out", t)))
        pool.eng.tensor_tensor(m.x[:, t, :], m.x[:, t, :], m.otmp[:, t, :], ALU.add).then_inc(pool.done, 1)
        pool.counted((pf, "x", t))


def split_rows(dve, m, rows, step):
    n = rows.shape[0]
    dve.wait_ge(dve.done, dve.so_far())
    dve.eng.tensor_copy(m.rnS[0:n, :], rows).then_inc(dve.done, 1)
    dve.counted((step, "hi"))
    dve.wait_ge(dve.done, dve.so_far())
    dve.eng.tensor_tensor(m.rnS[32:32 + n, :], rows, m.rnS[0:n, :].bitcast(F32), ALU.subtract).then_inc(dve.done, 1)
    dve.counted(step)


def halves(blocks, l, h):
    return blocks.rearrange("p a (n h i) -> p a n h i", h=2, i=1 << l)[:, :, :, h, :]


class Banks:

    def __init__(self, pe):
        self.pe, self.reader = pe, {}

    def use(self, bank, reader):
        if bank in self.reader:
            self.pe.wait_ge(*self.pe.point(self.reader[bank]))
        self.reader[bank] = reader


def turn(pe, m, banks, step, bank, reader, blocks, rows=P):
    banks.use(bank, reader)
    m.bank[step] = bank
    for i, b in enumerate(blocks):
        n = b.shape[1]
        last = pe.eng.transpose(m.PS[0:n, bank, rows * i:rows * i + rows], b, m.ident[0:rows, 0:rows])
    last.then_inc(pe.done, 1)
    pe.counted(step)


def project(pe, m, w, x, out, kt=KT, ks=None, opens=True):
    for k in range(kt) if ks is None else ks:
        for i, (a, b) in enumerate(((w[0], x[0]), (w[0], x[1]), (w[1], x[0]))):
            last = pe.eng.matmul(out, a(k), b(k), start=(opens and k == 0 and i == 0), stop=(k == kt - 1 and i == 2),
                                 skip_group_check=ks is not None)
    return last


def mixer(nc, m, A, steps, done, sems):
    pe_done, act_done, dve_done, pool_done = (done[n] for n in ("pe", "act", "dve", "pool"))
    PS = m.PS
    m.xn = m.xn1
    w_in, w_out = A["w_in"][0], A["w_out"][0]
    RC = 3 * BR
    panels = [(w_in, RC + 3 * BR, PW), (w_in, RC + 3 * BR + PW, 32)]
    panels += [(w_in, RC + c + PW * i, PW) for c in (BR, 0, 2 * BR) for i in range(2)]
    panels += [(w_in, c + PW * i, PW) for i in range(2) for c in (0, 2 * BR, BR)]
    NPROJ = len(panels)
    panels += [(w_out, PW * i, PW) for i in range(4)]
    NP = len(panels)
    w_loaded = sems("w_loaded0"), sems("w_loaded1")
    x_loaded = [sems(f"x_loaded{t}") for t in range(TT)]
    rows_loaded, lr_loaded, g2_loaded, gain_loaded = (sems(n) for n in ("rows_loaded", "lr_loaded", "g2_loaded",
                                                                        "gain_loaded"))

    def view(buf, p):
        return buf[:, p % 2, 0:KT * panels[p][2]].rearrange("p (k n) -> p k n", k=KT)

    ztiles = [(0, 0, P, ROW["mu_wa"], m.wad[:, :]), (0, 1, P, ROW["mu_g"], m.gd[:, :]),
               (1, 0, 32, ROW["mu_g"] + 1, m.gd2[:, :])]
    for p0, mu, dst in ((2, "mu_k", m.BK[:, 1]), (4, "mu_r", m.APR[:, 1]), (6, "mu_v", m.vq[:, :])):
        ztiles += [(p0 + j // 2, j % 2, P, ROW[mu] + j, dst[:, j, :]) for j in range(JT)]
    NZ = len(ztiles)

    def col(name, j=0, rows=P):
        return m.pcol[0:rows, ROW[name] + j:ROW[name] + j + 1]

    rowsrc = [(ROW["pre_mix"], A["pre_mix_g"].rearrange("l (a b) -> (l a) b", b=P)),
              (ROW["mu_r"], A["shift_mu"][:, 0:3 * BR + P].rearrange("l (a b) -> (l a) b", b=P)),
              (ROW["mu_g"], A["shift_mu"][:, 3 * BR + P:3 * BR + 2 * P]),
              (ROW["mu_g"] + 1, A["shift_mu"][:, 3 * BR + 2 * P:3 * BR + 2 * P + 32])]
    rowsrc += [(ROW[n], A[n].rearrange("l (a b) -> (l a) b", b=P)) for n in ("w0", "a0", "k_k", "k_a", "lnx_w", "lnx_b")]
    rowsrc += [(ROW["r_k"], A["r_k"].rearrange("l (a c) b -> (l a) (c b)", c=2)),
               (ROW["conv"], A["conv_a_w"].rearrange("l k (a b) -> (l k a) b", b=P))]

    with nc.Block() as block:

        @block.sync
        def _(sp):
            E = Engine(steps, "sp", sp, done)
            for t in range(TT):
                sp.dma_start(m.x[:, t, :], A["x"][0, P * t:P * t + P, :]).then_inc(x_loaded[t], 16)
            for p in range(NP):
                src, c, w = panels[p]
                if p >= 2:
                    E.wait_ge(dve_done, E.at(("w lo", p - 2)))
                s = src.rearrange("(k q) n -> q k n", q=P)
                for k in (0, 4):
                    sp.dma_start(view(m.raw, p)[:, k:k + 4, :], s[:, k:k + 4, c:c + w]).then_inc(w_loaded[p % 2], 16)
                if p == NPROJ + 1:
                    E.wait_ge(act_done, E.at(("y", TT - 1)))
                    for t in range(TT):
                        sp.dma_start(m.x[:, t, :], A["x"][0, P * t:P * t + P, :]).then_inc(x_loaded[t], 16)
                    E.wait_ge(dve_done, E.at(("mix", JT - 1)))
                    sp.dma_start(m.gain[:, :], A["post_mix_g"].partition_broadcast(P)).then_inc(gain_loaded, 16)

        @block.gpsimd
        def _(pool):
            E = Engine(steps, "pool", pool, done)
            constants(E, m)
            for t in range(TT):
                pool.wait_ge(x_loaded[t], 32)
            mix_out_pool(E, m, "n2")

        @block.tensor
        def _(pe):
            E = Engine(steps, "pe", pe, done)
            banks = Banks(E)
            aux = [0]

            def aux_bank(reader):
                b = 4 + aux[0] % 4
                aux[0] += 1
                banks.use(b, reader)
                return b

            def turned(step, reader, blocks, rows=P):
                b = 4 + aux[0] % 4
                aux[0] += 1
                turn(E, m, banks, step, b, reader, blocks, rows)

            def one(step, reader, lhsT, rhs):
                b = aux_bank(reader)
                m.bank[step] = b
                pe.matmul(PS[0:lhsT.shape[1], b, :], lhsT, rhs, start=True, stop=True).then_inc(pe_done, 1)
                E.counted(step)

            def panel(p):
                E.wait_ge(dve_done, E.at(("w lo", p)))
                H, L = view(m.wh, p), view(m.wl, p)
                for i in range((panels[p][2] + P - 1) // P):
                    n = min(P, panels[p][2] - P * i)
                    b, c = 2 * (p % 2) + i, slice(P * i, P * i + n)
                    banks.use(b, ("evac", p, i))
                    project(E, m, (lambda k: H[:, k, c], lambda k: L[:, k, c]),
                            (lambda k: m.hH[:, k, :], lambda k: m.hL[:, k, :]), PS[0:n, b, :]).then_inc(pe_done, 1)
                    E.counted(("panel", p, i))

            E.wait_ge(pool_done, E.at("ident"))
            E.wait_ge(pool_done, E.at("constants"))
            pe.wait_ge(rows_loaded, 16 * len(rowsrc))
            turned("turn params", "params", [m.prow[:, :]])
            for q in range(2):
                turned(("turn indh", q), ("indh", q), [m.indh[:, 4 * q + i, :] for i in range(4)])
            turned(("turn indw", 0), ("indw", 0), [m.indw[:, i, :] for i in range(4)])
            E.wait_ge(dve_done, E.at(("n1", "xn", TT - 1)))
            aux[0] = 0
            for j in range(KT):
                turned(("n1", "turn", j), ("n1", "lo", j), [m.xn[:, t, P * j:P * j + P] for t in range(TT)])
            turned(("turn indw", 1), ("indw", 1), [m.indw[:, 4 + i, :] for i in range(4)])
            E.wait_ge(dve_done, E.at(("n1", "lo", KT - 1)))
            for p in range(8):
                panel(p)
            E.wait_ge(act_done, E.at("tanh"))
            pe.wait_ge(lr_loaded, 32)
            for j in range(JT):
                one(("zw", j), ("wsig", j), m.w2a2[0:64, P * j:P * j + P], m.wad[0:64, :])
                one(("za", j), ("a", j), m.w2a2[64:P, P * j:P * j + P], m.wad[64:P, :])
            for c in range(TT):
                E.wait_ge(dve_done, E.at(("q", NZ - 1)))
                turned(("turn v", c), ("v tokens", c), [m.vq[:, j, P * c:P * c + P] for j in range(JT)])
            b = m.bank["ss"] = aux_bank("ss max")
            for j in range(JT):
                E.wait_ge(act_done, E.at(("kk sq", j)))
                last = pe.matmul(PS[0:16, b, :], m.indh[:, j, 0:16], m.sq[:, j, :], start=(j == 0), stop=(j == JT - 1))
            last.then_inc(pe_done, 1)
            E.counted("ss")
            panel(8)
            panel(9)
            E.wait_ge(dve_done, E.at("rn"))
            E.wait_ge(act_done, E.at(("indh", 1)))
            for j in range(JT):
                one(("rn spread", j), ("kkn", j), m.indhT[:, j, :], m.rnS[:, :])
            panel(10)
            panel(11)
            panel(12)
            for j in range(JT):
                E.wait_ge(dve_done, E.at(("rkr", j)))
                one(("bonus", j), ("bonus v", j), m.bd[:, :], m.sq[:, j, :])
            panel(13)

            def scores(c, hf):
                for i in range(4):
                    j, e = 2 * hf + i // 2, i % 2
                    rows, cc, b = slice(64 * e, 64 * e + 64), slice(P * c, P * c + P), 4 * hf + i
                    banks.use(b, ("scores", c, hf, i))
                    for q in range(2):
                        last = pe.matmul(PS[:, b, 256 * q:256 * q + 256], m.BK[rows, q, j, cc], m.APR[rows, :, j, cc],
                                         start=True, stop=True)
                    last.then_inc(pe_done, 1)
                    E.counted(("score mm", c, hf, i))

            def level(c, l, hf):
                b = 4 * hf
                E.wait_ge(dve_done, E.at(("scores", c, hf, 3) if l == 0 else ("X", c, l - 1, hf)))
                banks.use(b, ("T", c, l, hf))
                for i in range(4):
                    o, NT = PS[:, b, P * i:P * i + P], m.SC[:, c % 2, 4 * hf + i, 0, :]
                    if l == 0:
                        last = pe.transpose(o, NT, m.ident[:, :])
                    else:
                        last = pe.matmul(o, NT, m.Xi[:, hf, i, :], start=True, stop=True)
                last.then_inc(pe_done, 1)
                E.counted(("NX", c, l, hf))

            def update(c, l, hf):
                E.wait_ge(dve_done, E.at(("T", c, l, hf)))
                if l > 0:
                    E.wait_ge(dve_done, E.at(("XT", c, l - 1, hf)))
                if 0 < l < LEVELS - 1:
                    banks.use(4 * hf + 1, ("X", c, l, hf))
                    for i in range(4):
                        last = pe.matmul(PS[:, 4 * hf + 1, P * i:P * i + P], m.XTi[:, c % 2, hf, i, :], m.Ti[:, hf, i, :],
                                         start=True, stop=True)
                    last.then_inc(pe_done, 1)
                    E.counted(("dX", c, l, hf))
                banks.use(4 * hf + 2, ("XT", c, l, hf))
                for i in range(4):
                    o = PS[:, 4 * hf + 2, P * i:P * i + P]
                    if l == 0:
                        last = pe.transpose(o, m.Ti[:, hf, i, :], m.ident[:, :])
                    else:
                        last = pe.matmul(o, m.Ti[:, hf, i, :], m.XTi[:, c % 2, hf, i, :], start=True, stop=True)
                last.then_inc(pe_done, 1)
                E.counted(("dXT", c, l, hf))

            def state(c, step):
                par, cc = c % 2, slice(P * c, P * c + P)
                if step == 0:
                    for q in range(2):
                        turn(E, m, banks, ("turn bk", c, q), 3 + 4 * q, ("bk tokens", c, q),
                             [m.BK[:, q, j, cc] for j in range(JT)])
                if step == 1:
                    banks.use(3, ("rhs", c))
                    E.wait_ge(dve_done, E.at(("S", c - 1) if c else "S 0"))
                    for j in range(JT):
                        pe.matmul(PS[:, 3, P * j:P * j + P], m.APR[:, 0, j, cc], m.S[:, par, j, :], start=True, stop=False,
                                  skip_group_check=True)
                        for e in range(2):
                            h = 2 * j + e
                            last = pe.matmul(PS[:, 3, 64 * h:64 * h + 64], m.SC[:, par, h, 2, :],
                                             m.Vt[:, c, 64 * h:64 * h + 64], start=False, stop=True, skip_group_check=True)
                    last.then_inc(pe_done, 1)
                    E.counted(("rhs mm", c))
                if step == 2:
                    banks.use(7, ("sa", c))
                    E.wait_ge(act_done, E.at(("rhs", c)))
                    E.wait_ge(dve_done, E.at(("XT", c, LEVELS - 1, 0)))
                    E.wait_ge(dve_done, E.at(("XT", c, LEVELS - 1, 1)))
                    for h in range(2 * JT):
                        last = pe.matmul(PS[:, 7, 64 * h:64 * h + 64], m.XTi[:, par, h // 4, h % 4, :],
                                         m.rhs[:, 64 * h:64 * h + 64], start=True, stop=True)
                    last.then_inc(pe_done, 1)
                    E.counted(("sa mm", c))
                if step == 3 and c < TT - 1:
                    banks.use(3, ("S add", c))
                    E.wait_ge(act_done, E.at(("sa", c)))
                    E.wait_ge(act_done, E.at(("bk tokens", c, 0)))
                    E.wait_ge(act_done, E.at(("bk tokens", c, 1)))
                    for j in range(JT):
                        o = PS[:, 3, P * j:P * j + P]
                        pe.matmul(o, m.BKT[:, 0, j, :], m.sa[:, P * j:P * j + P], start=True, stop=False)
                        last = pe.matmul(o, m.BKT[:, 1, j, :], m.Vt[:, c, P * j:P * j + P], start=False, stop=True)
                    last.then_inc(pe_done, 1)
                    E.counted(("S mm", c))
                if step == 4:
                    banks.use(7, ("y", c))
                    for j in range(JT):
                        pe.matmul(PS[:, 7, P * j:P * j + P], m.S[:, par, j, :], m.APR[:, 1, j, cc], start=True, stop=False,
                                  skip_group_check=True)
                        for e in range(2):
                            h = 2 * j + e
                            o = PS[64 * e:64 * e + 64, 7, P * j:P * j + P]
                            pe.matmul(o, m.sa[:, 64 * h:64 * h + 64], m.SC[:, par, h, 1, :], start=False, stop=False,
                                      skip_group_check=True)
                            last = pe.matmul(o, m.Vt[:, c, 64 * h:64 * h + 64], m.SC[:, par, h, 3, :], start=False,
                                             stop=True, skip_group_check=True)
                    last.then_inc(pe_done, 1)
                    E.counted(("y mm", c))

            for before in [("prep", j) for j in range(JT)]:
                E.wait_ge(*E.point(before))
            E.wait_ge(*E.point(("v tokens", TT - 1)))
            for c in range(TT + 1):
                if c < TT:
                    scores(c, 0)
                    scores(c, 1)
                for l in range(LEVELS):
                    if c < TT:
                        for hf in range(2):
                            level(c, l, hf)
                        for hf in range(2):
                            update(c, l, hf)
                    if c > 0 and l < 5:
                        state(c - 1, l)

            aux[0] = 0
            E.wait_ge(act_done, E.at(("y", TT - 1)))
            for j in range(JT):
                one(("y mean", j), ("y centred", j), m.bd[:, :], m.yT[:, j, :])
            pe.wait_ge(g2_loaded, 32)
            for j in range(JT):
                banks.use(j, ("mix", j))
                pe.matmul(PS[:, j, :], m.g2a[:, P * j:P * j + P], m.gd[:, :], start=True, stop=False)
                pe.matmul(PS[:, j, :], m.g2b[:, P * j:P * j + P], m.gd2[:, :], start=False,
                          stop=True).then_inc(pe_done, 1)
                E.counted(("gate", j))
            b = m.bank["y ss"] = 5
            banks.use(b, "y var")
            for j in range(JT):
                E.wait_ge(act_done, E.at(("y sq", j)))
                last = pe.matmul(PS[0:16, b, :], m.indh[:, j, 0:16], m.ysq[:, j, :], start=(j == 0), stop=(j == JT - 1))
            last.then_inc(pe_done, 1)
            E.counted("y ss")
            def out_part(i, t, ks):
                p, tt = NPROJ + i, slice(P * t, P * t + P)
                H, L = view(m.wh, p), view(m.wl, p)
                return project(E, m, (lambda k: m.hH[:, k, tt], lambda k: m.hL[:, k, tt]),
                               (lambda k: H[:, k, :], lambda k: L[:, k, :]),
                               PS[:, 2 * t + i // 2, PW * (i % 2):PW * (i % 2) + PW], ks=ks, opens=i != 1)

            E.wait_ge(dve_done, E.at(("mix lo", JT - 1)))
            E.wait_ge(dve_done, E.at(("w lo", NPROJ + 1)))
            for t in (2, 3, 0, 1):
                if t == 0:
                    E.wait_ge(dve_done, E.at("y rstd"))
                    for j in range(JT):
                        b = m.bank["y rstd spread", j] = 5 + 2 * (j % 2)
                        banks.use(b, ("y scaled", j))
                        pe.matmul(PS[:, b, :], m.indhT[:, j, :], m.rnS[:, :], start=True, stop=True).then_inc(pe_done, 1)
                        E.counted(("y rstd spread", j))
                banks.use(2 * t, ("n2", "out", t))
                for i in range(2):
                    out_part(i, t, range(JT))
            E.wait_ge(dve_done, E.at(("mix lo", KT - 1)))
            for i in range(2):
                for t in range(TT):
                    out_part(i, t, range(JT, KT)).then_inc(pe_done, 1)
                    E.counted(("out mm", i, t))
            for i in range(2, 4):
                E.wait_ge(dve_done, E.at(("w lo", NPROJ + i)))
                for t in range(TT):
                    if i == 2:
                        banks.use(2 * t + 1, ("n2", "out", t))
                    out_part(i, t, range(KT)).then_inc(pe_done, 1)
                    E.counted(("out mm", i, t))

        @block.scalar
        def _(act):
            E = Engine(steps, "act", act, done)
            E.wait_ge(act_done, E.so_far())
            E.wait_ge(pool_done, E.at("prow zero"))
            for r0, src in rowsrc:
                n, w = src.shape
                act.dma_start(m.prow[r0:r0 + n, 0:w], src).then_inc(rows_loaded, 16)
            E.wait_ge(act_done, E.so_far())
            E.wait_ge(pool_done, E.at("eps"))
            for t in range(TT):
                act.wait_ge(x_loaded[t], 16)
                act.activation(m.xn[:, t, :], m.x[:, t, :], ACT.Square,
                               accum_out=m.stat[:, 0, t:t + 1]).then_inc(act_done, 1)
                E.counted(("n1", "ss", t))
            E.wait_ge(act_done, E.so_far())
            act.activation(m.stat[:, 1, :], m.stat[:, 0, :], ACT.Sqrt, bias=m.eps[:, 0:1],
                           scale=1.0 / D).then_inc(act_done, 1)
            E.counted(("n1", "sd"))

            def split(p):
                act.wait_ge(w_loaded[p % 2], 32 * (p // 2 + 1))
                if p >= 2:
                    last = (panels[p - 2][2] + P - 1) // P - 1
                    E.wait_ge(act_done, E.so_far())
                    E.wait_ge(pe_done,
                              E.at(("panel", p - 2, last) if p - 2 < NPROJ else ("out mm", p - 2 - NPROJ, TT - 1)))
                n = KT * panels[p][2]
                act.activation(m.wh[:, p % 2, 0:n], m.raw[:, p % 2, 0:n], ACT.Copy).then_inc(act_done, 1)
                E.counted(("w hi", p))

            split(0)
            split(1)
            E.wait_ge(pool_done, E.at("constants"))
            act.activation(m.rnS[:, :], m.zs[0:RN, 0, 0:T], ACT.Copy).then_inc(act_done, 1)
            E.counted("rows zero")
            for q in range(2):
                E.wait_ge(act_done, E.so_far())
                E.wait_ge(pe_done, E.at(("turn indh", q)))
                act.activation(m.indhT[:, 4 * q:4 * q + 4, :].rearrange("p a b -> p (a b)"),
                               PS[0:RN, m.bank["turn indh", q], :], ACT.Copy).then_inc(act_done, 1)
                E.counted(("indh", q))
            for q in (0,):
                E.wait_ge(act_done, E.so_far())
                E.wait_ge(pe_done, E.at(("turn indw", q)))
                act.activation(m.indwT[:, 4 * q:4 * q + 4, :].rearrange("p a b -> p (a b)"),
                               PS[0:RN, m.bank["turn indw", q], :], ACT.Copy).then_inc(act_done, 1)
                E.counted(("indw", q))
            E.wait_ge(act_done, E.so_far())
            E.wait_ge(dve_done, E.at("params"))
            norm_split_scalar(E, m, "n1", lambda j: col("pre_mix", j))
            for q in (1,):
                E.wait_ge(act_done, E.so_far())
                E.wait_ge(pe_done, E.at(("turn indw", q)))
                act.activation(m.indwT[:, 4 * q:4 * q + 4, :].rearrange("p a b -> p (a b)"),
                               PS[0:RN, m.bank["turn indw", q], :], ACT.Copy).then_inc(act_done, 1)
                E.counted(("indw", q))
            E.wait_ge(act_done, E.so_far())
            E.wait_ge(dve_done, E.at(("n1", "xn", TT - 1)))
            act.dma_start(m.w2a2[0:64, :], A["w2"][0]).then_inc(lr_loaded, 16)
            act.dma_start(m.w2a2[64:P, :], A["a2"][0]).then_inc(lr_loaded, 16)
            z = 0
            for p in range(8):
                while z < NZ and ztiles[z][0] == p:
                    _, i, rows, mu, _ = ztiles[z]
                    E.wait_ge(act_done, E.so_far())
                    E.wait_ge(pe_done, E.at(("panel", p, i)))
                    if z >= 2:
                        E.wait_ge(act_done, E.so_far())
                        E.wait_ge(dve_done, E.at(("q", z - 2)))
                    act.activation(m.zs[0:rows, z % 2, 1:T + 1], PS[0:rows, 2 * (p % 2) + i, :], ACT.Copy,
                                   scale=m.pcol[0:rows, mu:mu + 1]).then_inc(act_done, 1)
                    E.counted(("mu q", z))
                    z += 1
                split(p + 2)
                if p == 1:
                    E.wait_ge(act_done, E.so_far())
                    E.wait_ge(dve_done, E.at(("q", 2)))
                    act.activation(m.wad[0:64, :], m.wad[0:64, :], ACT.Tanh).then_inc(act_done, 1)
                    E.counted("tanh")
                    act.activation(m.gd[:, :], m.gd[:, :], ACT.Sigmoid).then_inc(act_done, 1)
                    E.counted("gd")
                    act.activation(m.gd2[:, :], m.gd2[:, :], ACT.Sigmoid).then_inc(act_done, 1)
                    E.counted("gd2")
                if p == 4:
                    for j in range(JT):
                        E.wait_ge(act_done, E.so_far())
                        E.wait_ge(dve_done, E.at(("kk", j)))
                        act.activation(m.sq[:, j, :], m.APR[:, 0, j, :], ACT.Square).then_inc(act_done, 1)
                        E.counted(("kk sq", j))
            for j in range(JT):
                E.wait_ge(act_done, E.so_far())
                E.wait_ge(pe_done, E.at(("zw", j)))
                act.activation(m.bv[:, j, :], PS[:, m.bank["zw", j], :], ACT.Sigmoid,
                               bias=col("w0", j)).then_inc(act_done, 1)
                E.counted(("wsig", j))
                E.wait_ge(act_done, E.so_far())
                E.wait_ge(pe_done, E.at(("za", j)))
                act.activation(m.BK[:, 0, j, :], PS[:, m.bank["za", j], :], ACT.Sigmoid,
                               bias=col("a0", j)).then_inc(act_done, 1)
                E.counted(("a", j))
            for c in range(TT):
                E.wait_ge(act_done, E.so_far())
                E.wait_ge(pe_done, E.at(("turn v", c)))
                act.activation(m.Vt[:, c, :], PS[:, m.bank["turn v", c], :], ACT.Copy).then_inc(act_done, 1)
                E.counted(("v tokens", c))
            E.wait_ge(act_done, E.so_far())
            E.wait_ge(dve_done, E.at("ss max"))
            act.activation(m.rn[:, :], m.rn[:, :], ACT.Sqrt).then_inc(act_done, 1)
            E.counted("kk norm")

            def conv_gate(p):
                for i in range(2):
                    E.wait_ge(act_done, E.so_far())
                    E.wait_ge(pe_done, E.at(("panel", p, i)))
                    if p > 8:
                        E.wait_ge(act_done, E.so_far())
                        E.wait_ge(dve_done, E.at(("conv in", p - 2, i)))
                    act.activation(m.gB[:, i, :], PS[:, 2 * (p % 2) + i, :], ACT.Copy).then_inc(act_done, 1)
                    E.counted(("evac", p, i))

            def decays(j):
                E.wait_ge(act_done, E.so_far())
                E.wait_ge(dve_done, E.at(("decay mid", j)))
                if j:
                    E.wait_ge(act_done, E.so_far())
                    E.wait_ge(dve_done, E.at(("prep", j - 1)))
                act.activation(m.emid[:, j, :], m.Gx[:, :, 64], ACT.Exp, scale=-DECAY).then_inc(act_done, 1)
                E.counted(("emid", j))
                act.activation(m.Ep[:, :, :], m.Gc[:, :, :], ACT.Exp, scale=-DECAY).then_inc(act_done, 1)
                E.counted(("Ep", j))
                act.activation(m.Em[:, :, :], m.Gc[:, :, :], ACT.Exp, scale=DECAY).then_inc(act_done, 1)
                E.counted(("Em", j))

            conv_gate(8)
            split(10)
            split(11)
            decays(0)
            decays(1)
            split(12)
            decays(2)
            conv_gate(11)
            split(13)
            decays(3)
            split(14)
            split(15)

            for c in range(TT + 1):
                for l in range(5):
                    if c == 0:
                        continue
                    cc = slice(P * (c - 1), P * c)
                    if l == 0:
                        for q in range(2):
                            E.wait_ge(act_done, E.so_far())
                            E.wait_ge(pe_done, E.at(("turn bk", c - 1, q)))
                            if c > 1:
                                E.wait_ge(act_done, E.so_far())
                                E.wait_ge(pe_done, E.at(("S mm", c - 2)))
                            act.activation(m.BKT[:, q, :, :], PS[:, 3 + 4 * q, :], ACT.Copy).then_inc(act_done, 1)
                            E.counted(("bk tokens", c - 1, q))
                    if l == 1:
                        E.wait_ge(act_done, E.so_far())
                        E.wait_ge(pe_done, E.at(("rhs mm", c - 1)))
                        act.activation(m.rhs[:, :], PS[:, 3, :], ACT.Copy).then_inc(act_done, 1)
                        E.counted(("rhs", c - 1))
                    if l == 2:
                        E.wait_ge(act_done, E.so_far())
                        E.wait_ge(pe_done, E.at(("sa mm", c - 1)))
                        act.activation(m.sa[:, :], PS[:, 7, :], ACT.Copy).then_inc(act_done, 1)
                        E.counted(("sa", c - 1))
                    if l == 4:
                        E.wait_ge(act_done, E.so_far())
                        E.wait_ge(pe_done, E.at(("y mm", c - 1)))
                        act.activation(m.yT[:, :, cc], PS[:, 7, :].rearrange("p (a b) -> p a b", a=JT),
                                       ACT.Copy).then_inc(act_done, 1)
                        E.counted(("y", c - 1))
            act.dma_start(m.g2a[:, :], A["g2"][0, 0:P, :]).then_inc(g2_loaded, 16)
            act.dma_start(m.g2b[:, :], A["g2"][0, P:P + 32, :]).then_inc(g2_loaded, 16)
            for j in range(JT):
                act.activation(m.hH[:, j, :], m.ya[:, j, :], ACT.Copy).then_inc(act_done, 1)
                E.counted(("mix hi", j))
            for j in range(JT):
                E.wait_ge(act_done, E.so_far())
                E.wait_ge(dve_done, E.at(("y centred", j)))
                act.activation(m.ysq[:, j, :], m.yT[:, j, :], ACT.Square).then_inc(act_done, 1)
                E.counted(("y sq", j))
            E.wait_ge(act_done, E.so_far())
            E.wait_ge(dve_done, E.at("y var"))
            act.activation(m.rn2[:, :], m.rn2[:, :], ACT.Sqrt).then_inc(act_done, 1)
            E.counted("y sd")
            for j in range(JT):
                E.wait_ge(act_done, E.so_far())
                E.wait_ge(dve_done, E.at(("mix", j)))
                act.activation(m.hH[:, JT + j, :], m.yT[:, j, :], ACT.Copy).then_inc(act_done, 1)
                E.counted(("mix hi", JT + j))
            split(16)
            split(17)
            mix_out_scalar(E, m, "n2", lambda t: [("out mm", 3, t)])

        @block.vector
        def _(dve):
            E = Engine(steps, "dve", dve, done)
            E.wait_ge(dve_done, E.so_far())
            E.wait_ge(pe_done, E.at("turn params"))
            dve.tensor_copy(m.pcol[:, :], PS[:, m.bank["turn params"], 0:P]).then_inc(dve_done, 1)
            E.counted("params")
            E.wait_ge(dve_done, E.so_far())
            mus = ROW["w0"] - ROW["mu_r"]
            dve.tensor_scalar(m.omm[:, 0:mus], m.pcol[:, ROW["mu_r"]:ROW["w0"]], -1.0, 1.0, ALU.mult,
                              ALU.add).then_inc(dve_done, 1)
            E.counted("1 - mu")
            dve.tensor_scalar(m.omm[:, 16:20], m.pcol[:, ROW["k_a"]:ROW["k_a"] + 4], -1.0, 1.0, ALU.mult,
                              ALU.add).then_inc(dve_done, 1)
            E.counted("1 - k_a")
            scale_rows(E, m, "n1", range(TT))

            def split(p):
                n = KT * panels[p][2]
                E.wait_ge(dve_done, E.so_far())
                E.wait_ge(act_done, E.at(("w hi", p)))
                dve.tensor_tensor(m.wl[:, p % 2, 0:n], m.raw[:, p % 2, 0:n], m.wh[:, p % 2, 0:n].bitcast(F32),
                                  ALU.subtract).then_inc(dve_done, 1)
                E.counted(("w lo", p))

            split(0)
            split(1)
            norm_split_vector(E, m, "n1", lambda j: col("pre_mix", j))
            z = 0
            E.wait_ge(dve_done, E.so_far())
            for p in range(8):
                while z < NZ and ztiles[z][0] == p:
                    _, i, rows, mu, dst = ztiles[z]
                    E.wait_ge(dve_done, E.so_far())
                    E.wait_ge(act_done, E.at(("mu q", z)))
                    dve.scalar_tensor_tensor(dst, PS[0:rows, 2 * (p % 2) + i, :],
                                             m.omm[0:rows, mu - ROW["mu_r"]:mu - ROW["mu_r"] + 1],
                                             m.zs[0:rows, z % 2, 0:T], ALU.mult, ALU.add).then_inc(dve_done, 1)
                    E.counted(("q", z))
                    steps.found["evac", p, i] = steps.found["q", z]
                    z += 1
                    if p in (2, 3):
                        j = z - 4
                        E.wait_ge(dve_done, E.so_far())
                        dve.tensor_scalar(m.APR[:, 0, j, :], m.BK[:, 1, j, :], col("k_k", j), None,
                                          ALU.mult).then_inc(dve_done, 1)
                        E.counted(("kk", j))
                split(p + 2)
            E.wait_ge(dve_done, E.so_far())
            E.wait_ge(pe_done, E.at("ss"))
            dve.tensor_scalar(m.rn[:, :], PS[0:16, m.bank["ss"], :], 1e-24, None, ALU.max).then_inc(dve_done, 1)
            E.counted("ss max")
            for j in range(JT):
                E.wait_ge(dve_done, E.so_far())
                E.wait_ge(act_done, E.at(("a", j)))
                dve.tensor_scalar(m.cv[:, :], m.BK[:, 0, j, :], col("k_a", j), m.omm[:, 16 + j:17 + j], ALU.mult,
                                  ALU.add).then_inc(dve_done, 1)
                E.counted(("k scale", j))
                E.wait_ge(dve_done, E.so_far())
                dve.tensor_tensor(m.BK[:, 1, j, :], m.BK[:, 1, j, :], m.cv[:, :], ALU.mult).then_inc(dve_done, 1)
                E.counted(("k4", j))
                E.wait_ge(dve_done, E.so_far())
                dve.scalar_tensor_tensor(m.sq[:, j, :], m.BK[:, 1, j, :], col("r_k", j), m.APR[:, 1, j, :], ALU.mult,
                                         ALU.mult).then_inc(dve_done, 1)
                E.counted(("rkr", j))
            E.wait_ge(dve_done, E.so_far())
            E.wait_ge(act_done, E.at("kk norm"))
            dve.reciprocal(m.rn[:, :], m.rn[:, :]).then_inc(dve_done, 1)
            E.counted("rn whole")
            split_rows(E, m, m.rn[:, :], "rn")

            def conv_in(p):
                for i in range(2):
                    E.wait_ge(dve_done, E.so_far())
                    E.wait_ge(act_done, E.at(("evac", p - 1, i)))
                    E.wait_ge(pe_done, E.at(("panel", p, i)))
                    dve.tensor_tensor(m.cu[:, i, :], PS[:, 2 * (p % 2) + i, :], m.gB[:, i, :],
                                      ALU.mult).then_inc(dve_done, 1)
                    E.counted(("conv in", p, i))
                    steps.found["evac", p, i] = steps.found["conv in", p, i]

            def conv_out(p):
                for i in range(2):
                    j = (p - 10) // 3 * 2 + i
                    E.wait_ge(dve_done, E.so_far())
                    tap = lambda k: col("conv", 4 * k + j)
                    dve.tensor_scalar(m.cv[:, :], m.cu[:, i, :], tap(2), None, ALU.mult).then_inc(dve_done, 1)
                    E.counted(("tap 2", j))
                    E.wait_ge(dve_done, E.so_far())
                    dve.scalar_tensor_tensor(m.cv[:, 1:T], m.cu[:, i, 0:T - 1], tap(1), m.cv[:, 1:T], ALU.mult,
                                             ALU.add).then_inc(dve_done, 1)
                    E.counted(("tap 1", j))
                    E.wait_ge(dve_done, E.so_far())
                    dve.scalar_tensor_tensor(m.cv[:, 2:T], m.cu[:, i, 0:T - 2], tap(0), m.cv[:, 2:T], ALU.mult,
                                             ALU.add).then_inc(dve_done, 1)
                    E.counted(("tap 0", j))
                    E.wait_ge(dve_done, E.so_far())
                    E.wait_ge(pe_done, E.at(("panel", p, i)))
                    dve.tensor_tensor(m.ya[:, j, :], PS[:, 2 * (p % 2) + i, :], m.cv[:, :],
                                      ALU.mult).then_inc(dve_done, 1)
                    E.counted(("ya", j))
                    steps.found["evac", p, i] = steps.found["ya", j]

            def prep(j):
                for c in range(TT):
                    if j:
                        E.wait_ge(dve_done, E.so_far())
                        E.wait_ge(act_done, E.at(("emid", j - 1)))
                    dve.tensor_tensor_scan(m.Gx[:, c, 1:P + 1], m.onesP[:, :], m.bv[:, j, P * c:P * c + P], 0.0,
                                           ALU.mult, ALU.add).then_inc(dve_done, 1)
                    E.counted(("decay sum", j, c))
                E.wait_ge(dve_done, E.so_far())
                if j:
                    E.wait_ge(dve_done, E.so_far())
                    E.wait_ge(act_done, E.at(("Em", j - 1)))
                dve.tensor_tensor(m.Gc[:, :, :], m.Gx[:, :, :], m.Gx[:, :, 64:65].to_broadcast([P, TT, P + 1]),
                                  ALU.subtract).then_inc(dve_done, 1)
                E.counted(("decay mid", j))
                E.wait_ge(dve_done, E.so_far())
                E.wait_ge(pe_done, E.at(("rn spread", j)))
                dve.tensor_tensor(m.APR[:, 0, j, :], PS[:, m.bank["rn spread", j], :], m.APR[:, 0, j, :],
                                  ALU.mult).then_inc(dve_done, 1)
                E.counted(("kkn", j))
                E.wait_ge(dve_done, E.so_far())
                dve.tensor_tensor(m.BK[:, 0, j, :], m.BK[:, 0, j, :], m.APR[:, 0, j, :], ALU.mult).then_inc(dve_done, 1)
                E.counted(("kk a", j))
                E.wait_ge(dve_done, E.so_far())
                E.wait_ge(act_done, E.at(("Em", j)))
                r = lambda ap: ap.rearrange("p (a b) -> p a b", a=TT)
                dve.tensor_tensor(m.fac[:, j, 0:TT - 1], m.Ep[:, 0:TT - 1, P], m.emid[:, j, 1:TT],
                                  ALU.mult).then_inc(dve_done, 1)
                E.counted(("fac", j))
                dve.tensor_tensor(r(m.APR[:, 1, j, :]), r(m.APR[:, 1, j, :]), m.Ep[:, :, 1:P + 1], ALU.mult)
                dve.tensor_tensor(r(m.BK[:, 1, j, :]), r(m.BK[:, 1, j, :]), m.Em[:, :, 1:P + 1], ALU.mult)
                dve.tensor_tensor(r(m.APR[:, 0, j, :]), r(m.APR[:, 0, j, :]), m.Ep[:, :, 0:P], ALU.mult)
                dve.scalar_tensor_tensor(r(m.BK[:, 0, j, :]), r(m.BK[:, 0, j, :]), -1.0, m.Em[:, :, 1:P + 1], ALU.mult,
                                         ALU.mult).then_inc(dve_done, 1)
                E.counted(("prep", j))

            conv_in(9)
            split(10)
            split(11)
            prep(0)
            prep(1)
            conv_out(10)
            split(12)
            prep(2)
            split(13)
            prep(3)
            conv_in(12)
            split(14)
            for j in range(JT):
                E.wait_ge(dve_done, E.so_far())
                E.wait_ge(pe_done, E.at(("bonus", j)))
                dve.tensor_tensor(m.bv[:, j, :], PS[:, m.bank["bonus", j], :], m.vq[:, j, :],
                                  ALU.mult).then_inc(dve_done, 1)
                E.counted(("bonus v", j))
            conv_out(13)
            split(15)
            dve.memset(m.S[:, 0, :, :], 0.0).then_inc(dve_done, 1)
            E.counted("S 0")

            def four(ap2):
                return bass.AP(tensor=ap2.tensor, offset=ap2.offset, ap=[ap2.ap[0], [0, 4], ap2.ap[1]])

            def f4(ap):
                return ap.rearrange("p (a b) -> p a b", a=4)

            for c in range(TT + 1):
                par = c % 2
                if c < TT:
                    for hf in range(2):
                        for i in range(4):
                            E.wait_ge(dve_done, E.so_far())
                            E.wait_ge(pe_done, E.at(("score mm", c, hf, i)))
                            if c > 1:
                                E.wait_ge(dve_done, E.so_far())
                                E.wait_ge(pe_done, E.at(("y mm", c - 2)))
                            dve.tensor_tensor(m.SC[:, par, 4 * hf + i, :, :], f4(PS[:, 4 * hf + i, :]),
                                              m.smask[:, :, :], ALU.mult).then_inc(dve_done, 1)
                            E.counted(("scores", c, hf, i))
                for l in range(LEVELS):
                    if c < TT:
                        for hf in range(2):
                            E.wait_ge(dve_done, E.so_far())
                            E.wait_ge(pe_done, E.at(("NX", c, l, hf)))
                            dve.tensor_tensor(m.Ti[:, hf, :, :], f4(PS[:, 4 * hf, :]), four(m.lmask[:, l, :]),
                                              ALU.mult).then_inc(dve_done, 1)
                            E.counted(("T", c, l, hf))
                        for hf in range(2):
                            if l == 0:
                                E.wait_ge(dve_done, E.so_far())
                                dve.tensor_tensor(m.Xi[:, hf, :, :], m.Ti[:, hf, :, :], four(m.ident[:, :]),
                                                  ALU.add).then_inc(dve_done, 1)
                                E.counted(("X", c, l, hf))
                                E.wait_ge(dve_done, E.so_far())
                                E.wait_ge(pe_done, E.at(("dXT", c, l, hf)))
                                if c > 1:
                                    E.wait_ge(dve_done, E.so_far())
                                    E.wait_ge(pe_done, E.at(("sa mm", c - 2)))
                                dve.tensor_tensor(m.XTi[:, par, hf, :, :], f4(PS[:, 4 * hf + 2, :]),
                                                  four(m.ident[:, :]), ALU.add).then_inc(dve_done, 1)
                                E.counted(("XT", c, l, hf))
                                continue
                            if l < LEVELS - 1:
                                E.wait_ge(dve_done, E.so_far())
                                E.wait_ge(pe_done, E.at(("dX", c, l, hf)))
                                x = halves(m.Xi[:, hf, :, :], l, 0)
                                dve.tensor_tensor(x, halves(f4(PS[:, 4 * hf + 1, :]), l, 0), x,
                                                  ALU.add).then_inc(dve_done, 1)
                                E.counted(("X", c, l, hf))
                            E.wait_ge(dve_done, E.so_far())
                            E.wait_ge(pe_done, E.at(("dXT", c, l, hf)))
                            x = halves(m.XTi[:, par, hf, :, :], l, 1)
                            dve.tensor_tensor(x, halves(f4(PS[:, 4 * hf + 2, :]), l, 1), x, ALU.add).then_inc(dve_done, 1)
                            E.counted(("XT", c, l, hf))
                    if 0 < c < TT and l == 3:
                        q = (c - 1) % 2
                        E.wait_ge(dve_done, E.so_far())
                        E.wait_ge(pe_done, E.at(("S mm", c - 1)))
                        dve.tensor_tensor(m.stmp[:, :, :], f4(PS[:, 3, :]), four(m.bd[:, :]),
                                          ALU.mult).then_inc(dve_done, 1)
                        E.counted(("S add", c - 1))
                        E.wait_ge(dve_done, E.so_far())
                        dve.tensor_tensor(m.stmp[:, :, :], m.stmp[:, :, :], m.S[:, q, :, :],
                                          ALU.add).then_inc(dve_done, 1)
                        E.counted(("S sum", c - 1))
                        E.wait_ge(dve_done, E.so_far())
                        dve.tensor_tensor(m.S[:, 1 - q, :, :], m.stmp[:, :, :],
                                          m.fac[:, :, c - 1:c].to_broadcast([P, JT, P]), ALU.mult).then_inc(dve_done, 1)
                        E.counted(("S", c - 1))

            for j in range(JT):
                E.wait_ge(dve_done, E.so_far())
                E.wait_ge(pe_done, E.at(("y mean", j)))
                dve.scalar_tensor_tensor(m.yT[:, j, :], PS[:, m.bank["y mean", j], :], -1.0 / 64, m.yT[:, j, :],
                                         ALU.mult, ALU.add).then_inc(dve_done, 1)
                E.counted(("y centred", j))
            for j in range(JT):
                E.wait_ge(dve_done, E.so_far())
                E.wait_ge(act_done, E.at(("mix hi", j)))
                dve.tensor_tensor(m.hL[:, j, :], m.ya[:, j, :], m.hH[:, j, :].bitcast(F32),
                                  ALU.subtract).then_inc(dve_done, 1)
                E.counted(("mix lo", j))
            E.wait_ge(dve_done, E.so_far())
            E.wait_ge(pe_done, E.at("y ss"))
            dve.tensor_scalar(m.rn2[:, :], PS[0:16, m.bank["y ss"], :], 1.0 / 64, GN_EPS, ALU.mult,
                              ALU.add).then_inc(dve_done, 1)
            E.counted("y var")
            E.wait_ge(dve_done, E.so_far())
            E.wait_ge(act_done, E.at("y sd"))
            dve.reciprocal(m.rn2[:, :], m.rn2[:, :]).then_inc(dve_done, 1)
            E.counted("y rstd whole")
            split_rows(E, m, m.rn2[:, :], "y rstd")
            for j in range(JT):
                y = m.yT[:, j, :]
                E.wait_ge(dve_done, E.so_far())
                E.wait_ge(pe_done, E.at(("y rstd spread", j)))
                dve.tensor_tensor(y, PS[:, m.bank["y rstd spread", j], :], y, ALU.mult).then_inc(dve_done, 1)
                E.counted(("y scaled", j))
                E.wait_ge(dve_done, E.so_far())
                dve.tensor_scalar(y, y, col("lnx_w", j), col("lnx_b", j), ALU.mult, ALU.add).then_inc(dve_done, 1)
                E.counted(("y affine", j))
                E.wait_ge(dve_done, E.so_far())
                dve.tensor_tensor(y, y, m.bv[:, j, :], ALU.add).then_inc(dve_done, 1)
                E.counted(("y bonus", j))
                E.wait_ge(dve_done, E.so_far())
                E.wait_ge(pe_done, E.at(("gate", j)))
                dve.tensor_tensor(y, PS[:, j, :], y, ALU.mult).then_inc(dve_done, 1)
                E.counted(("mix", j))
            for j in range(JT):
                E.wait_ge(dve_done, E.so_far())
                E.wait_ge(act_done, E.at(("mix hi", JT + j)))
                dve.tensor_tensor(m.hL[:, JT + j, :], m.yT[:, j, :], m.hH[:, JT + j, :].bitcast(F32),
                                  ALU.subtract).then_inc(dve_done, 1)
                E.counted(("mix lo", JT + j))
            split(16)
            split(17)
            dve.wait_ge(gain_loaded, 16)
            for t in range(TT):
                dve.wait_ge(x_loaded[t], 32)
            mix_out_vector(E, m, "n2")


def ffn(nc, m, A, steps, done, sems):
    pe_done, act_done, dve_done, pool_done = (done[n] for n in ("pe", "act", "dve", "pool"))
    PS, m.xn, m.gain, m.otmp = m.PS, m.xn2, m.fgain, m.ftmp
    w_up, w_down = A["w_up"][0], A["w_down"][0]
    w_loaded = sems("w_loaded0"), sems("w_loaded1")
    rows_loaded, gain_loaded = sems("rows_loaded"), sems("gain_loaded")
    UP = FT // 2
    DN = FT // 2
    DR = (DN - 3) // 2
    assert DN == 2 + 2 * DR + 1
    rowsrc = [(0, FROW["pre_ffn"], A["pre_ffn_g"].rearrange("l (a b) -> (l a) b", b=P)),
              (0, FROW["bias"], A["ffn_conv_b"].rearrange("l (a b) -> (l a) b", b=P)),
              (0, FROW["conv0"], A["ffn_conv_w"][0, 0:1, :].rearrange("l (a b) -> (l a) b", b=P)),
              (1, FROW2["conv1"], A["ffn_conv_w"][0, 1:2, :].rearrange("l (a b) -> (l a) b", b=P)),
              (1, FROW2["conv2"], A["ffn_conv_w"][0, 2:3, :].rearrange("l (a b) -> (l a) b", b=P))]

    def up_view(buf, s):
        return buf[:, s, :].rearrange("p (k n) -> p k n", k=KT)

    def dn_view(buf, s):
        return buf[:, s, :].rearrange("p (k n) -> p k n", k=2)

    with nc.Block() as block:

        @block.sync
        def _(sp):
            E = Engine(steps, "sp", sp, done)

            def load_up(s, col):
                src = w_up.rearrange("(k q) n -> q k n", q=P)
                for i in range(2):
                    c = col + DFF if i else col
                    sp.dma_start(up_view(m.raw, s)[:, :, P * i:P * i + P],
                                 src[:, :, bass.ds(c, P)]).then_inc(w_loaded[s], 16)

            def load_down(s, row):
                for i in range(2):
                    r = row + P if i else row
                    sp.dma_start(dn_view(m.raw, s)[:, i, :], w_down[bass.ds(r, P), :]).then_inc(w_loaded[s], 16)

            for b, r, src in rowsrc:
                sp.dma_start(m.frow[r:r + src.shape[0], b, :], src).then_inc(rows_loaded, 16)
            load_up(0, 0)
            load_up(1, P)
            sp.dma_start(m.gain[:, :], A["post_ffn_g"].partition_broadcast(P)).then_inc(gain_loaded, 16)
            E.wait_ge(dve_done, E.at(("up lo first", 1)))
            with E.loop("up", UP - 1) as i:
                for u in range(2):
                    col = sp.snap(i * (2 * P) + (2 + u) * P)
                    E.wait_ge(dve_done, E.at(("up lo", u), back=1))
                    load_up(u, col)
            for kk in range(2):
                E.wait_ge(dve_done, E.at(("up lo", kk), at=UP - 2))
                load_down(kk, 2 * P * kk)
            for kk in range(2, 4):
                E.wait_ge(dve_done, E.at(("up lo", kk % 2)))
                load_down(kk % 2, 2 * P * kk)
            with E.loop("down", DR - 1) as i:
                for u in range(2):
                    row = sp.snap(i * (4 * P) + (4 + u) * 2 * P)
                    E.wait_ge(dve_done, E.at(("dn lo", u), back=1))
                    load_down(u, row)
            E.wait_ge(dve_done, E.at(("dn lo", 0)))
            load_down(0, 2 * P * (DN - 1))

        @block.gpsimd
        def _(pool):
            E = Engine(steps, "pool", pool, done)
            for kk in range(2):
                g = m.G[:, 2 * kk:2 * kk + 2, :]
                E.wait_ge(dve_done, E.at(("G", 1), at=kk))
                pool.tensor_copy(m.gH[:, kk, :, :], g).then_inc(pool_done, 1)
                E.counted(("g hi first", kk))
                E.wait_ge(pool_done, E.at(("g hi first", kk)))
                pool.tensor_tensor(m.gL[:, kk, :, :], g, m.gH[:, kk, :, :].bitcast(F32),
                                   ALU.subtract).then_inc(pool_done, 1)
                E.counted(("g lo first", kk))
            mix_out_pool(E, m, "n4")

        @block.tensor
        def _(pe):
            E = Engine(steps, "pe", pe, done)
            banks = Banks(E)
            E.wait_ge(dve_done, E.at(("n3", "xn", 1)))
            E.wait_ge(act_done, E.at(("n3", "xn", 3)))
            for j in range(KT):
                if j == 4:
                    pe.wait_ge(rows_loaded, 16 * len(rowsrc))
                    for b, n in ((0, FROWS), (1, FROWS2)):
                        turn(E, m, banks, ("turn frow", b), b, ("fcol", b), [m.frow[0:n, b, :]], rows=n)
                turn(E, m, banks, ("n3", "turn", j), 4 + j % 4, ("n3", "lo", j),
                     [m.xn[:, t, P * j:P * j + P] for t in range(TT)])
            E.wait_ge(dve_done, E.at(("n3", "lo", KT - 1)))
            E.wait_ge(dve_done, E.at(("up lo first", 1)))
            with E.loop("up", UP):
                for u in range(2):
                    E.wait_ge(dve_done, E.at(("up lo", u), back=1))
                    H, L = up_view(m.wh, u), up_view(m.wl, u)
                    for i in range(2):
                        E.wait_ge(dve_done, E.at(("conv", u, i), back=1))
                        c = slice(P * i, P * i + P)
                        project(E, m, (lambda k: H[:, k, c], lambda k: L[:, k, c]),
                                (lambda k: m.hH[:, k, :], lambda k: m.hL[:, k, :]), PS[:, 2 * u + i, :]).then_inc(pe_done, 1)
                        E.counted(("up mm", u, i))

            def down(s, start, stop):
                H, L = dn_view(m.wh, s), dn_view(m.wl, s)
                for k in range(2):
                    for t in range(TT):
                        tt = slice(P * t, P * t + P)
                        for n in range(2):
                            cc = slice(T * n, T * n + T)
                            for i, (g, w) in enumerate(((m.gH, H), (m.gL, H), (m.gH, L))):
                                last = pe.matmul(PS[:, 2 * t + n, :], g[:, s, k, tt], w[:, k, cc],
                                                 start=(start and k == 0 and i == 0), stop=(stop and k == 1 and i == 2),
                                                 skip_group_check=True)
                return last

            E.wait_ge(dve_done, E.at(("conv", 1, 1)))
            for kk in range(2):
                E.wait_ge(pool_done, E.at(("g lo first", kk)))
                E.wait_ge(dve_done, E.at(("up lo", kk)))
                down(kk, kk == 0, False).then_inc(pe_done, 1)
                E.counted(("dn mm first", kk))
            with E.loop("down", DR):
                for u in range(2):
                    E.wait_ge(dve_done, E.at(("dn lo", u), back=1))
                    down(u, False, False).then_inc(pe_done, 1)
                    E.counted(("dn mm", u))
            E.wait_ge(dve_done, E.at("dn lo last"))
            H, L = dn_view(m.wh, 0), dn_view(m.wl, 0)
            for t in range(TT):
                tt = slice(P * t, P * t + P)
                for n in range(2):
                    cc = slice(T * n, T * n + T)
                    for k in range(2):
                        for i, (g, w) in enumerate(((m.gH, H), (m.gL, H), (m.gH, L))):
                            last = pe.matmul(PS[:, 2 * t + n, :], g[:, 0, k, tt], w[:, k, cc], start=False,
                                             stop=(k == 1 and i == 2), skip_group_check=True)
                last.then_inc(pe_done, 1)
                E.counted(("dn mm last", t))

        @block.scalar
        def _(act):
            E = Engine(steps, "act", act, done)
            norm_scalar(E, m, "n3")
            for s in range(2):
                act.wait_ge(w_loaded[s], 32)
                split_hi(E, m, s, ("up hi first", s))
            E.wait_ge(act_done, E.so_far())
            E.wait_ge(dve_done, E.at(("fcol", 0)))
            norm_split_scalar(E, m, "n3", lambda j: m.fcol[:, 0, j:j + 1])
            with E.loop("up", UP) as i:
                for u in range(2):
                    E.wait_ge(act_done, E.so_far())
                    E.wait_ge(dve_done, E.at(("G", u), back=1))
                    E.wait_ge(act_done, E.so_far())
                    E.wait_ge(dve_done, E.at(("conv", u, 0)))
                    act.activation(m.gel[:, u, :], m.cgu[:, u, 0, :], ACT.Gelu_apprx_tanh).then_inc(act_done, 1)
                    E.counted(("gelu", u))
                    act.wait_ge(w_loaded[u], i * 32 + 64)
                    split_hi(E, m, u, ("up hi", u), ("up mm", u, 1))

            def g_hi(s, k, step):
                act.activation(m.gH[:, s, :, :], m.G[:, bass.ds(k, 2), :], ACT.Copy).then_inc(act_done, 1)
                E.counted(step)

            E.wait_ge(act_done, E.so_far())
            E.wait_ge(dve_done, E.at(("G", 1)))
            for kk in range(2, 4):
                s = kk % 2
                act.wait_ge(w_loaded[s], 32 * (UP + kk // 2 + 1))
                split_hi(E, m, s, ("dn hi first", kk), ("dn mm first", s))
                g_hi(s, 2 * kk, ("g hi first", kk))
            with E.loop("down", DR - 1) as i:
                for u in range(2):
                    k = act.snap(i * 4 + 8 + 2 * u)
                    act.wait_ge(w_loaded[u], i * 32 + 32 * (UP + 3))
                    split_hi(E, m, u, ("dn hi", u), ("dn mm", u))
                    g_hi(u, k, ("g hi", u))
            act.wait_ge(w_loaded[0], 32 * (UP + DN // 2 + 1))
            split_hi(E, m, 0, "dn hi last", ("dn mm", 0))
            g_hi(0, 2 * (DN - 1), "g hi last")
            mix_out_scalar(E, m, "n4", lambda t: [("dn mm last", t)])

        @block.vector
        def _(dve):
            E = Engine(steps, "dve", dve, done)
            norm_vector(E, m, "n3")
            for b, n in ((0, FROWS), (1, FROWS2)):
                E.wait_ge(dve_done, E.so_far())
                E.wait_ge(pe_done, E.at(("turn frow", b)))
                dve.tensor_copy(m.fcol[:, b, 0:n], PS[:, b, 0:n]).then_inc(dve_done, 1)
                E.counted(("fcol", b))
            for s in range(2):
                split_lo(E, m, s, ("up lo first", s), ("up hi first", s))
            norm_split_vector(E, m, "n3", lambda j: m.fcol[:, 0, j:j + 1])
            with E.loop("up", UP) as i:
                for u in range(2):
                    for h in range(2):
                        j = FT * h + u
                        tap = [m.fcol[:, 0, bass.ds(i * 2 + FROW["conv0"] + j, 1)],
                               m.fcol[:, 1, bass.ds(i * 2 + FROW2["conv1"] + j, 1)],
                               m.fcol[:, 1, bass.ds(i * 2 + FROW2["conv2"] + j, 1)]]
                        bias = m.fcol[:, 0, bass.ds(i * 2 + FROW["bias"] + j, 1)]
                        z, c = PS[:, 2 * u + h, :], m.cgu[:, u, h, :]
                        E.wait_ge(dve_done, E.so_far())
                        E.wait_ge(pe_done, E.at(("up mm", u, h)))
                        dve.tensor_scalar(c, z, tap[2], bias, ALU.mult, ALU.add).then_inc(dve_done, 1)
                        E.counted(("tap2", u, h))
                        E.wait_ge(dve_done, E.so_far())
                        dve.scalar_tensor_tensor(c[:, 1:T], z[:, 0:T - 1], tap[1], c[:, 1:T], ALU.mult,
                                                 ALU.add).then_inc(dve_done, 1)
                        E.counted(("tap1", u, h))
                        E.wait_ge(dve_done, E.so_far())
                        dve.scalar_tensor_tensor(c[:, 2:T], z[:, 0:T - 2], tap[0], c[:, 2:T], ALU.mult,
                                                 ALU.add).then_inc(dve_done, 1)
                        E.counted(("conv", u, h))
                    E.wait_ge(dve_done, E.so_far())
                    E.wait_ge(act_done, E.at(("gelu", u)))
                    dve.tensor_tensor(m.G[:, bass.ds(i * 2 + u, 1), :], m.gel[:, u:u + 1, :], m.cgu[:, u, 1:2, :],
                                      ALU.mult).then_inc(dve_done, 1)
                    E.counted(("G", u))
                    split_lo(E, m, u, ("up lo", u), ("up hi", u))

            def g_lo(s, k, step, hi):
                E.wait_ge(dve_done, E.so_far())
                E.wait_ge(act_done, E.at(hi))
                dve.tensor_tensor(m.gL[:, s, :, :], m.G[:, bass.ds(k, 2), :], m.gH[:, s, :, :].bitcast(F32),
                                  ALU.subtract).then_inc(dve_done, 1)
                E.counted(step)

            for kk in range(2, 4):
                g_lo(kk % 2, 2 * kk, ("g lo first", kk), ("g hi first", kk))
                split_lo(E, m, kk % 2, ("dn lo first", kk), ("dn hi first", kk))
            with E.loop("down", DR - 1) as i:
                for u in range(2):
                    k = i * 4 + 8 + 2 * u
                    g_lo(u, k, ("g lo", u), ("g hi", u))
                    split_lo(E, m, u, ("dn lo", u), ("dn hi", u))
            g_lo(0, 2 * (DN - 1), "g lo last", "g hi last")
            split_lo(E, m, 0, "dn lo last", "dn hi last")
            dve.wait_ge(gain_loaded, 16)
            mix_out_vector(E, m, "n4")


_WIDTHS = (("gq", 256), ("gk", 256), ("gv", 512), ("ga", 16), ("gz", 512), ("bq", 512), ("bk", 512), ("bv", 512),
           ("iq", 512), ("ik", 64), ("iw", 8), ("bz", 512), ("cq", 512), ("ck", 512), ("cv", 512), ("cz", 512),
           ("gate", 3 * D))
COL, N_IN = numbered(_WIDTHS)
LROW, LROWS = numbered((("norm", KT), ("gla", 1), ("dsa_q", 1), ("dsa_k", 1), ("diff_q", 1), ("diff_k", 1)))
NH = 4
IH = 8
CH = T // 64
RANK = 16
TAU = 16.0
TOP = 128
LAMBDA = tuple(0.8 - 0.6 * 2.718281828459045 ** (-0.3 * l) for l in range(2))
TAKEN, HIDDEN, MASK = -3e38, -1e38, 1e30


def lay_out_layers(nc, m):
    at = [m.arena]

    def take(name, shape, dt=F32, over=None):
        n = 4
        for s in shape[1:]:
            n *= s
        start = at[0] if over is None else over
        t = nc.alloc_sbuf_tensor_at(name, shape, dt, offset=start)
        if over is None:
            at[0] += (n + 31) // 32 * 32
            assert at[0] <= nc.sbuf_usable_end // 32 * 32, (name, at[0])
        return t

    KB = 1024
    mg = at[0]
    m.mg = take("merged", [P, KT, T])
    m.gq = take("gla_q", [P, 2, T], over=mg)
    m.gk = take("gla_k_tokens", [P, TT, 256], over=mg + 4 * KB)
    m.la = take("gla_log_decay", [P, TT, 256], over=mg + 8 * KB)
    m.gt = take("gla_tmp", [P, TT, 256], over=mg + 12 * KB)
    yh = at[0]
    m.yH = take("y_hi", [P, NH, T], F32R)
    m.yL = take("y_lo", [P, NH, T], F32R)
    m.gv = take("gla_v_tokens", [P, TT, BR], over=yh)
    m.St = take("gla_states", [P, 2, CH, P], over=yh + 8 * KB)
    q = at[0]
    m.Q = take("q_feats", [P, NH, T])
    m.K = take("k_feats", [P, NH, T])
    m.V = take("v_toks", [P, TT, BR])
    m.Z = take("z_feats", [P, NH, T])
    m.ikf = take("ik_feats", [P, T], over=q + 8 * KB)
    m.lw = take("lowrank_iw", [RANK + IH, T], over=q + 24 * KB)
    o = at[0]
    m.O = take("branch_out", [P, NH, T])
    m.sq3 = take("squares3", [P, NH, T])
    m.xn3 = take("x_normed3", [P, TT, D], over=o)
    p = at[0]
    m.Px = take("probs", [P, 2, 2, T])
    m.gz = take("gla_z", [P, NH, T], over=p)
    m.relu = take("index_relu", [P, 4, T], over=p)
    pt = at[0]
    m.PT = take("probs_t", [P, 2, T])
    m.rn3 = take("norm_rows3", [16, T], over=pt)
    m.wa2 = take("gla_wa2", [RANK, 256], over=pt)
    m.ba = take("gla_ba", [1, 256], over=pt + KB)
    m.lam_in = take("lambda_in", [P, 4, 64], over=pt + 2 * KB)
    m.lamt = take("lambda_tmp", [P, 2, 64], over=pt + 3 * KB)
    m.lrow = take("layer_rows", [LROWS, P], over=pt + 7 * KB // 2)
    m.sc = take("index_scores", [P, P * sum(range(2, TT + 1))])
    m.later = m.bd
    m.lcol = take("layer_cols", [P, 16])
    m.lam = take("lambda", [P, 8])
    m.lamc = take("lambda_init", [P, 2, 2])
    m.lc = take("lambda_const", [P, 2])
    m.iw = take("index_weights", [P, TT, IH])
    m.dec = take("gla_decay", [P, 2, CH])
    m.top8 = take("top8", [P, 8])
    m.st = take("softmax_stats", [P, 2, 8])
    m.half = take("first_half", [P, P])
    m.neg = take("mask_values", [P, 64])


def layers(nc, m, A, steps, done, sems, clear):
    pe_done, act_done, dve_done, pool_done = (done[n] for n in ("pe", "act", "dve", "pool"))
    lay_out_layers(nc, m)
    PS, m.xn = m.PS, m.xn3
    w_loaded = sems("w_loaded0"), sems("w_loaded1")
    rows_loaded, small_loaded = sems("rows_loaded"), sems("small_loaded")

    panels = []

    def add(name, pieces, kt=KT, tokens=False):
        panels.append(Panel(name, pieces, kt, tokens))
        return len(panels) - 1

    def full(name, n, tokens=False):
        return [add(name, [("w_in_2", COL[name] + PW * i, PW)], tokens=tokens) for i in range(n)]

    add("ik", [("w_in_2", COL["ik"], 64)] * 2)
    add("ga iw", [("w_in_2", COL["ga"], RANK), ("w_in_2", COL["iw"], IH)])
    iq = full("iq", 2)
    gk, gv, gq, gz = full("gk", 1, True), full("gv", 2, True), full("gq", 1), full("gz", 2)
    cq, ck, cv, cz = full("cq", 2), full("ck", 2), full("cv", 2, True), full("cz", 2)

    def merge(b):
        first = len(panels)
        for r in range(4):
            add("gate", [("w_in_2", COL["gate"] + D * b + PW * r, PW)])
            add("br", [(b, PW * r, PW)], kt=4)
        return first

    mergeA = merge(0)
    bq, bk, bv, bz = full("bq", 2), full("bk", 2), full("bv", 2, True), full("bz", 2)
    mergeC = merge(2)
    mergeB = merge(1)
    outs = [add("out", [("w_out_2", PW * r, PW)], tokens=True) for r in range(4)]
    NP = len(panels)

    def view(buf, p):
        a = panels[p]
        return buf[:, p % 2, 0:a.kt * a.w].rearrange("p (k n) -> p k n", k=a.kt)

    def tiles(p):
        a = panels[p]
        return [min(P, a.w - P * i) for i in range((a.w + P - 1) // P)]

    def bank(p, i):
        if mergeA <= p < mergeA + 8 or mergeC <= p < mergeC + 8:
            return i
        return 2 * (p % 2) + i

    def logit_bank(u, c):
        return 4 + c if u % 2 == 0 else 2 + c

    tokdst = {}
    for i in range(2):
        tokdst[gv[i]], tokdst[cv[i]], tokdst[bv[i]] = (m.gv, i), (m.V, i), (m.V, i)
    tokdst[gk[0]] = (m.gk, 0)
    featdst = {}
    for i in range(2):
        for ps, dst, scale, fn in ((iq, m.Q, 1.0, ACT.Copy), (gz, m.gz, 1.0, ACT.Silu), (cq, m.Q, 1.0, ACT.Copy),
                                   (ck, m.K, 1.0, ACT.Copy), (cz, m.Z, 1.0, ACT.Silu), (bq, m.Q, 1.0, ACT.Copy),
                                   (bk, m.K, 1.0, ACT.Copy), (bz, m.Z, 1.0, ACT.Silu)):
            for t in range(2):
                featdst[ps[i], t] = (dst[:, 2 * i + t, :], scale, fn)
    for t in range(2):
        featdst[gq[0], t] = (m.gq[:, t, :], 64 ** -0.5, ACT.Copy)
    featdst[0, 0] = (m.ikf[:, :], 1.0, ACT.Copy)
    featdst[1, 0] = (m.lw[:, :], 1.0, ACT.Copy)
    by_dve = set(cq + ck + bq + bk)

    def lname(col):
        return m.lcol[:, LROW[col]:LROW[col] + 1]

    def score(i):
        at = P * sum(range(2, i + 1))
        return m.sc[:, at:at + P * (i + 1)]

    units = [(h, i) for h in range(NH) for i in (3, 2, 1, 0)]
    NU = len(units)
    idx = [(i, h) for i in range(1, TT) for h in range(IH)]

    with nc.Block() as block:

        @block.gpsimd
        def _(pool):
            E = Engine(steps, "pool", pool, done)

            def step(ins, name):
                ins.then_inc(pool_done, 1)
                E.counted(name)
                E.wait_ge(pool_done, E.at(name))

            step(pool.affine_select(out=m.later[:, :], in_=m.later[:, :], compare_op=ALU.is_gt, fill=0.0, base=0,
                                    pattern=[[-1, P]], channel_multiplier=1), "later 3")
            for l in range(2):
                step(pool.memset(m.lamc[:, l, 0:1], LAMBDA[l]), ("lambda 0", l))
                step(pool.memset(m.lamc[:, l, 1:2], 1.0 - LAMBDA[l]), ("lambda 1", l))
            step(pool.memset(m.half[:, :], 0.0), "half 0")
            step(pool.memset(m.half[:, 0:64], 1.0), "half 1")
            step(pool.memset(m.neg[:, :], -MASK), "neg")
    clear()

    with nc.Fori(0, 2) as L:
        one_layer = bass.ds(L, 1)
        with nc.Block() as block:

            @block.sync
            def _(sp):
                E = Engine(steps, "sp", sp, done)
                rows = [(LROW["norm"], KT, 0, A["norm_g_2"][one_layer, :].rearrange("l (a b) -> (l a) b", b=P)),
                        (LROW["gla"], 1, 0, A["gla_norm_g_2"][one_layer, :]),
                        (LROW["dsa_q"], 1, 0, A["dsa_qn_g_2"][one_layer, :]), (LROW["dsa_k"], 1, 0,
                         A["dsa_kn_g_2"][one_layer, :])]
                for c in (0, 64):
                    rows += [(LROW["diff_q"], 1, c, A["diff_qn_g_2"][one_layer, :]),
                             (LROW["diff_k"], 1, c, A["diff_kn_g_2"][one_layer, :])]
                assert len(rows) == 8
                for r, n, c, src in rows:
                    sp.dma_start(m.lrow[r:r + n, c:c + src.shape[1]], src).then_inc(rows_loaded, 16)
                for p in range(NP):
                    if p >= 2:
                        E.wait_ge(dve_done, E.at(("Lw lo", p - 2)))
                    v, at, q = view(m.raw, p), 0, w_loaded[p % 2]
                    pieces, kt = panels[p].pieces, panels[p].kt
                    ks = kt if len(pieces) == 2 else kt // 2
                    for name, c, w in pieces:
                        for k in range(0, kt, ks):
                            if name in (0, 1, 2):
                                s = A["w_br_2"][one_layer, name, P * k:P * (k + ks), c:c + w]
                            else:
                                s = A[name][one_layer, P * k:P * (k + ks), c:c + w]
                            sp.dma_start(v[:, k:k + ks, at:at + w],
                                         s.rearrange("l (k q) n -> q (l k) n", q=P)).then_inc(q, 16)
                        at += w
                    if p == 1:
                        for i, n in enumerate(("diff_lq1_2", "diff_lk1_2", "diff_lq2_2", "diff_lk2_2")):
                            sp.dma_start(m.lam_in[:, i, :],
                                         A[n][one_layer, :].partition_broadcast(P)).then_inc(small_loaded, 16)
                        sp.dma_start(m.wa2[:, :],
                                     A["gla_wa2_2"][one_layer, :, :].rearrange("l a b -> (l a) b")).then_inc(small_loaded, 16)
                        sp.dma_start(m.ba[:, :], A["gla_ba_2"][one_layer, :]).then_inc(small_loaded, 16)

            @block.tensor
            def _(pe):
                E = Engine(steps, "pe", pe, done)
                banks = Banks(E)

                def start(step, b, reader):
                    banks.use(b, reader)
                    m.bank[step] = b
                    return PS[:, b, :]

                def panel(p, only=None):
                    a = panels[p]
                    E.wait_ge(dve_done, E.at(("Lw lo", p)))
                    H, W = view(m.wh, p), view(m.wl, p)
                    for i in range(2 if a.tokens else len(tiles(p))):
                        if only is not None and i != only:
                            continue
                        b = bank(p, i)
                        banks.use(b, ("Levac", p, i))
                        if p == outs[0] and i == 0:
                            banks.use(bank(p, 1), ("Levac", p, 1))
                            for k in range(KT):
                                E.wait_ge(dve_done, E.at(("merged lo", k)))
                                for t in range(TT):
                                    tt = slice(P * t, P * t + P)
                                    last = project(E, m, (lambda k: m.hH[:, k, tt], lambda k: m.hL[:, k, tt]),
                                                   (lambda k: H[:, k, :], lambda k: W[:, k, :]),
                                                   PS[:, bank(p, t // 2), PW * (t % 2):PW * (t % 2) + PW], ks=[k],
                                                   opens=t % 2 == 0)
                                    if k == KT - 1 and t % 2:
                                        last.then_inc(pe_done, 1)
                                        E.counted(("Lpanel", p, t // 2))
                            return
                        if a.tokens:
                            for t in (2 * i, 2 * i + 1):
                                tt = slice(P * t, P * t + P)
                                last = project(E, m, (lambda k: m.hH[:, k, tt], lambda k: m.hL[:, k, tt]),
                                               (lambda k: H[:, k, :], lambda k: W[:, k, :]),
                                               PS[:, b, PW * (t % 2):PW * (t % 2) + PW])
                        else:
                            n = tiles(p)[i]
                            c = slice(P * i, P * i + n)
                            x = (m.yH, m.yL) if a.name == "br" else (m.hH, m.hL)
                            for k in range(a.kt):
                                if p == 0:
                                    E.wait_ge(dve_done, E.at(("l1", "lo", k)))
                                last = project(E, m, (lambda k: H[:, k, c], lambda k: W[:, k, c]),
                                               (lambda k: x[0][:, k, :], lambda k: x[1][:, k, :]), PS[0:n, b, :],
                                               kt=a.kt, ks=[k])
                        last.then_inc(pe_done, 1)
                        E.counted(("Lpanel", p, i))

                def index_dots(i):
                    vis = P * (i + 1)
                    for h in range(IH):
                        n = idx.index((i, h))
                        o = start(("dots", n), 4 + n % 4, ("relu", n))
                        r = slice(64 * (h % 2), 64 * (h % 2) + 64)
                        pe.matmul(o[:, 0:vis], m.Q[r, h // 2, P * i:P * i + P], m.ikf[r, 0:vis], start=True,
                                  stop=True).then_inc(pe_done, 1)
                        E.counted(("dots", n))

                def squares(step, reader, tag, ind, b, n0, n1, begin, end):
                    o = start(step, b, reader) if begin else PS[:, b, :]
                    rows = KT if ind is m.indw else 16
                    for n in range(n0, n1):
                        E.wait_ge(act_done, E.at((tag, n)))
                        last = pe.matmul(o[0:rows, :], ind[:, n, 0:rows], m.sq3[:, n % 4, :], start=(begin and n == n0),
                                         stop=(end and n == n1 - 1))
                    last.then_inc(pe_done, 1)
                    E.counted(step)

                def spread(tag, indT, n0, n1, reader, bk=(4, 5, 6)):
                    for n in range(n0, n1):
                        o = start((tag, n), bk[n % len(bk)], (reader, n))
                        pe.matmul(o, indT[:, n, :], m.rnS[:, :], start=True, stop=True).then_inc(pe_done, 1)
                        E.counted((tag, n))

                def mask(o, vis, r):
                    return pe.matmul(o[:, vis - 64:vis], m.half[r, :], m.neg[r, :], start=False, stop=True,
                                     skip_group_check=True)

                def diff_logits(u):
                    h, i = units[u]
                    vis = P * (i + 1)
                    for c in range(2):
                        r = slice(64 * c, 64 * c + 64)
                        o = start(("dlogits", u, c), logit_bank(u, c), ("dexp", u, c))
                        pe.matmul(o[:, 0:vis], m.Q[r, h, P * i:P * i + P], m.K[r, h, 0:vis], start=True, stop=False,
                                  skip_group_check=True)
                        last = mask(o, vis, r)
                    last.then_inc(pe_done, 1)
                    E.counted(("dlogits", u))

                def dsa_logits(u):
                    h, i = units[u]
                    vis = P * (i + 1)
                    o = start(("slogits", u), 4 + u % 2, ("sread", u))
                    last = pe.matmul(o[:, 0:vis], m.Q[:, h, P * i:P * i + P], m.K[:, h, 0:vis], start=True, stop=(i > 0),
                                     skip_group_check=True)
                    if i == 0:
                        last = mask(o, vis, slice(0, P))
                    last.then_inc(pe_done, 1)
                    E.counted(("slogits", u))

                def turn_probs(u, pf):
                    h, i = units[u]
                    E.wait_ge(dve_done, E.at((pf + "normed", u)))
                    blocks = [m.Px[:, u % 2, 1 if pf == "s" else 0, P * k:P * k + P] for k in range(i + 1)]
                    turn(E, m, banks, (pf + "pt mm", u), 6, (pf + "pt", u), blocks)

                def values(u, pf):
                    h, i = units[u]
                    E.wait_ge(act_done, E.at((pf + "pt", u)))
                    o = start((pf + "pv", u), 7, (pf + "out", u))
                    for k in range(i + 1):
                        last = pe.matmul(o[:, 0:P], m.V[:, k, P * h:P * h + P], m.PT[:, u % 2, P * k:P * k + P],
                                         start=(k == 0), stop=(k == i))
                    last.then_inc(pe_done, 1)
                    E.counted((pf + "pv", u))

                E.wait_ge(dve_done, E.at(("l1", "xn", 1)))
                E.wait_ge(act_done, E.at(("l1", "xn", 3)))
                for j in range(KT):
                    if j == 4:
                        pe.wait_ge(rows_loaded, 16 * 8)
                        turn(E, m, banks, "turn lrow", 0, "lcol", [m.lrow[:, :]], rows=LROWS)
                    turn(E, m, banks, ("l1", "turn", j), 4 + j % 4, ("l1", "lo", j),
                         [m.xn[:, t, P * j:P * j + P] for t in range(TT)])
                panel(0)
                panel(1)
                panel(2)
                E.wait_ge(act_done, E.at(("Levac", 1, 0)))
                turn(E, m, banks, "turn iw", 6, "iw", [m.lw[:, P * t:P * t + P] for t in range(TT)], rows=RANK + IH)
                pe.wait_ge(small_loaded, 16 * 6)
                for g in range(2):
                    o = start(("z", g), 4 + g, ("la", g))
                    for q in range(2):
                        t = 2 * g + q
                        oo = o[:, 256 * q:256 * q + 256]
                        pe.matmul(oo, m.lw[0:RANK, P * t:P * t + P], m.wa2[:, :], start=True, stop=False)
                        last = pe.matmul(oo, m.indwT[0:1, 0, :].bitcast(F32), m.ba[:, :], start=False, stop=True)
                    last.then_inc(pe_done, 1)
                    E.counted(("z", g))
                panel(3)
                for i in range(1, TT):
                    panel(3 + i)
                    if i == 1:
                        E.wait_ge(act_done, E.at(("Levac", 3, 1)))
                    index_dots(i)
                E.wait_ge(dve_done, E.at(("la", 1)))
                for g in range(2):
                    o = start(("later", g), 4 + g, ("kdec", g))
                    last = pe.matmul(o, m.later[:, :], m.la[:, 2 * g:2 * g + 2, :].rearrange("p a b -> p (a b)"),
                                     start=True, stop=True)
                    last.then_inc(pe_done, 1)
                    E.counted(("later", g))
                o = start("total", 6, "decay")
                for f in range(2):
                    for t in range(TT):
                        last = pe.matmul(o[:, CH * f + 2 * t:CH * f + 2 * t + 2], m.la[:, t, P * f:P * f + P],
                                         m.indh[:, 0, 0:2], start=True, stop=True)
                last.then_inc(pe_done, 1)
                E.counted("total")
                panel(7)
                E.wait_ge(dve_done, E.at(("kd", 1)))
                for f in range(2):
                    for g in range(2):
                        o = start(("u", f, g), 4 + 2 * f + g, ("S", f, CH - 2 + g))
                        r = slice(64 * g, 64 * g + 64)
                        for t in range(TT):
                            for e in range(2):
                                h = 2 * f + e
                                last = pe.matmul(o[64 * e:64 * e + 64, P * t:P * t + P], m.gk[r, t, 64 * h:64 * h + 64],
                                                 m.gv[r, t, P * h:P * h + P], start=True, stop=True)
                        last.then_inc(pe_done, 1)
                        E.counted(("u", f, g))
                panel(8)
                panel(9)
                panel(10)
                E.wait_ge(act_done, E.at(("Levac", 7, 1)))
                for h in range(NH):
                    o = start(("o", h), 4 + h, ("gla sq", h))
                    E.wait_ge(dve_done, E.at(("S", h // 2, CH - 1)))
                    r = slice(64 * (h % 2), 64 * (h % 2) + 64)
                    for c in range(CH):
                        cc = slice(64 * c, 64 * c + 64)
                        last = pe.matmul(o[:, cc], m.St[r, h // 2, c, :], m.gq[r, h // 2, cc], start=True, stop=True)
                    last.then_inc(pe_done, 1)
                    E.counted(("o", h))
                panel(11)
                squares("gla ss", "gla sd", "gla sq", m.indw, 7, 0, 4, True, True)
                panel(12)
                E.wait_ge(dve_done, E.at("gla rn"))
                spread("gla spread", m.indwT, 0, 4, "gla y1")
                panel(13)
                squares("diff ss q", "diff sd", "diff sq", m.indh, 7, 0, 4, True, False)
                panel(14)
                squares("diff ss", "diff sd", "diff sq", m.indh, 7, 4, 8, False, True)
                panel(15)
                E.wait_ge(dve_done, E.at("diff rn"))
                spread("diff spread", m.indhT, 0, 4, "diff n")
                panel(16)
                spread("diff spread", m.indhT, 4, 8, "diff n")
                panel(17)

                E.wait_ge(dve_done, E.at(("diff n", 7)))
                E.wait_ge(act_done, E.at(("Levac", cv[1], 1)))
                diff_logits(0)
                diff_logits(1)
                panel(mergeA, only=0)
                for u in range(NU):
                    turn_probs(u, "d")
                    if u + 2 < NU:
                        diff_logits(u + 2)
                    if u + 1 < NU:
                        if u + 1 == 2:
                            E.wait_ge(dve_done, E.at(("gla lo", NH - 1)))
                        panel(mergeA + (u + 1) // 2, only=(u + 1) % 2)
                    values(u, "d")
                panel(26)
                panel(27)
                squares("dout ss", "dout sd", "dout sq", m.indw, 4, 0, 4, True, True)
                panel(28)
                squares("dsa ss q", "dsa sd", "dsa sq", m.indw, 7, 0, 4, True, False)
                E.wait_ge(dve_done, E.at("dout rn"))
                spread("dout spread", m.indwT, 0, 4, "dout y1")
                panel(29)
                panel(30)
                squares("dsa ss", "dsa sd", "dsa sq", m.indw, 7, 4, 8, False, True)
                panel(31)
                E.wait_ge(dve_done, E.at("dsa rn"))
                spread("dsa spread", m.indwT, 0, 4, "dsa n")
                panel(32)
                spread("dsa spread", m.indwT, 4, 8, "dsa n")
                panel(33)

                E.wait_ge(dve_done, E.at(("dsa n", 7)))
                E.wait_ge(act_done, E.at(("Levac", bv[1], 1)))
                dsa_logits(0)
                dsa_logits(1)
                panel(mergeC, only=0)
                for u in range(NU):
                    turn_probs(u, "s")
                    if u + 2 < NU:
                        dsa_logits(u + 2)
                    if u + 1 < NU:
                        if u + 1 == 2:
                            E.wait_ge(dve_done, E.at(("diff lo", NH - 1)))
                        panel(mergeC + (u + 1) // 2, only=(u + 1) % 2)
                    values(u, "s")
                panel(mergeB)
                E.wait_ge(dve_done, E.at(("dsa lo", NH - 1)))
                for p in range(mergeB + 1, mergeB + 8):
                    panel(p)
                for p in outs:
                    panel(p)

            @block.scalar
            def _(act):
                E = Engine(steps, "act", act, done)

                def high(p):
                    if p < NP:
                        act.wait_ge(w_loaded[p % 2], 32 * (p // 2 + 1))
                        if p >= 2:
                            E.wait_ge(act_done, E.so_far())
                            E.wait_ge(pe_done, E.at(("Lpanel", p - 2, 0 if len(tiles(p - 2)) == 1 else 1)))
                        n = panels[p].kt * panels[p].w
                        act.activation(m.wh[:, p % 2, 0:n], m.raw[:, p % 2, 0:n], ACT.Copy).then_inc(act_done, 1)
                        E.counted(("Lw hi", p))

                def evac(p, i):
                    if p in by_dve or i >= (2 if panels[p].tokens else len(tiles(p))):
                        return
                    b = bank(p, i)
                    E.wait_ge(act_done, E.so_far())
                    E.wait_ge(pe_done, E.at(("Lpanel", p, i)))
                    if panels[p].tokens:
                        dst, q = tokdst[p]
                        ins = act.activation(dst[:, 2 * i:2 * i + 2, PW * q:PW * q + PW],
                                             PS[:, b, :].rearrange("p (a b) -> p a b", a=2), ACT.Copy)
                    else:
                        dst, scale, fn = featdst[p, i]
                        ins = act.activation(dst, PS[0:tiles(p)[i], b, :], fn, scale=scale)
                    ins.then_inc(act_done, 1)
                    E.counted(("Levac", p, i))

                def relus(i):
                    vis = P * (i + 1)
                    for h in range(IH):
                        n = idx.index((i, h))
                        E.wait_ge(act_done, E.so_far())
                        E.wait_ge(pe_done, E.at(("dots", n)))
                        if n > 3:
                            E.wait_ge(act_done, E.so_far())
                            E.wait_ge(dve_done, E.at(("score", n - 4)))
                        act.activation(m.relu[:, n % 4, 0:vis], PS[:, 4 + n % 4, 0:vis], ACT.Relu).then_inc(act_done, 1)
                        E.counted(("relu", n))

                def square(tag, n, src, *need):
                    E.wait_ge(act_done, E.so_far())
                    for before in need:
                        E.wait_ge(*E.point(before))
                    act.activation(m.sq3[:, n % 4, :], src, ACT.Square).then_inc(act_done, 1)
                    E.counted((tag, n))

                def root(step, need, b, rows, scale):
                    E.wait_ge(act_done, E.so_far())
                    E.wait_ge(pe_done, E.at(need))
                    act.activation(m.rn3[0:rows, :], PS[0:rows, b, :], ACT.Sqrt, bias=m.eps[0:rows, 0:1],
                                   scale=scale).then_inc(act_done, 1)
                    E.counted(step)

                def exps(u, pf, comps, scale):
                    h, i = units[u]
                    vis = P * (i + 1)
                    E.wait_ge(act_done, E.so_far())
                    E.wait_ge(dve_done, E.at((pf + "max", u)))
                    if u > 1:
                        E.wait_ge(act_done, E.so_far())
                        E.wait_ge(pe_done, E.at((pf + "pt mm", u - 2)))
                    for c in comps:
                        if pf == "d":
                            src, dst = PS[:, logit_bank(u, c), 0:vis], m.Px[:, u % 2, c, 0:vis]
                        elif i == 0:
                            src, dst = PS[:, 4 + u % 2, 0:vis], m.Px[:, u % 2, 1, 0:vis]
                        else:
                            src, dst = m.Px[:, u % 2, 0, 0:vis], m.Px[:, u % 2, 1, 0:vis]
                        ins = act.activation(dst, src, ACT.Exp, bias=m.st[:, u % 2, 2 + c:3 + c], scale=scale,
                                             accum_out=m.st[:, u % 2, 4 + c:5 + c])
                        ins.then_inc(act_done, 1)
                        E.counted((pf + "exp", u, c))
                        if pf == "s" and i == 0:
                            steps.found["sread", u] = steps.found["sexp", u, 0]

                def probs_t(u, pf):
                    vis = P * (units[u][1] + 1)
                    E.wait_ge(act_done, E.so_far())
                    E.wait_ge(pe_done, E.at((pf + "pt mm", u)))
                    if u > 1:
                        E.wait_ge(act_done, E.so_far())
                        E.wait_ge(pe_done, E.at((pf + "pv", u - 2)))
                    act.activation(m.PT[:, u % 2, 0:vis], PS[:, 6, 0:vis], ACT.Copy).then_inc(act_done, 1)
                    E.counted((pf + "pt", u))

                def head_out(u, pf):
                    h, i = units[u]
                    E.wait_ge(act_done, E.so_far())
                    E.wait_ge(pe_done, E.at((pf + "pv", u)))
                    act.activation(m.O[:, h, P * i:P * i + P], PS[:, 7, 0:P], ACT.Copy).then_inc(act_done, 1)
                    E.counted((pf + "out", u))

                def gate(p, i):
                    E.wait_ge(act_done, E.so_far())
                    E.wait_ge(pe_done, E.at(("Lpanel", p, i)))
                    base = max(b for b in (mergeA, mergeB, mergeC) if b <= p)
                    r = (p - base) // 2
                    if r >= 2:
                        E.wait_ge(act_done, E.so_far())
                        E.wait_ge(dve_done, E.at(("gated", base, 2 * (r - 2) + i)))
                    act.activation(m.sq3[:, 2 * (r % 2) + i, :], PS[:, bank(p, i), :], ACT.Tanh,
                                   scale=0.5).then_inc(act_done, 1)
                    E.counted(("Levac", p, i))

                def branch_hi(tag, ready):
                    for h in range(NH):
                        E.wait_ge(act_done, E.so_far())
                        E.wait_ge(dve_done, E.at((ready, h)))
                        act.activation(m.yH[:, h, :], m.O[:, h, :], ACT.Copy).then_inc(act_done, 1)
                        E.counted((tag, h))

                def step(p):
                    evac(p, 0)
                    high(p + 2)
                    evac(p, 1)

                norm_scalar(E, m, "l1")
                high(0)
                high(1)
                E.wait_ge(act_done, E.so_far())
                E.wait_ge(dve_done, E.at("lcol"))
                norm_split_scalar(E, m, "l1", lambda j: m.lcol[:, j:j + 1])
                step(0)
                step(1)
                step(2)
                E.wait_ge(act_done, E.so_far())
                E.wait_ge(dve_done, E.at("lambda sums"))
                act.activation(m.lam[:, 2:4], m.lam[:, 0:2], ACT.Exp).then_inc(act_done, 1)
                E.counted("lambda exps")
                for g in range(2):
                    E.wait_ge(act_done, E.so_far())
                    E.wait_ge(pe_done, E.at(("z", g)))
                    act.activation(m.gt[:, 2 * g:2 * g + 2, :], PS[:, 4 + g, :].rearrange("p (a b) -> p a b", a=2),
                                   ACT.Abs).then_inc(act_done, 1)
                    E.counted(("z abs", g))
                E.wait_ge(act_done, E.so_far())
                act.activation(m.gt[:, :, :], m.gt[:, :, :], ACT.Exp, scale=-1.0).then_inc(act_done, 1)
                E.counted("z exp")
                E.wait_ge(act_done, E.so_far())
                act.activation(m.gt[:, :, :], m.gt[:, :, :], ACT.Ln, bias=m.eps[:, 1:2], scale=1.0).then_inc(act_done, 1)
                E.counted("z ln")
                step(3)
                for i in range(1, TT):
                    step(3 + i)
                    relus(i)
                for g in range(2):
                    E.wait_ge(act_done, E.so_far())
                    E.wait_ge(pe_done, E.at(("later", g)))
                    E.wait_ge(dve_done, E.at(("la", 1)))
                    act.activation(m.gt[:, 2 * g:2 * g + 2, :], PS[:, 4 + g, :].rearrange("p (a b) -> p a b", a=2),
                                   ACT.Exp, scale=1.0 / TAU).then_inc(act_done, 1)
                    E.counted(("kdec", g))
                E.wait_ge(act_done, E.so_far())
                E.wait_ge(pe_done, E.at("total"))
                act.activation(m.dec[:, :, :], PS[:, 6, 0:2 * CH].rearrange("p (a b) -> p a b", a=2), ACT.Exp,
                               scale=1.0 / TAU).then_inc(act_done, 1)
                E.counted("decay")
                step(7)
                E.wait_ge(act_done, E.so_far())
                E.wait_ge(dve_done, E.at(("score", len(idx) - 1)))
                step(8)
                step(9)
                step(10)
                for h in range(NH):
                    E.wait_ge(act_done, E.so_far())
                    E.wait_ge(pe_done, E.at(("o", h)))
                    act.activation(m.O[:, h, :], PS[:, 4 + h, :], ACT.Copy, scale=lname("gla")).then_inc(act_done, 1)
                    E.counted(("gla out", h))
                    square("gla sq", h, PS[:, 4 + h, :])
                step(11)
                root("gla sd", "gla ss", 7, KT, 1.0 / P)
                step(12)
                for n in range(4):
                    square("diff sq", n, m.Q[:, n, :], "gla ss", ("Levac", cq[n // 2], n % 2))
                step(13)
                for n in range(4):
                    square("diff sq", 4 + n, m.K[:, n, :], "diff ss q", ("Levac", ck[n // 2], n % 2))
                step(14)
                E.wait_ge(act_done, E.so_far())
                E.wait_ge(dve_done, E.at("gla spread done"))
                root("diff sd", "diff ss", 7, 16, 1.0 / 64)
                branch_hi("gla hi", "gla y")
                step(15)
                step(16)
                step(17)

                exps(0, "d", (0, 1), 64 ** -0.5)
                exps(1, "d", (0, 1), 64 ** -0.5)
                gate(mergeA, 0)
                for u in range(NU):
                    probs_t(u, "d")
                    if u + 2 < NU:
                        exps(u + 2, "d", (0, 1), 64 ** -0.5)
                    if u + 1 < NU:
                        p, i = mergeA + (u + 1) // 2, (u + 1) % 2
                        if panels[p].name == "gate":
                            gate(p, i)
                        if i:
                            high(p + 2)
                    head_out(u, "d")
                for h in range(NH):
                    square("dout sq", h, m.O[:, h, :], ("dout", NU - 1), "diff ss", ("gated", mergeA, 7))
                step(26)
                step(27)
                root("dout sd", "dout ss", 4, KT, 1.0 / P)
                for n in range(4):
                    square("dsa sq", n, m.Q[:, n, :], "dout ss", ("Levac", bq[n // 2], n % 2))
                step(28)
                branch_hi("diff hi", "diff y")
                step(29)
                for n in range(4):
                    square("dsa sq", 4 + n, m.K[:, n, :], "dsa ss q", ("Levac", bk[n // 2], n % 2))
                step(30)
                root("dsa sd", "dsa ss", 7, KT, 1.0 / P)
                step(31)
                E.wait_ge(act_done, E.so_far())
                E.wait_ge(dve_done, E.at(("diff y", NH - 1)))
                step(32)
                step(33)

                exps(0, "s", (0,), P ** -0.5)
                exps(1, "s", (0,), P ** -0.5)
                gate(mergeC, 0)
                for u in range(NU):
                    probs_t(u, "s")
                    if u + 2 < NU:
                        exps(u + 2, "s", (0,), P ** -0.5)
                    if u + 1 < NU:
                        p, i = mergeC + (u + 1) // 2, (u + 1) % 2
                        if panels[p].name == "gate":
                            gate(p, i)
                        if i:
                            high(p + 2)
                    head_out(u, "s")
                E.wait_ge(act_done, E.so_far())
                E.wait_ge(pe_done, E.at(("Lpanel", mergeC + 7, 1)))
                branch_hi("dsa hi", "dsa y")
                for p in range(mergeB, mergeB + 7):
                    if panels[p].name == "gate":
                        gate(p, 0)
                        gate(p, 1)
                    high(p + 2)
                for j in range(KT):
                    E.wait_ge(act_done, E.so_far())
                    E.wait_ge(dve_done, E.at(("gated", mergeB, j)))
                    act.activation(m.hH[:, j, :], m.mg[:, j, :], ACT.Copy).then_inc(act_done, 1)
                    E.counted(("merged hi", j))
                high(outs[1])
                high(outs[2])
                high(outs[3])

            @block.vector
            def _(dve):
                E = Engine(steps, "dve", dve, done)

                def low(p):
                    if p < NP:
                        n = panels[p].kt * panels[p].w
                        E.wait_ge(dve_done, E.so_far())
                        E.wait_ge(act_done, E.at(("Lw hi", p)))
                        dve.tensor_tensor(m.wl[:, p % 2, 0:n], m.raw[:, p % 2, 0:n],
                                          m.wh[:, p % 2, 0:n].bitcast(F32), ALU.subtract).then_inc(dve_done, 1)
                        E.counted(("Lw lo", p))

                def evac(p, i):
                    if p in by_dve:
                        E.wait_ge(dve_done, E.so_far())
                        E.wait_ge(pe_done, E.at(("Lpanel", p, i)))
                        if p == bq[0] and i == 0:
                            E.wait_ge(dve_done, E.so_far())
                            E.wait_ge(pe_done, E.at(("dlogits", NU - 1)))
                        dve.tensor_copy(featdst[p, i][0], PS[:, bank(p, i), :]).then_inc(dve_done, 1)
                        E.counted(("Levac", p, i))

                def step(p):
                    evac(p, 0)
                    low(p + 2)
                    evac(p, 1)

                def scores(i):
                    vis = P * (i + 1)
                    for h in range(IH):
                        n = idx.index((i, h))
                        r, w, s = m.relu[:, n % 4, 0:vis], m.iw[:, i, h:h + 1], score(i)
                        E.wait_ge(dve_done, E.so_far())
                        E.wait_ge(act_done, E.at(("relu", n)))
                        if h == 0:
                            ins = dve.tensor_scalar(s, r, w, None, ALU.mult)
                        else:
                            ins = dve.scalar_tensor_tensor(s, r, w, s, ALU.mult, ALU.add)
                        ins.then_inc(dve_done, 1)
                        E.counted(("score", n))
                    E.wait_ge(dve_done, E.so_far())
                    dve.memset(score(i)[0:64, vis - 64:vis], HIDDEN).then_inc(dve_done, 1)
                    E.counted(("hidden", i))

                tops = [(i, r) for i in range(1, TT) for r in range(TOP // 8)]

                def top(n0, n1):
                    for i, r in tops[n0:n1]:
                        s = score(i)
                        E.wait_ge(dve_done, E.so_far())
                        dve.max(m.top8[:, :], s).then_inc(dve_done, 1)
                        E.counted(("top", i, r))
                        E.wait_ge(dve_done, E.so_far())
                        dve.match_replace(s, m.top8[:, :], s, TAKEN).then_inc(dve_done, 1)
                        E.counted(("taken", i, r))

                def bias(i):
                    s = score(i)
                    E.wait_ge(dve_done, E.so_far())
                    dve.tensor_scalar(s, s, TAKEN, 1.0, ALU.is_equal, ALU.subtract).then_inc(dve_done, 1)
                    E.counted(("mask", i))
                    E.wait_ge(dve_done, E.so_far())
                    dve.tensor_scalar(s, s, MASK, None, ALU.mult).then_inc(dve_done, 1)
                    E.counted(("bias", i))

                def rows(step, need, n):
                    E.wait_ge(dve_done, E.so_far())
                    E.wait_ge(act_done, E.at(need))
                    dve.reciprocal(m.rn3[0:n, :], m.rn3[0:n, :]).then_inc(dve_done, 1)
                    E.counted((step, "whole"))
                    split_rows(E, m, m.rn3[0:n, :], step)

                def normed(tag, spread, n, bk=(4, 5, 6)):
                    x = (m.Q if n < 4 else m.K)[:, n % 4, :]
                    g = lname(("diff_" if tag == "diff n" else "dsa_") + ("q" if n < 4 else "k"))
                    E.wait_ge(dve_done, E.so_far())
                    E.wait_ge(pe_done, E.at((spread, n)))
                    dve.scalar_tensor_tensor(x, PS[:, bk[n % 3], :], g, x, ALU.mult, ALU.mult).then_inc(dve_done, 1)
                    E.counted((tag, n))

                def softmax_max(u, pf):
                    h, i = units[u]
                    vis, st = P * (i + 1), m.st[:, u % 2, :]
                    n, scale = (2, 64 ** -0.5) if pf == "d" else (1, P ** -0.5)
                    E.wait_ge(dve_done, E.so_far())
                    E.wait_ge(pe_done, E.at((pf + "logits", u)))
                    if pf == "d":
                        ins = dve.tensor_reduce(st[:, 0:2], PS[:, logit_bank(u, 0):logit_bank(u, 0) + 2, 0:vis], AX_X,
                                                ALU.max)
                    elif i == 0:
                        ins = dve.tensor_reduce(st[:, 0:1], PS[:, 4 + u % 2, 0:vis], AX_X, ALU.max)
                    else:
                        if u > 1:
                            E.wait_ge(dve_done, E.so_far())
                            E.wait_ge(act_done, E.at(("sexp", u - 2, 0)))
                        ins = dve.tensor_tensor_reduce(m.Px[:, u % 2, 0, 0:vis], PS[:, 4 + u % 2, 0:vis], score(i),
                                                       1.0, -3e38, ALU.add, ALU.max, st[:, 0:1])
                    ins.then_inc(dve_done, 1)
                    E.counted((pf + "rowmax", u))
                    if pf == "s" and i > 0:
                        steps.found["sread", u] = steps.found["srowmax", u]
                    E.wait_ge(dve_done, E.so_far())
                    dve.tensor_scalar(st[:, 2:2 + n], st[:, 0:n], -scale, None, ALU.mult).then_inc(dve_done, 1)
                    E.counted((pf + "max", u))

                def softmax_norm(u, pf):
                    vis, st = P * (units[u][1] + 1), m.st[:, u % 2, :]
                    n = 2 if pf == "d" else 1
                    E.wait_ge(dve_done, E.so_far())
                    E.wait_ge(act_done, E.at((pf + "exp", u, n - 1)))
                    dve.reciprocal(st[:, 6:6 + n], st[:, 4:4 + n]).then_inc(dve_done, 1)
                    E.counted((pf + "rsum", u))
                    E.wait_ge(dve_done, E.so_far())
                    p0, p1 = m.Px[:, u % 2, 0, 0:vis], m.Px[:, u % 2, 1, 0:vis]
                    if pf == "d":
                        dve.tensor_scalar(p1, p1, st[:, 7:8], m.lam[:, 5:6], ALU.mult, ALU.mult).then_inc(dve_done, 1)
                        E.counted(("weighed", u))
                        E.wait_ge(dve_done, E.so_far())
                        dve.scalar_tensor_tensor(p0, p0, st[:, 6:7], p1, ALU.mult, ALU.add).then_inc(dve_done, 1)
                    else:
                        dve.tensor_scalar(p1, p1, st[:, 6:7], None, ALU.mult).then_inc(dve_done, 1)
                    E.counted((pf + "normed", u))

                def gated(p, i):
                    base = max(b for b in (mergeA, mergeB, mergeC) if b <= p)
                    r = (p - base) // 2
                    s, g = m.sq3[:, 2 * (r % 2) + i, :], m.mg[:, 2 * r + i, :]
                    E.wait_ge(dve_done, E.so_far())
                    E.wait_ge(pe_done, E.at(("Lpanel", p, i)))
                    E.wait_ge(act_done, E.at(("Levac", p - 1, i)))
                    dve.scalar_tensor_tensor(s, s, 1.0, PS[:, bank(p, i), :], ALU.add, ALU.mult).then_inc(dve_done, 1)
                    E.counted(("Levac", p, i))
                    E.wait_ge(dve_done, E.so_far())
                    if base == mergeA:
                        ins = dve.tensor_scalar(g, s, 0.5, None, ALU.mult)
                    else:
                        ins = dve.scalar_tensor_tensor(g, s, 0.5, g, ALU.mult, ALU.add)
                    ins.then_inc(dve_done, 1)
                    E.counted(("gated", base, 2 * r + i))

                def branch_lo(tag, hi):
                    for h in range(NH):
                        E.wait_ge(dve_done, E.so_far())
                        E.wait_ge(act_done, E.at((hi, h)))
                        dve.tensor_tensor(m.yL[:, h, :], m.O[:, h, :], m.yH[:, h, :].bitcast(F32),
                                          ALU.subtract).then_inc(dve_done, 1)
                        E.counted((tag, h))

                norm_vector(E, m, "l1")
                low(0)
                E.wait_ge(dve_done, E.so_far())
                E.wait_ge(pe_done, E.at("turn lrow"))
                dve.tensor_copy(m.lcol[:, 0:LROWS], PS[:, 0, 0:LROWS]).then_inc(dve_done, 1)
                E.counted("lcol")
                low(1)
                norm_split_vector(E, m, "l1", lambda j: m.lcol[:, j:j + 1])
                dve.wait_ge(small_loaded, 16 * 6)
                v = m.lam_in[:, :, :].rearrange("p (a b) n -> p a b n", b=2)
                dve.tensor_tensor(m.lamt[:, :, :], v[:, :, 0, :], v[:, :, 1, :], ALU.mult).then_inc(dve_done, 1)
                E.counted("lambda products")
                E.wait_ge(dve_done, E.so_far())
                dve.tensor_reduce(m.lam[:, 0:2], m.lamt[:, :, :], AX_X, ALU.add).then_inc(dve_done, 1)
                E.counted("lambda sums")
                dve.tensor_copy(m.lc[:, :], m.lamc[:, one_layer, :].rearrange("p a b -> p (a b)")).then_inc(dve_done, 1)
                E.counted("lambda const")
                step(0)
                step(1)
                step(2)
                E.wait_ge(dve_done, E.so_far())
                E.wait_ge(pe_done, E.at("turn iw"))
                dve.tensor_scalar(m.iw[:, :, :],
                                  PS[:, 6, 0:TT * (RANK + IH)].rearrange("p (t n) -> p t n", t=TT)[:, :, RANK:],
                                  64 ** -0.5 * IH ** -0.5, None, ALU.mult).then_inc(dve_done, 1)
                E.counted("iw")
                E.wait_ge(dve_done, E.so_far())
                E.wait_ge(act_done, E.at("lambda exps"))
                dve.tensor_tensor(m.lam[:, 4:5], m.lam[:, 3:4], m.lam[:, 2:3], ALU.subtract).then_inc(dve_done, 1)
                E.counted("lambda diff")
                E.wait_ge(dve_done, E.so_far())
                dve.tensor_tensor(m.lam[:, 5:6], m.lam[:, 4:5], m.lc[:, 0:1], ALU.subtract).then_inc(dve_done, 1)
                E.counted("lambda")
                E.wait_ge(dve_done, E.so_far())
                E.wait_ge(act_done, E.at("z ln"))
                for g in range(2):
                    dve.scalar_tensor_tensor(m.la[:, 2 * g:2 * g + 2, :], PS[:, 4 + g, :].rearrange("p (a b) -> p a b", a=2),
                                             0.0, m.gt[:, 2 * g:2 * g + 2, :], ALU.min, ALU.subtract).then_inc(dve_done, 1)
                    E.counted(("la", g))
                step(3)
                for i in range(1, TT):
                    step(3 + i)
                    scores(i)
                E.wait_ge(dve_done, E.so_far())
                E.wait_ge(act_done, E.at(("Levac", gk[0], 1)))
                for g in range(2):
                    s = m.gk[:, 2 * g:2 * g + 2, :]
                    E.wait_ge(dve_done, E.so_far())
                    E.wait_ge(act_done, E.at(("kdec", g)))
                    dve.tensor_tensor(s, s, m.gt[:, 2 * g:2 * g + 2, :], ALU.mult).then_inc(dve_done, 1)
                    E.counted(("kd", g))
                step(7)
                E.wait_ge(dve_done, E.so_far())
                E.wait_ge(act_done, E.at("decay"))
                for c in range(CH):
                    for f in range(2):
                        u = PS[:, 4 + 2 * f + c % 2, P * (c // 2):P * (c // 2) + P]
                        E.wait_ge(dve_done, E.so_far())
                        E.wait_ge(pe_done, E.at(("u", f, c % 2)))
                        if c == 0:
                            ins = dve.tensor_copy(m.St[:, f, 0, :], u)
                        else:
                            ins = dve.scalar_tensor_tensor(m.St[:, f, c, :], m.St[:, f, c - 1, :], m.dec[:, f, c:c + 1], u,
                                                           ALU.mult, ALU.add)
                        ins.then_inc(dve_done, 1)
                        E.counted(("S", f, c))
                step(8)
                top(0, 3)
                step(9)
                top(3, 6)
                step(10)
                top(6, 9)
                step(11)
                rows("gla rn", "gla sd", KT)
                top(9, 11)
                evac(12, 0)
                evac(12, 1)
                for h in range(NH):
                    o = m.O[:, h, :]
                    E.wait_ge(dve_done, E.so_far())
                    E.wait_ge(pe_done, E.at(("gla spread", h)))
                    dve.tensor_tensor(o, PS[:, (4, 5, 6)[h % 3], :], o, ALU.mult).then_inc(dve_done, 1)
                    E.counted(("gla y1", h))
                    if h == NH - 1:
                        steps.found["gla spread done"] = steps.found["gla y1", h]
                    E.wait_ge(dve_done, E.so_far())
                    dve.tensor_tensor(o, o, m.gz[:, h, :], ALU.mult).then_inc(dve_done, 1)
                    E.counted(("gla y", h))
                low(14)
                top(11, 13)
                step(13)
                top(13, 15)
                step(14)
                rows("diff rn", "diff sd", 16)
                top(15, 17)
                branch_lo("gla lo", "gla hi")
                evac(15, 0)
                evac(15, 1)
                for n in range(4):
                    normed("diff n", "diff spread", n)
                low(17)
                top(17, 19)
                evac(16, 0)
                evac(16, 1)
                for n in range(4, 8):
                    normed("diff n", "diff spread", n)
                low(18)
                top(19, 21)
                step(17)
                top(21, 23)
                softmax_max(0, "d")
                softmax_norm(0, "d")
                softmax_max(1, "d")
                softmax_norm(1, "d")
                for u in range(1, NU):
                    p, i = mergeA + u // 2, u % 2
                    if u + 1 < NU:
                        softmax_max(u + 1, "d")
                        softmax_norm(u + 1, "d")
                    top(22 + u, 23 + u)
                    if panels[p].name == "br":
                        gated(p, i)
                    if i:
                        low(p + 2)
                step(26)
                top(38, 41)
                step(27)
                rows("dout rn", "dout sd", KT)
                top(41, 43)
                evac(28, 0)
                evac(28, 1)
                for h in range(NH):
                    o = m.O[:, h, :]
                    E.wait_ge(dve_done, E.so_far())
                    E.wait_ge(pe_done, E.at(("dout spread", h)))
                    dve.scalar_tensor_tensor(o, PS[:, (4, 5, 6)[h % 3], :], m.lc[:, 1:2], o, ALU.mult,
                                             ALU.mult).then_inc(dve_done, 1)
                    E.counted(("dout y1", h))
                    E.wait_ge(dve_done, E.so_far())
                    dve.tensor_tensor(o, o, m.Z[:, h, :], ALU.mult).then_inc(dve_done, 1)
                    E.counted(("diff y", h))
                low(30)
                branch_lo("diff lo", "diff hi")
                step(29)
                top(43, 45)
                step(30)
                rows("dsa rn", "dsa sd", KT)
                top(45, 47)
                evac(31, 0)
                evac(31, 1)
                for n in range(4):
                    normed("dsa n", "dsa spread", n)
                low(33)
                top(47, 48)
                evac(32, 0)
                evac(32, 1)
                for n in range(4, 8):
                    normed("dsa n", "dsa spread", n)
                low(34)
                step(33)
                for i in range(1, TT):
                    bias(i)
                softmax_max(0, "s")
                softmax_norm(0, "s")
                softmax_max(1, "s")
                softmax_norm(1, "s")
                for u in range(1, NU):
                    p, i = mergeC + u // 2, u % 2
                    if u + 1 < NU:
                        softmax_max(u + 1, "s")
                        softmax_norm(u + 1, "s")
                    if panels[p].name == "br":
                        gated(p, i)
                    if i:
                        low(p + 2)
                for h in range(NH):
                    o = m.O[:, h, :]
                    E.wait_ge(dve_done, E.so_far())
                    E.wait_ge(act_done, E.at(("sout", 4 * h + 3)))
                    dve.tensor_tensor(o, o, m.Z[:, h, :], ALU.mult).then_inc(dve_done, 1)
                    E.counted(("dsa y", h))
                branch_lo("dsa lo", "dsa hi")
                def merged_lo(j):
                    E.wait_ge(dve_done, E.so_far())
                    E.wait_ge(act_done, E.at(("merged hi", j)))
                    dve.tensor_tensor(m.hL[:, j, :], m.mg[:, j, :], m.hH[:, j, :].bitcast(F32),
                                      ALU.subtract).then_inc(dve_done, 1)
                    E.counted(("merged lo", j))

                for p in range(mergeB, mergeB + 6):
                    if panels[p].name == "br":
                        gated(p, 0)
                        gated(p, 1)
                    low(p + 2)
                low(outs[0])
                for j in range(KT - 2):
                    merged_lo(j)
                for i in range(2):
                    gated(mergeB + 7, i)
                    merged_lo(KT - 2 + i)
                low(outs[1])
                for n, p in enumerate(outs):
                    for i in range(2):
                        E.wait_ge(dve_done, E.so_far())
                        E.wait_ge(pe_done, E.at(("Lpanel", p, i)))
                        x = m.x[:, 2 * i:2 * i + 2, PW * n:PW * n + PW]
                        dve.tensor_tensor(x, PS[:, bank(p, i), :].rearrange("p (a b) -> p a b", a=2), x,
                                          ALU.add).then_inc(dve_done, 1)
                        E.counted(("Levac", p, i))
                    low(outs[0] + n + 2 if n < 2 else NP)
        clear()


def program(nc, A, out, steps):
    m = lay_out(nc, A)
    m.PS = nc.alloc_psum_tensor("psum", [P, 8, T], F32)
    m.bank = {}
    made = {}

    def sems(name):
        if name not in made:
            made[name] = nc.alloc_semaphore(name)
        return made[name]

    done = {n: sems(f"{n}_done") for n in ("pe", "act", "dve", "pool")}

    def clear():
        with nc.Block() as block:
            @block.sync
            def _(sp):
                for s in made.values():
                    sp.sem_clear(s)

    mixer(nc, m, A, steps, done, sems)
    clear()
    ffn(nc, m, A, steps, done, sems)
    clear()
    layers(nc, m, A, steps, done, sems, clear)
    stored = sems("stored")
    with nc.Block() as block:
        @block.sync
        def _(sp):
            for t in range(TT):
                sp.dma_start(out[0, P * t:P * t + P, :], m.x[:, t, :]).then_inc(stored, 16)
            sp.wait_ge(stored, 16 * TT)


_INS = ["x", "pre_mix_g", "w_in", "conv_a_w", "shift_mu", "w0", "w2", "a0", "a2", "g2", "k_k", "k_a", "r_k", "lnx_w",
        "lnx_b", "w_out", "post_mix_g", "pre_ffn_g", "w_up", "ffn_conv_w", "ffn_conv_b", "w_down", "post_ffn_g",
        "norm_g_2", "w_in_2", "gla_wa2_2", "gla_ba_2", "gla_norm_g_2", "dsa_qn_g_2", "dsa_kn_g_2", "diff_qn_g_2",
        "diff_kn_g_2", "diff_lq1_2", "diff_lk1_2", "diff_lq2_2", "diff_lk2_2", "w_br_2", "w_out_2"]


def kernel(**inputs):
    import numpy as _np
    import concourse.bacc as _bacc
    from concourse import mybir as _mybir
    from concourse.bass_utils import run_bass_kernel_spmd as _run

    def write(known):
        nc = _bacc.Bacc("TRN2", target_bir_lowering=False, num_devices=1)
        arrays, A = {}, {}
        for name in _INS:
            a = _np.ascontiguousarray(inputs[name])
            arrays[f"in_{name}_dram"] = a
            A[name] = nc.dram_tensor(f"in_{name}_dram", a.shape, _mybir.dt.from_np(a.dtype), kind="ExternalInput").ap()
        out = nc.dram_tensor("out_0_dram", (1, T, D), _mybir.dt.float32, kind="ExternalOutput").ap()
        steps = Steps(known)
        program(nc, A, out, steps)
        return nc, arrays, steps

    _, _, known = write(None)
    nc, arrays, _ = write(known)
    r = _run(nc, [arrays], core_ids=[0])
    return r.results[0]["out_0_dram"]
```
